# Optimizing a Trainium2 kernel written in Bass

```python
import math
import jax, jax.numpy as jnp
from jax import lax
import numpy as np

D_MODEL = 1024
BATCH = 1
SEQ = 512
DEPTH = 2

D_MIX = D_MODEL
GROUP = D_MIX // 4
HEAD_DIM = 64
N_HEADS = GROUP // HEAD_DIM
D_IN = 10 * GROUP
CONV_WIDTH = 31
RET_CHUNK = 128
RET_ROT_THETA = 10000.0
MOBA_BLOCK = 256
MOBA_TOPK = 3
MOBA_QCHUNK = 64
ROPE_THETA = 500000.0
ROT_DIM = HEAD_DIM // 4
POOL_WINDOWS = (2, 4, 8, 16)
POOL_GROUP = GROUP // len(POOL_WINDOWS)
D_FF = -(-8 * D_MODEL // (3 * 256)) * 256
NEG = -1e30

kernel_name = "hybrid_parallel_conv_ret_moba_pool"

def rms_norm(x, g, eps=1e-6):
    xf = x.astype(jnp.float32)
    y = xf * lax.rsqrt(jnp.mean(xf * xf, axis=-1, keepdims=True) + eps)
    return (y * g.astype(jnp.float32)).astype(x.dtype)

def apply_rotary(x, rot_dim, theta):
    s = x.shape[1]
    pos = jnp.arange(s, dtype=jnp.float32)
    inv = 1.0 / (theta ** (jnp.arange(0, rot_dim, 2, dtype=jnp.float32) / rot_dim))
    ang = pos[:, None] * inv[None, :]
    cos = jnp.cos(ang)[None, :, None, :]
    sin = jnp.sin(ang)[None, :, None, :]
    xf = x.astype(jnp.float32)
    half = rot_dim // 2
    x1 = xf[..., :half]
    x2 = xf[..., half:rot_dim]
    out = jnp.concatenate([x1 * cos - x2 * sin, x1 * sin + x2 * cos, xf[..., rot_dim:]], axis=-1)
    return out.astype(x.dtype)

def conv_mixer(u, w_dw, b_dw, ln_g, ln_b):
    a, gate = jnp.split(u, 2, axis=-1)
    h = a * jax.nn.sigmoid(gate)
    h = lax.conv_general_dilated(
        h, w_dw[:, None, :].astype(h.dtype), window_strides=(1,),
        padding=[(CONV_WIDTH - 1, 0)],
        dimension_numbers=('NWC', 'WIO', 'NWC'),
        feature_group_count=GROUP) + b_dw
    hf = h.astype(jnp.float32)
    mu = jnp.mean(hf, axis=-1, keepdims=True)
    var = jnp.mean(jnp.square(hf - mu), axis=-1, keepdims=True)
    hf = (hf - mu) * lax.rsqrt(var + 1e-5) * ln_g + ln_b
    return jax.nn.silu(hf).astype(u.dtype)

def retention(q, k, v, g, gn_g, gn_b):
    b, s, _ = q.shape
    dt = q.dtype
    q = apply_rotary(q.reshape(b, s, N_HEADS, HEAD_DIM), HEAD_DIM, RET_ROT_THETA).astype(jnp.float32)
    k = apply_rotary(k.reshape(b, s, N_HEADS, HEAD_DIM), HEAD_DIM, RET_ROT_THETA).astype(jnp.float32)
    k = k * (HEAD_DIM ** -0.5)
    v = v.reshape(b, s, N_HEADS, HEAD_DIM).astype(jnp.float32)
    c = RET_CHUNK
    nc = s // c

    def to_chunks(t):
        return t.reshape(b, nc, c, N_HEADS, HEAD_DIM).transpose(1, 0, 3, 2, 4)

    log_gamma = jnp.log(1.0 - 2.0 ** (-5.0 - jnp.arange(N_HEADS, dtype=jnp.float32)))
    idx = jnp.arange(c, dtype=jnp.float32)
    diff = idx[:, None] - idx[None, :]
    decay_mask = jnp.where(diff[None] >= 0,
                           jnp.exp(jnp.maximum(diff, 0.0)[None] * log_gamma[:, None, None]), 0.0)
    q_decay = jnp.exp((idx + 1.0)[None, :] * log_gamma[:, None])
    k_decay = jnp.exp((c - 1.0 - idx)[None, :] * log_gamma[:, None])
    chunk_decay = jnp.exp(c * log_gamma)

    def step(state, xs):
        qc, kc, vc = xs
        scores = jnp.einsum('bhid,bhjd->bhij', qc, kc) * decay_mask
        o = jnp.einsum('bhij,bhjd->bhid', scores, vc)
        o = o + jnp.einsum('bhid,bhde->bhie', qc * q_decay[:, :, None], state)
        state = state * chunk_decay[:, None, None] + jnp.einsum(
            'bhjd,bhje->bhde', kc * k_decay[:, :, None], vc)
        return state, o

    state0 = jnp.zeros((b, N_HEADS, HEAD_DIM, HEAD_DIM), jnp.float32)
    _, o = lax.scan(step, state0, (to_chunks(q), to_chunks(k), to_chunks(v)))
    o = o.transpose(1, 0, 3, 2, 4).reshape(b, s, N_HEADS, HEAD_DIM)
    mu = jnp.mean(o, axis=-1, keepdims=True)
    var = jnp.mean(jnp.square(o - mu), axis=-1, keepdims=True)
    o = ((o - mu) * lax.rsqrt(var + 1e-5)).reshape(b, s, GROUP) * gn_g + gn_b
    return (jax.nn.silu(g.astype(jnp.float32)) * o).astype(dt)

def moba_attention(q, k, v):
    b, s, _ = q.shape
    dt = q.dtype
    q = apply_rotary(q.reshape(b, s, N_HEADS, HEAD_DIM), ROT_DIM, ROPE_THETA)
    k = apply_rotary(k.reshape(b, s, N_HEADS, HEAD_DIM), ROT_DIM, ROPE_THETA)
    v = v.reshape(b, s, N_HEADS, HEAD_DIM)
    nb = -(-s // MOBA_BLOCK)
    sp = nb * MOBA_BLOCK
    if sp != s:
        pad = ((0, 0), (0, sp - s), (0, 0), (0, 0))
        q, k, v = jnp.pad(q, pad), jnp.pad(k, pad), jnp.pad(v, pad)
    bh = b * N_HEADS
    q = q.transpose(0, 2, 1, 3).reshape(bh, sp, HEAD_DIM)
    kb = k.transpose(0, 2, 1, 3).reshape(bh, nb, MOBA_BLOCK, HEAD_DIM)
    vb = v.transpose(0, 2, 1, 3).reshape(bh, nb, MOBA_BLOCK, HEAD_DIM)
    k_mean = jnp.mean(kb.astype(jnp.float32), axis=2)
    topk = min(MOBA_TOPK, nb)
    nq = sp // MOBA_QCHUNK
    q_chunks = q.reshape(bh, nq, MOBA_QCHUNK, HEAD_DIM).transpose(1, 0, 2, 3)
    scale = HEAD_DIM ** -0.5
    bh_idx = jnp.arange(bh)[:, None, None]

    def attend(args):
        qc, ci = args
        start = ci * MOBA_QCHUNK
        n = start // MOBA_BLOCK
        qpos = start + jnp.arange(MOBA_QCHUNK)
        gate = jnp.einsum('zqd,znd->zqn', qc.astype(jnp.float32), k_mean)
        gate = jnp.where((jnp.arange(nb) < n)[None, None, :], gate, NEG)
        _, sel = lax.top_k(gate, topk)
        sel_valid = jnp.arange(topk) < n
        kg = kb[bh_idx, sel]
        vg = vb[bh_idx, sel]
        s_sel = jnp.einsum('zqd,zqtkd->zqtk', qc, kg).astype(jnp.float32) * scale
        s_sel = jnp.where(sel_valid[None, None, :, None], s_sel, NEG)
        s_sel = s_sel.reshape(bh, MOBA_QCHUNK, topk * MOBA_BLOCK)
        k_own = lax.dynamic_index_in_dim(kb, n, axis=1, keepdims=False)
        v_own = lax.dynamic_index_in_dim(vb, n, axis=1, keepdims=False)
        s_own = jnp.einsum('zqd,zkd->zqk', qc, k_own).astype(jnp.float32) * scale
        kpos = n * MOBA_BLOCK + jnp.arange(MOBA_BLOCK)
        s_own = jnp.where(kpos[None, None, :] <= qpos[None, :, None], s_own, NEG)
        p = jax.nn.softmax(jnp.concatenate([s_sel, s_own], axis=-1), axis=-1)
        p_sel = p[..., :topk * MOBA_BLOCK].reshape(bh, MOBA_QCHUNK, topk, MOBA_BLOCK)
        p_own = p[..., topk * MOBA_BLOCK:]
        o = (jnp.einsum('zqtk,zqtkd->zqd', p_sel.astype(vg.dtype), vg)
             + jnp.einsum('zqk,zkd->zqd', p_own.astype(v_own.dtype), v_own))
        return o.astype(dt)

    o = lax.map(attend, (q_chunks, jnp.arange(nq)))
    o = o.transpose(1, 0, 2, 3).reshape(b, N_HEADS, sp, HEAD_DIM)[:, :, :s]
    return o.transpose(0, 2, 1, 3).reshape(b, s, GROUP)

def pool_mixer(u, w_pool, b_pool, pool_scale):
    b, s, _ = u.shape
    uf = u.astype(jnp.float32)
    cs = jnp.concatenate([jnp.zeros((b, 1, GROUP), jnp.float32), jnp.cumsum(uf, axis=1)], axis=1)
    t = jnp.arange(s)
    outs = []
    for gi, w in enumerate(POOL_WINDOWS):
        sl = slice(gi * POOL_GROUP, (gi + 1) * POOL_GROUP)
        lo = jnp.maximum(t + 1 - w, 0)
        cnt = (t + 1 - lo).astype(jnp.float32)[None, :, None]
        mean = (cs[:, 1:, sl] - cs[:, lo, sl]) / cnt
        outs.append(mean - uf[:, :, sl])
    pooled = jnp.stack(outs, axis=2)
    y = jnp.einsum('bsgc,gcd->bsgd', pooled, w_pool.astype(jnp.float32)).reshape(b, s, GROUP)
    return ((y + b_pool) * pool_scale).astype(u.dtype)

def setup_inputs(seed: int = 0) -> dict:
    key = jax.random.key(seed)
    ks = jax.random.split(key, 24)
    f32 = jnp.float32
    nrm = lambda k, shp, sc: jax.random.normal(k, shp, f32) * sc
    L = DEPTH
    return {
        "x": nrm(ks[0], (BATCH, SEQ, D_MODEL), 1.0),
        "attn_pre_g": 1.0 + nrm(ks[1], (L, D_MODEL), 0.05),
        "w_in": nrm(ks[2], (L, D_MODEL, D_IN), D_MODEL ** -0.5),
        "conv_w": nrm(ks[3], (L, CONV_WIDTH, GROUP), CONV_WIDTH ** -0.5),
        "conv_b": nrm(ks[4], (L, GROUP), 0.02),
        "conv_ln_g": 1.0 + nrm(ks[5], (L, GROUP), 0.05),
        "conv_ln_b": nrm(ks[6], (L, GROUP), 0.02),
        "ret_gn_g": 1.0 + nrm(ks[7], (L, GROUP), 0.05),
        "ret_gn_b": nrm(ks[8], (L, GROUP), 0.02),
        "pool_w": nrm(ks[9], (L, len(POOL_WINDOWS), POOL_GROUP, POOL_GROUP), POOL_GROUP ** -0.5),
        "pool_b": nrm(ks[10], (L, GROUP), 0.02),
        "pool_scale": 1.0 + nrm(ks[11], (L, GROUP), 0.1),
        "w_out": nrm(ks[12], (L, D_MIX, D_MODEL), D_MIX ** -0.5),
        "attn_post_g": 1.0 + nrm(ks[13], (L, D_MODEL), 0.05),
        "ffn_pre_g": 1.0 + nrm(ks[14], (L, D_MODEL), 0.05),
        "w_gate": nrm(ks[15], (L, D_MODEL, D_FF), D_MODEL ** -0.5),
        "w_up": nrm(ks[16], (L, D_MODEL, D_FF), D_MODEL ** -0.5),
        "w_down": nrm(ks[17], (L, D_FF, D_MODEL), D_FF ** -0.5),
        "ffn_post_g": 1.0 + nrm(ks[18], (L, D_MODEL), 0.05),
    }

def reference(x, attn_pre_g, w_in, conv_w, conv_b, conv_ln_g, conv_ln_b, ret_gn_g, ret_gn_b,
              pool_w, pool_b, pool_scale, w_out, attn_post_g, ffn_pre_g, w_gate, w_up, w_down,
              ffn_post_g):
    G = GROUP
    for l in range(DEPTH):
        h = rms_norm(x, attn_pre_g[l])
        u = jnp.einsum('bsd,de->bse', h, w_in[l])
        u_conv, rq, rk, rv, rg, mq, mk, mv, u_pool = jnp.split(
            u, [2 * G, 3 * G, 4 * G, 5 * G, 6 * G, 7 * G, 8 * G, 9 * G], axis=-1)
        y_a = conv_mixer(u_conv, conv_w[l], conv_b[l], conv_ln_g[l], conv_ln_b[l])
        y_b = retention(rq, rk, rv, rg, ret_gn_g[l], ret_gn_b[l])
        y_c = moba_attention(mq, mk, mv)
        y_d = pool_mixer(u_pool, pool_w[l], pool_b[l], pool_scale[l])
        y = jnp.concatenate([y_a, y_b, y_c, y_d], axis=-1)
        y = jnp.einsum('bse,ed->bsd', y, w_out[l])
        x = x + rms_norm(y, attn_post_g[l])
        h = rms_norm(x, ffn_pre_g[l])
        f = jax.nn.silu(jnp.einsum('bsd,df->bsf', h, w_gate[l])) * jnp.einsum('bsd,df->bsf', h, w_up[l])
        f = jnp.einsum('bsf,fd->bsd', f, w_down[l])
        x = x + rms_norm(f, ffn_post_g[l])
    return x


_drawn_inputs = setup_inputs


def setup_inputs(seed=0):
    import zlib

    import numpy as np

    out = dict(_drawn_inputs(seed))
    spreads = {}
    factors = {'conv_ln_b': 4.734, 'ret_gn_b': 5.349, 'pool_b': 2.938}
    for name, (base, spread) in spreads.items():
        noise = np.random.default_rng([zlib.crc32(name.encode()), seed]).standard_normal(out[name].shape)
        drawn = base * np.exp(spread * noise) if base else spread * noise
        out[name] = __import__('jax').numpy.asarray(drawn.astype(out[name].dtype))
    for name, factor in factors.items():
        out[name] = (out[name] * factor).astype(out[name].dtype)
    return out
```

```python
import math
from contextlib import ExitStack

import concourse.bass as bass
from concourse import mybir

F32 = mybir.dt.float32
F16 = mybir.dt.float16
I32 = mybir.dt.int32
ALU = mybir.AluOpType
ACT = mybir.ActivationFunctionType
AX_X = mybir.AxisListType.X

P = 128
DM = 1024
S = 512
L = 2
KT = DM // P
HALF = S // 2
NT = S // P
G = DM // 4
HD = 64
NH = G // HD
CW = 31
FF = 2816
FT = FF // P
WINDOWS = (2, 4, 8, 16)

SLOT = 2048
RAW = SLOT // 2
NRAW = 2
RING = 8

W_SCALE = 1024.0
A_SCALE = 32.0
UNSCALE = 1.0 / (W_SCALE * A_SCALE)
RSQRT_MAGIC = float(0x5F3759DF)

CONV_A, CONV_G, RQ, RK, RV, POOL, MQ, MK, MV, RG = range(10)
BLOCK_OF = {CONV_A: 0, CONV_G: 1, RQ: 2, RK: 3, RV: 4, POOL: 9, MQ: 6, MK: 7, MV: 8, RG: 5}
TOKEN_MAJOR = (RQ, RK, RV, MQ, MK, MV)
IN_GROUP = 5
N_IN, N_OUT, N_GU, N_DN = 10, 4, FT, FT // 2
OUT0 = N_IN
GU0 = OUT0 + N_OUT
DN0 = GU0 + N_GU
SLOTS = DN0 + N_DN
GU_HEAD = 5
DN_TAIL = 4

FIRST_BY_DVE = (0, 1)

UNITS = []
for g in range(2):
    for s in range(2):
        UNITS += [(IN_GROUP * g + c, s) for c in range(IN_GROUP)]
for s in range(2):
    UNITS += [(OUT0 + c, s) for c in range(N_OUT)]
for s in range(2):
    UNITS += [(GU0 + c, s) for c in range(GU_HEAD)]
UNITS += [(GU0 + c, s) for c in range(GU_HEAD, N_GU) for s in range(2)]
UNITS += [(DN0 + c, s) for c in range(N_DN - DN_TAIL) for s in range(2)]
for s in range(2):
    UNITS += [(DN0 + c, s) for c in range(N_DN - DN_TAIL, N_DN)]
NU = len(UNITS)
UNIT_AT = {u: i for i, u in enumerate(UNITS)}
HIDDEN = [(c - GU0, s) for c, s in UNITS if GU0 <= c < DN0]
GU_EARLY = 2
RING_UNITS = UNIT_AT[(DN0, 0)]
assert NU == 2 * SLOTS and RING_UNITS % 4 == 0

PAR = {}
PAR_COLS = 0
for name, cols in (("pre", KT), ("post", KT), ("fpre", KT), ("fpost", KT), ("cw", 2 * CW), ("cb", 2),
                   ("lng", 2), ("lnb", 2), ("gng", 2), ("gnb", 2), ("pb", 2), ("ps", 2)):
    PAR[name] = PAR_COLS
    PAR_COLS += cols

PARX = {}
PARX_COLS = 0
PARX_FROM = (("pre", KT, A_SCALE), ("fpre", KT, A_SCALE), ("cw", 2 * CW, 0.5 * UNSCALE), ("lng", 2, 0.5),
             ("lnb", 2, 0.5))
for name, cols, _ in PARX_FROM:
    PARX[name] = PARX_COLS
    PARX_COLS += cols

CST = {}
CST_COLS = 0
for name, cols in (("ident", P), ("tri", P), ("neg", P), ("ones", P), ("rqc", NT * NH * 32),
                   ("rqs", NT * NH * 32), ("rkc", NT * NH * 32), ("rks", NT * NH * 32),
                   ("mc", NT * NH * 8), ("ms", NT * NH * 8), ("adj", 2 * 16)):
    CST[name] = CST_COLS
    CST_COLS += cols


def trunk_program(nc, x, weights, params, pool_w, consts, out):
    with ExitStack() as ctx:
        def sb(name, shape, dt=F32):
            return ctx.enter_context(nc.sbuf_tensor(name, shape, dt))

        def sem(name):
            return ctx.enter_context(nc.semaphore(name))

        xT = sb("xT", [P, KT, S])
        hT = sb("hT", [P, 2, KT, S], F16)
        yT = sb("yT", [P, 2, KT, HALF])
        sq = sb("sq", [P, KT, HALF])
        raw = sb("raw", [P, NRAW, RAW])
        ring = sb("ring", [P, RING, 2, SLOT], F16)
        U = sb("U", [P, FT * S])
        E = sb("E", [P, 5184])
        cst = sb("cst", [P, CST_COLS])
        par = sb("par", [P, L, PAR_COLS])
        parx = sb("parx", [P, L, PARX_COLS])
        bd = sb("bd", [P, L, 2, P])
        small = sb("small", [P, 136])
        bank = [ctx.enter_context(nc.psum_tensor(f"bank{i}", [P, 512], F32)) for i in range(8)]

        def C(name):
            at = CST[name]
            nxt = min([v for v in CST.values() if v > at] + [CST_COLS])
            return cst[:, at:nxt]

        ident, tri, neg, ones = C("ident"), C("tri"), C("neg"), C("ones")

        fT = U[:, :].bitcast(F16).rearrange("p (h f t) -> p h f t", h=2, f=FT)

        def carve(buf, sizes):
            at, got = 0, []
            for n in sizes:
                got.append(buf[:, at:at + n])
                at += n
            return got

        (ycat_w, ubuf_w, rv_w, mv_w, mqk_w, mkT_w, mqT_w, o_w, th_w, state_w) = carve(
            U, [KT * S, 2 * (16 + S), NT * G, NT * G, 2 * 2 * G, 2 * S, 2 * 2 * P, 2 * G, 2 * HALF, 2 * P])
        ycat = ycat_w.bitcast(F16).rearrange("p (h k t) -> p h k t", h=2, k=KT)
        ubuf = ubuf_w.rearrange("p (c t) -> p c t", c=2)
        rv = rv_w.rearrange("p (t c) -> p t c", t=NT)
        mv = mv_w.rearrange("p (t c) -> p t c", t=NT)
        mqk = mqk_w.rearrange("p (q t c) -> p q t c", q=2, t=2)
        mkT = mkT_w.rearrange("p (c t) -> p c t", c=2)
        mqT = mqT_w.rearrange("p (b c t) -> p b c t", b=2, c=2)
        osb = o_w.rearrange("p (t c) -> p t c", t=2)
        th = th_w.rearrange("p (c t) -> p c t", c=2)
        yA = yT[:, 0, :, :].rearrange("p k t -> p (k t)")
        yB = yT[:, 1, :, :].rearrange("p k t -> p (k t)")
        qk_w, rT_w, sm_w = carve(yA, [2 * 2 * G, 4 * P, 4 * P])
        qk = qk_w.rearrange("p (q t c) -> p q t c", q=2, t=2)
        rT = rT_w.rearrange("p (c t) -> p c t", c=4)
        sm = sm_w.rearrange("p (h t) -> p h t", h=4)
        pr_w, pT_w = carve(yB, [2 * S, 2 * S])
        pr = pr_w.rearrange("p (b t) -> p b t", b=2)
        pT = pT_w.rearrange("p (b j t) -> p b j t", b=2, j=NT)
        sqf = sq[:, :, :].rearrange("p k t -> p (k t)")
        t2_w, t4_w, t8, pooled_w = carve(sqf, [2 * (HALF + 14), 2 * (HALF + 12), HALF + 8, 2 * HALF])
        t2 = t2_w.rearrange("p (c t) -> p c t", c=2)
        t4 = t4_w.rearrange("p (c t) -> p c t", c=2)
        pooled = pooled_w.rearrange("p (c t) -> p c t", c=2)
        (rz_w, cn_w, yb_w, hb_w, ca_w, m1, m2, ssq, diag, mo_w) = carve(
            E, [2 * HALF, 2 * G, 2 * HALF, 2 * (CW - 1 + S), 2 * HALF, 512, 512, HALF, HALF, 2 * G])
        mo = mo_w.rearrange("p (t c) -> p t c", t=2)
        rz = rz_w.rearrange("p (c t) -> p c t", c=2)
        cn = cn_w.rearrange("p (t c) -> p t c", t=2)
        ybuf = yb_w.rearrange("p (c t) -> p c t", c=2)
        hbuf = hb_w.rearrange("p (c t) -> p c t", c=2)
        cacc = ca_w.rearrange("p (c t) -> p c t", c=2)
        state = state_w.rearrange("p (c e) -> p c e", c=2)
        sil = m1.rearrange("p (b t) -> p b t", b=2)
        fbuf = m2.rearrange("p (b t) -> p b t", b=2)
        xin = yT[:, :, :, :].rearrange("p s k t -> p (s k t)").rearrange("p (t c) -> p t c", t=NT)
        xout = hT[:, :, :, :].rearrange("p h k t -> p (h k t)").bitcast(F32).rearrange(
            "p (t c) -> p t c", t=NT)
        (rsx, rst, rsy, nms, sums, rinv, bst, mvr, cst_st, cmv) = carve(
            small, [10, 10, 10, 8, 8, 8, 48, 16, 12, 4])

        def half(s):
            return slice(HALF * s, HALF * (s + 1))

        def tok(t):
            return slice(P * t, P * (t + 1))

        def b256(b):
            return bank[b][:, :].rearrange("p (c t) -> p c t", c=2)

        def b128(b):
            return bank[b][:, :].rearrange("p (c t) -> p c t", c=4)

        def par_col(l, name, c):
            return par[:, l, PAR[name] + c:PAR[name] + c + 1]

        def px(l, name, c):
            return parx[:, l, PARX[name] + c:PARX[name] + c + 1]

        def gain(kind, l, k):
            return px(l, kind, k)

        consts_in = sem("consts_in")
        params_in = sem("params_in")
        maps_in = sem("maps_in")
        x_in = sem("x_in")
        hi_split = sem("hi_split")
        raw_scaled = sem("raw_scaled")
        lo_pool = sem("lo_pool")
        lo_dve = sem("lo_dve")
        unit_done = sem("unit_done")
        act_tick = sem("act_tick")
        dve_tick = sem("dve_tick")
        setup_done = sem("setup_done")
        xt_ps = sem("xt_ps")
        xt_sb = sem("xt_sb")
        y_sb = sem("y_sb")
        sq_done = sem("sq_done")
        ssq_done = sem("ssq_done")
        nsum_ps = sem("nsum_ps")
        diag_done = sem("diag_done")
        rstd_ps = sem("rstd_ps")
        xr_done = sem("xr_done")
        x_upd = sem("x_upd")
        h_hi = sem("h_hi")
        h_lo = sem("h_lo")
        glu_th = sem("glu_th")
        hb_sb = sem("hb_sb")
        rot_done = sem("rot_done")
        rv_sb = sem("rv_sb")
        retT_ps = sem("retT_ps")
        retT_sb = sem("retT_sb")
        retS_ps = sem("retS_ps")
        retS_sb = sem("retS_sb")
        retO_ps = sem("retO_ps")
        retO_sb = sem("retO_sb")
        state_sb = sem("state_sb")
        retN_sb = sem("retN_sb")
        retY_ps = sem("retY_ps")
        ret_z = sem("ret_z")
        rg_th = sem("rg_th")
        ret_g = sem("ret_g")
        ret_y32 = sem("ret_y32")
        ret_hi = sem("ret_hi")
        ret_y = sem("ret_y")
        conv_sb = sem("conv_sb")
        convT_ps = sem("convT_ps")
        convN_sb = sem("convN_sb")
        convY_ps = sem("convY_ps")
        conv_th = sem("conv_th")
        conv_z = sem("conv_z")
        conv_y32 = sem("conv_y32")
        conv_hi = sem("conv_hi")
        conv_y = sem("conv_y")
        pool_u = sem("pool_u")
        pool_sb = sem("pool_sb")
        poolY_ps = sem("poolY_ps")
        pool_y32 = sem("pool_y32")
        pool_hi = sem("pool_hi")
        pool_y = sem("pool_y")
        mq_sb = sem("mq_sb")
        mk_sb = sem("mk_sb")
        mrot = sem("mrot")
        mv_sb = sem("mv_sb")
        mT_ps = sem("mT_ps")
        mT_sb = sem("mT_sb")
        mS_ps = sem("mS_ps")
        mM = sem("mM")
        mP = sem("mP")
        mPT_ps = sem("mPT_ps")
        mPT_sb = sem("mPT_sb")
        mPV = sem("mPV")
        mO_sb = sem("mO_sb")
        mY_ps = sem("mY_ps")
        moba_hi = sem("moba_hi")
        moba_y = sem("moba_y")
        sil_done = sem("sil_done")
        f_sb = sem("f_sb")
        f_hi = sem("f_hi")
        f_lo = sem("f_lo")
        xo_ps = sem("xo_ps")
        xo_sb = sem("xo_sb")
        stored = sem("stored")
        raw_in = [sem(f"raw_in{i}") for i in range(NRAW)]

        def dve_splits(n):
            return n in FIRST_BY_DVE or (n >= RING and GU0 <= (n - RING) % SLOTS < SLOTS - DN_TAIL)

        def split_count(n):
            by_dve = dve_splits(n // 2)
            count = sum(dve_splits(i // 2) == by_dve for i in range(n + 1))
            return (lo_dve if by_dve else lo_pool), count

        def unit_no(l, slot, s):
            return l * NU + UNIT_AT[(slot, s)] + 1

        def hs(l, s):
            return 2 * l + s + 1

        def ts(l, t):
            return NT * l + t + 1

        def ths(l, t, h):
            return NH * (NT * l + t) + h + 1

        def fno(l, f, s):
            return 2 * FT * l + UNIT_AT[(GU0 + f, s)] - UNIT_AT[(GU0, 0)] + 1

        def unit_bank(slot, s):
            return UNIT_AT[(slot, s)] % 4

        NORMS = [("pre", 0, 0), ("pre", 0, 1)]
        for l in range(L):
            for s in range(2):
                NORMS += [("post", l, s), ("fpre", l, s)]
            for s in range(2):
                NORMS += [("fpost", l, s)] + ([("pre", l + 1, s)] if l + 1 < L else [])
        PRES = [n for n in NORMS if n[0] in ("pre", "fpre")]
        POSTS = [n for n in NORMS if n[0] in ("post", "fpost")]

        def norm_no(*n):
            return NORMS.index(n)

        def pre_no(*n):
            return PRES.index(n)

        def post_no(*n):
            return POSTS.index(n)

        def norm_bank(kind, l, s):
            return 3 if s == 0 and (kind == "fpost" or (kind == "pre" and l)) else 7

        def raw_part(i):
            return slice(RAW * i, RAW * (i + 1))

        block = ctx.enter_context(nc.Block())

        @block.sync
        def _(sp):
            for t in range(NT):
                sp.dma_start(xin[:, t, :], x[tok(t), :]).then_inc(x_in, 16)
            sp.dma_start(cst[:, :], consts).then_inc(consts_in, 16)
            for n in range(2 * L * SLOTS):
                if n >= NRAW:
                    sp.wait_ge(*split_count(n - NRAW))
                sp.dma_start(raw[:, n % NRAW, :], weights[n // 2, :, raw_part(n % 2)]).then_inc(
                    raw_in[n % NRAW], 16)
                if n == 1:
                    sp.dma_start(par[:, :, :], params).then_inc(params_in, 16)
                    sp.wait_ge(dve_tick, 1)
                    for l in range(L):
                        for g in range(4):
                            r = slice(HD * (g % 2), HD * (g % 2) + HD)
                            sp.dma_start(bd[r, l, g // 2, r], pool_w[l, g, :, :]).then_inc(maps_in, 16)
            for t in range(NT):
                sp.wait_ge(xo_sb, 2 * (t + 1))
                sp.dma_start(out[tok(t), :], xout[:, t, :]).then_inc(stored, 16)
            sp.wait_ge(stored, 16 * NT)

        @block.gpsimd
        def _(pool):
            for n in range(2 * L * SLOTS):
                slot, part = n // 2, n % 2
                hi = ring[:, slot % RING, 0, raw_part(part)]
                lo = ring[:, slot % RING, 1, raw_part(part)]
                pool.wait_ge(raw_in[n % NRAW], 16 * (n // NRAW + 1))
                if slot >= RING:
                    old = slot - RING
                    pool.wait_ge(unit_done, unit_no(old // SLOTS, old % SLOTS, 1))
                src = raw[:, n % NRAW, :]
                nc.gpsimd.tensor_scalar(hi, src, W_SCALE, 1.0, ALU.mult, ALU.mult).then_inc(hi_split, 1)
                if not dve_splits(slot):
                    pool.wait_ge(hi_split, n + 1)
                    nc.gpsimd.tensor_scalar(src, src, W_SCALE, 1.0, ALU.mult, ALU.mult).then_inc(raw_scaled, 1)
                    pool.wait_ge(raw_scaled, split_count(n)[1])
                    nc.gpsimd.tensor_tensor(lo, src, hi, ALU.subtract).then_inc(lo_pool, 1)

        @block.tensor
        def _(pe):
            mm = nc.tensor.matmul
            freed_by = [None] * 8

            def take(b, sem, value):
                if freed_by[b] is not None:
                    pe.wait_ge(*freed_by[b])
                freed_by[b] = (sem, value)

            def split3(dst, w, a, first, last, weights_still, **kw):
                for i, (pw, pa) in enumerate(((0, 0), (0, 1), (1, 0))):
                    st, mv_ = (w[pw], a[pa]) if weights_still else (a[pa], w[pw])
                    ins = mm(dst, st, mv_, start=first and i == 0, stop=last and i == 2, **kw)
                return ins

            def transpose(dst, src):
                return nc.tensor.transpose(dst, src, ident)

            def last_read(l, slot, s):
                if slot >= GU0:
                    return f_sb, fno(l, slot - GU0, s)
                if slot >= OUT0:
                    return y_sb, 4 * post_no("post", l, s) + slot - OUT0 + 1
                return {CONV_A: (hb_sb, hs(l, s)), CONV_G: (glu_th, hs(l, s)), RQ: (rot_done, 2 * hs(l, s) - 1),
                        RK: (rot_done, 2 * hs(l, s)), RV: (rv_sb, hs(l, s)), POOL: (pool_u, hs(l, s)),
                        MQ: (mq_sb, hs(l, s)), MK: (mk_sb, hs(l, s)), MV: (mv_sb, hs(l, s)),
                        RG: (ret_y32, hs(l, s))}[slot]

            def unit(l, slot, s, mid):
                if s == 0:
                    pe.wait_ge(*split_count(2 * (l * SLOTS + slot) + 1))
                w = [ring[:, (l * SLOTS + slot) % RING, i, :].rearrange(
                    "p (k n) -> p k n", k=KT if slot < DN0 else 2) for i in range(2)]
                if slot < DN0:
                    b = unit_bank(slot, s)
                    take(b, *last_read(l, slot, s))
                    order, src = range(KT), hT
                    if slot == 0:
                        pe.wait_ge(h_lo, KT * (pre_no("pre", l, s) + 1))
                    elif slot == GU0:
                        pe.wait_ge(h_lo, KT * (pre_no("fpre", l, s) + 1))
                    if OUT0 <= slot < GU0:
                        src, order = ycat, [6, 7, 0, 1, 2, 3, 4, 5]
                    for c in range(2):
                        for i, k in enumerate(order):
                            if slot == OUT0 and c == 0 and i % 2 == 0:
                                pe.wait_ge((pool_y, conv_y, ret_y, moba_y)[i // 2], hs(l, s))
                            if slot in TOKEN_MAJOR:
                                cols, rows = slice(0, G), tok(2 * s + c)
                            else:
                                cols, rows = slice(P * c, P * (c + 1)), half(s)
                            last = split3(b256(b)[:, c, :], [w[0][:, k, cols], w[1][:, k, cols]],
                                          [src[:, 0, k, rows], src[:, 1, k, rows]],
                                          i == 0, i == KT - 1, slot not in TOKEN_MAJOR)
                        if c == 0:
                            mid()
                else:
                    for c in range(2):
                        f = 2 * (slot - DN0) + c
                        pe.wait_ge(f_lo, fno(l, f, s))
                        for m in range(KT):
                            b = 4 * s + m // 2
                            if f == 0 and m % 2 == 0:
                                take(b, y_sb, 4 * post_no("fpost", l, s) + m // 2 + 1)
                            ms = slice(P * m, P * (m + 1))
                            last = split3(b256(b)[:, m % 2, :], [w[0][:, c, ms], w[1][:, c, ms]],
                                          [fT[:, 0, f, half(s)], fT[:, 1, f, half(s)]],
                                          f == 0 and m % 2 == 0, f == FT - 1, True, skip_group_check=True)
                        if c == 0:
                            mid()
                last.then_inc(unit_done, 1)

            def norm_sum(kind, l, s):
                n, b = norm_no(kind, l, s), norm_bank(kind, l, s)
                take(b, xr_done, n + 1)
                pe.wait_ge(ssq_done, n + 1)
                for t in range(2):
                    last = mm(bank[b][:, t:t + 1], ssq[:, tok(t)], ones[:, 0:1], start=True, stop=True)
                last.then_inc(nsum_ps, 1)

            def norm_bcast(kind, l, s):
                n, b = norm_no(kind, l, s), norm_bank(kind, l, s)
                pe.wait_ge(diag_done, n + 1)
                mm(bank[b][:, HALF:2 * HALF], ones, diag, start=True, stop=True).then_inc(rstd_ps, 1)

            def rows_of(h):
                return slice(HD * (h % 2), HD * (h % 2) + HD)

            def ret_T(l, t):
                pe.wait_ge(rot_done, 2 * hs(l, t // 2))
                take(4, retT_sb, ts(l, t))
                for q in range(2):
                    for c in range(2):
                        last = transpose(b128(4)[:, 2 * q + c, :], qk[:, q, t % 2, P * c:P * (c + 1)])
                last.then_inc(retT_ps, 1)

            def ret_S(l, t):
                pe.wait_ge(retT_sb, ts(l, t))
                take(6, retS_sb, 2 * ts(l, t) - 1)
                take(4, retS_sb, 2 * ts(l, t))
                for h in range(NH):
                    r = rows_of(h)
                    last = mm(b128((6, 4)[h % 2])[:, h // 2, :], rT[r, 2 + h // 2, :], rT[r, h // 2, :],
                              start=True, stop=True)
                last.then_inc(retS_ps, 1)

            def ret_O(l, t):
                pe.wait_ge(retS_sb, 2 * ts(l, t))
                pe.wait_ge(rv_sb, hs(l, t // 2))
                if t:
                    pe.wait_ge(state_sb, (NT - 1) * l + t)
                take(5, retO_sb, ts(l, t))
                o = bank[5][:, 0:NH * HD].rearrange("p (h e) -> p h e", h=NH)
                for c in range(2):
                    for h in (2 * c, 2 * c + 1):
                        last = mm(o[:, h, :], sm[:, h, :], rv[:, t, HD * h:HD * (h + 1)], start=h == 0,
                                  stop=t == 0 and h == NH - 1, skip_group_check=True)
                    if t:
                        last = mm(bank[5][:, P * c:P * (c + 1)], rT[:, c, :], state[:, c, :], start=False,
                                  stop=c == 1, skip_group_check=True)
                if t < NT - 1:
                    take(6, state_sb, (NT - 1) * l + t + 1)
                    for c in range(2):
                        pc = slice(P * c, P * (c + 1))
                        last = mm(b128(6)[:, c, :], qk[:, 1, t % 2, pc], rv[:, t, pc], start=True, stop=True)
                last.then_inc(retO_ps, 1)

            def to_channels(b, src, done):
                for c in range(2):
                    for t in range(2):
                        last = transpose(b256(b)[:, c, tok(t)], src[:, t, P * c:P * (c + 1)])
                last.then_inc(done, 1)

            def ret_Y(l, s):
                pe.wait_ge(retN_sb, hs(l, s))
                take(5, ret_z, hs(l, s))
                to_channels(5, osb, retY_ps)

            def conv_T(l, s):
                pe.wait_ge(conv_sb, hs(l, s))
                take(5, convN_sb, hs(l, s))
                for t in range(2):
                    for c in range(2):
                        last = transpose(b256(5)[:, t, P * c:P * (c + 1)], cacc[:, c, tok(t)])
                last.then_inc(convT_ps, 1)

            def conv_Y(l, s):
                pe.wait_ge(convN_sb, hs(l, s))
                take(5, conv_z, hs(l, s))
                to_channels(5, cn, convY_ps)

            def pool_Y(l, s):
                pe.wait_ge(pool_sb, hs(l, s))
                pe.wait_ge(maps_in, 16 * 4 * L)
                take(6, pool_y32, hs(l, s))
                for c in range(2):
                    last = mm(b256(6)[:, c, :], bd[:, l, c, :], pooled[:, c, :], start=True, stop=True)
                last.then_inc(poolY_ps, 1)

            def moba_T(l, t):
                pe.wait_ge(mrot, hs(l, t // 2))
                take(4, mT_sb, ts(l, t))
                for q in range(2):
                    for c in range(2):
                        last = transpose(b128(4)[:, 2 * q + c, :], mqk[:, q, t % 2, P * c:P * (c + 1)])
                last.then_inc(mT_ps, 1)

            def moba_S(l, t, h):
                if h == 0:
                    pe.wait_ge(mT_sb, ts(l, t))
                b, r = (4, 6)[h % 2], rows_of(h)
                take(b, mP, ths(l, t, h))
                q = mqT[r, t % 2, h // 2, :]
                mm(bank[b][:, tok(t)], ident, neg, start=True, stop=False)
                last = mm(bank[b][:, tok(t)], q, mkT[r, h // 2, tok(t)], start=False, stop=True)
                if t:
                    last = mm(bank[b][:, 0:P * t], q, mkT[r, h // 2, 0:P * t], start=True, stop=True)
                last.then_inc(mS_ps, 1)

            def moba_PT(l, t, h):
                pe.wait_ge(mP, ths(l, t, h))
                take(5, mPT_sb, ths(l, t, h))
                for j in range(t + 1):
                    last = transpose(b128(5)[:, j, :], pr[:, h % 2, tok(j)])
                last.then_inc(mPT_ps, 1)

            def moba_O(l, t, h):
                if h == 0:
                    take(7, mO_sb, ts(l, t))
                    pe.wait_ge(mv_sb, hs(l, t // 2))
                pe.wait_ge(mPT_sb, ths(l, t, h))
                for j in range(t + 1):
                    last = mm(bank[7][:, HD * h:HD * (h + 1)], pT[:, h % 2, j, :],
                              mv[:, j, HD * h:HD * (h + 1)], start=j == 0, stop=j == t)
                last.then_inc(mPV, 1)

            def moba_Y(l, s):
                pe.wait_ge(mO_sb, ts(l, 2 * s + 1))
                take(5, moba_y, hs(l, s))
                to_channels(5, mo, mY_ps)

            def moba_stage(l, s, k):
                def th_of(g, i):
                    return 2 * s + g // 2, 2 * (g % 2) + i
                if 1 <= k <= 4:
                    moba_PT(l, *th_of(k - 1, 0))
                if k <= 3:
                    moba_S(l, *th_of(k, 0))
                    moba_S(l, *th_of(k, 1))
                if k >= 2:
                    moba_O(l, *th_of(k - 2, 0))
                    moba_O(l, *th_of(k - 2, 1))
                if 1 <= k <= 4:
                    moba_PT(l, *th_of(k - 1, 1))

            def x_in_T():
                pe.wait_ge(consts_in, 16)
                pe.wait_ge(x_in, 16 * NT)
                for k in range(KT):
                    take(k % 4, xt_sb, k + 1)
                    for t in range(NT):
                        last = transpose(bank[k % 4][:, tok(t)], xin[:, t, P * k:P * (k + 1)])
                    last.then_inc(xt_ps, 1)

            def x_out_T(t):
                pe.wait_ge(x_upd, KT * (post_no("fpost", L - 1, t // 2) + 1))
                for i in range(2):
                    b = i + 2 * (t % 2)
                    take(b, xo_sb, 2 * t + i + 1)
                    for k in range(4):
                        last = transpose(b128(b)[:, k, :], xT[:, 4 * i + k, tok(t)])
                    last.then_inc(xo_ps, 1)

            def small_products(l, at):
                mid_last = l == L - 1
                if l and at == 3: norm_sum("fpost", l - 1, 1)
                if l and at == 5: norm_bcast("fpost", l - 1, 1)
                if at == (8 if l else 2): norm_sum("pre", l, 1)
                if at == (10 if l else 4): norm_bcast("pre", l, 1)
                for s, t0 in ((0, 11), (1, 21)):
                    for i in range(2):
                        if at == t0 + 3 * i: ret_T(l, 2 * s + i)
                        if at == t0 + 3 * i + 1: ret_S(l, 2 * s + i)
                        if at == t0 + 3 * i + 2: ret_O(l, 2 * s + i)
                if at == 21: conv_T(l, 0)
                if at == 23: conv_Y(l, 0)
                if at == 25: pool_Y(l, 0)
                if at == 28: moba_T(l, 0)
                if at == 29: moba_T(l, 1)
                if at == 20: ret_Y(l, 0)
                if at == 31: conv_T(l, 1)
                if at == 33: conv_Y(l, 1)
                if at == 34: pool_Y(l, 1)
                if 31 <= at <= 36: moba_stage(l, 0, at - 31)
                if at == 38: moba_Y(l, 0)
                if at == 39: ret_Y(l, 1)
                if at == 39: moba_T(l, 2)
                if at == 40: moba_T(l, 3)
                if 40 <= at <= 45: moba_stage(l, 1, at - 40)
                if at == 47: moba_Y(l, 1)
                if at == 50: norm_sum("post", l, 0)
                if at == 51: norm_bcast("post", l, 0)
                if at == 54: norm_sum("fpre", l, 0)
                if at == 56: norm_bcast("fpre", l, 0)
                if at == 58: norm_sum("post", l, 1)
                if at == 60: norm_bcast("post", l, 1)
                if at == 64: norm_sum("fpre", l, 1)
                if at == 66: norm_bcast("fpre", l, 1)
                if at == 182: norm_sum("fpost", l, 0)
                if at == 183: norm_bcast("fpost", l, 0)
                if at == 186 and not mid_last: norm_sum("pre", l + 1, 0)
                if at == 188 and not mid_last: norm_bcast("pre", l + 1, 0)
                if at == 186 and mid_last: x_out_T(0)
                if at == 187 and mid_last: x_out_T(1)

            x_in_T()
            norm_sum("pre", 0, 0)
            norm_bcast("pre", 0, 0)
            for l in range(L):
                for i, (slot, s) in enumerate(UNITS):
                    unit(l, slot, s, lambda: small_products(l, 2 * i + 1))
                    small_products(l, 2 * i + 2)
            norm_sum("fpost", L - 1, 1)
            norm_bcast("fpost", L - 1, 1)
            x_out_T(2)
            x_out_T(3)

        @block.scalar
        def _(act):
            A = nc.scalar.activation

            def copy(dst, src, scale=1.0):
                return A(dst, src, ACT.Copy, scale=scale)

            def squares_of_x(kind, l, s):
                n = norm_no(kind, l, s)
                if n:
                    act.wait_ge(ssq_done, n)
                upd = post_no("post" if kind == "fpre" else "fpost", l if kind == "fpre" else l - 1, s) \
                    if kind == "fpre" or l else None
                for c in range(4):
                    if upd is None:
                        act.wait_ge(xt_sb, KT)
                    else:
                        act.wait_ge(x_upd, KT * upd + 2 * c + 2)
                    A(sq[:, 2 * c:2 * c + 2, :], xT[:, 2 * c:2 * c + 2, half(s)],
                      ACT.Square).then_inc(sq_done, 1)

            def squares_of_y(kind, l, s):
                n = norm_no(kind, l, s)
                act.wait_ge(ssq_done, n)
                if kind == "post":
                    act.wait_ge(poolY_ps, hs(l, 1))
                    act.wait_ge((retO_ps, mPV)[s], (ts(l, 3), ths(l, 3, 3))[s])
                else:
                    act.wait_ge(h_lo, KT * (pre_no("fpre", l, s) + 1))
                for c in range(4):
                    if kind == "post":
                        act.wait_ge(unit_done, unit_no(l, OUT0 + c, s))
                        b = unit_bank(OUT0 + c, s)
                    else:
                        act.wait_ge(unit_done, unit_no(l, DN0 + N_DN - 1, s))
                        b = 4 * s + c
                    A(sq[:, 2 * c:2 * c + 2, :], b256(b), ACT.Square, scale=UNSCALE).then_inc(sq_done, 1)
                    copy(yT[:, s, 2 * c:2 * c + 2, :], b256(b), UNSCALE).then_inc(y_sb, 1)

            def h_split_hi(kind, l, s):
                n = norm_no(kind, l, s)
                act.wait_ge(xr_done, n + 1)
                if kind == "fpre":
                    act.wait_ge(unit_done, unit_no(l, RG, s))
                elif l:
                    act.wait_ge(unit_done, unit_no(l - 1, GU0 + N_GU - 1, s))
                for k in range(KT):
                    copy(hT[:, 0, k, half(s)], yT[:, s, k, :], gain(kind, l, k)).then_inc(h_hi, 1)

            def hi_of(src, ready, kt, l, s, scale, done):
                act.wait_ge(ready, hs(l, s))
                copy(ycat[:, 0, kt:kt + 2, half(s)], src, scale).then_inc(done, 1)

            def glu_tanh(l, s):
                act.wait_ge(unit_done, unit_no(l, CONV_G, s))
                if l or s:
                    act.wait_ge(hb_sb, hs(l, s) - 1)
                if l and s == 0:
                    act.wait_ge(ret_g, 2 * l)
                A(th, b256(unit_bank(CONV_G, s)), ACT.Tanh, scale=0.5 * UNSCALE).then_inc(glu_th, 1)

            def rg_tanh(l, s):
                act.wait_ge(unit_done, unit_no(l, RG, s))
                act.wait_ge(hb_sb, hs(l, 1))
                act.wait_ge(conv_y32, hs(l, s))
                if s:
                    act.wait_ge(ret_g, hs(l, 0))
                A(th, b256(unit_bank(RG, s)), ACT.Tanh, scale=0.5 * UNSCALE).then_inc(rg_th, 1)

            def conv_tanh(l, s):
                act.wait_ge(convY_ps, hs(l, s))
                act.wait_ge(hb_sb, hs(l, 1))
                if s:
                    act.wait_ge(ret_g, hs(l, 0))
                for c in range(2):
                    A(th[:, c, :], b256(5)[:, c, :], ACT.Tanh, scale=px(l, "lng", c),
                      bias=px(l, "lnb", c)).then_inc(conv_th, 1)

            def from_unit(l, slot, s, dst, done):
                act.wait_ge(unit_done, unit_no(l, slot, s))
                copy(dst, b256(unit_bank(slot, s)), UNSCALE).then_inc(done, 1)

            def ret_T_copy(l, t):
                act.wait_ge(retT_ps, ts(l, t))
                if l or t:
                    act.wait_ge(retO_ps, ts(l, t) - 1)
                copy(rT, b128(4)).then_inc(retT_sb, 1)

            def ret_O_copy(l, t):
                act.wait_ge(retO_ps, ts(l, t))
                if hs(l, t // 2) > 1:
                    act.wait_ge(retY_ps, hs(l, t // 2) - 1)
                copy(osb[:, t % 2, :], bank[5][:, 0:G]).then_inc(retO_sb, 1)

            def m_qk(l, s):
                for q, (slot, done) in enumerate(((MQ, mq_sb), (MK, mk_sb))):
                    act.wait_ge(unit_done, unit_no(l, slot, s))
                    if l or s:
                        act.wait_ge(mT_ps, ts(l, 2 * s) - 1)
                    copy(mqk[:, q, :, :], b256(unit_bank(slot, s)),
                         UNSCALE * (HD ** -0.5 if q == 0 else 1.0)).then_inc(done, 1)

            def m_T_copy(l, t):
                act.wait_ge(mT_ps, ts(l, t))
                if ts(l, t) > 2:
                    act.wait_ge(mS_ps, ths(l, t, 3) - 2 * NH)
                if l:
                    act.wait_ge(mS_ps, ths(l - 1, NT - 1, NH - 1))
                copy(mqT[:, t % 2, :, :], b128(4)[:, 0:2, :]).then_inc(act_tick, 1)
                copy(mkT[:, :, tok(t)], b128(4)[:, 2:4, :]).then_inc(mT_sb, 1)

            def m_exp(l, t, h):
                i = ths(l, t, h)
                act.wait_ge(mM, i)
                if i > 2:
                    act.wait_ge(mPT_ps, i - 2)
                if ts(l, t) > 2:
                    act.wait_ge(mO_sb, ts(l, t) - 2)
                c = (i - 1) % 8
                w = P * (t + 1)
                A(pr[:, h % 2, 0:w], bank[(4, 6)[h % 2]][:, 0:w], ACT.Exp, bias=nms[:, c:c + 1],
                  accum_out=sums[:, c:c + 1]).then_inc(mP, 1)

            def m_PT_copy(l, t, h):
                i = ths(l, t, h)
                act.wait_ge(mPT_ps, i)
                if i > 2:
                    act.wait_ge(mPV, i - 2)
                copy(pT[:, h % 2, 0:t + 1, :], b128(5)[:, 0:t + 1, :]).then_inc(mPT_sb, 1)

            def m_stage(l, s, k):
                def th_of(g, i):
                    return 2 * s + g // 2, 2 * (g % 2) + i
                if 1 <= k <= 4:
                    m_PT_copy(l, *th_of(k - 1, 0))
                if k <= 3:
                    m_exp(l, *th_of(k, 0))
                    m_exp(l, *th_of(k, 1))
                if 1 <= k <= 4:
                    m_PT_copy(l, *th_of(k - 1, 1))

            def silu(l, f, s):
                n = fno(l, f, s)
                act.wait_ge(unit_done, unit_no(l, GU0 + f, s))
                if n > 2:
                    act.wait_ge(f_sb, n - 2)
                A(sil[:, n % 2, :], b256(unit_bank(GU0 + f, s))[:, 0, :], ACT.Silu,
                  scale=UNSCALE).then_inc(sil_done, 1)

            def hidden_hi(l, f, s):
                n = fno(l, f, s)
                act.wait_ge(f_sb, n)
                copy(fT[:, 0, f, half(s)], fbuf[:, n % 2, :]).then_inc(f_hi, 1)

            def hidden_steps(l, i0, i1):
                for i in range(i0, i1):
                    silu(l, *HIDDEN[i])
                    if i:
                        hidden_hi(l, *HIDDEN[i - 1])

            act.wait_ge(setup_done, 1)
            for k in range(KT):
                act.wait_ge(xt_ps, k + 1)
                copy(xT[:, k, :], bank[k % 4][:, :]).then_inc(xt_sb, 1)
            squares_of_x("pre", 0, 0)
            h_split_hi("pre", 0, 0)
            for l in range(L):
                if l:
                    squares_of_y("fpost", l - 1, 1)
                    glu_tanh(l, 0)
                    squares_of_x("pre", l, 1)
                else:
                    squares_of_x("pre", l, 1)
                    glu_tanh(l, 0)
                h_split_hi("pre", l, 1)
                from_unit(l, RV, 0, rv[:, 0:2, :], rv_sb)
                ret_T_copy(l, 0)
                ret_O_copy(l, 0)
                glu_tanh(l, 1)
                ret_T_copy(l, 1)
                ret_O_copy(l, 1)
                from_unit(l, RV, 1, rv[:, 2:4, :], rv_sb)
                ret_T_copy(l, 2)
                ret_O_copy(l, 2)
                from_unit(l, POOL, 0, ubuf[:, :, 16:16 + HALF], pool_u)
                conv_tanh(l, 0)
                hi_of(ybuf, conv_y32, 0, l, 0, 0.5 * A_SCALE, conv_hi)
                ret_T_copy(l, 3)
                m_qk(l, 0)
                ret_O_copy(l, 3)
                hi_of(ybuf, pool_y32, 6, l, 0, A_SCALE, pool_hi)
                m_T_copy(l, 0)
                from_unit(l, MV, 0, mv[:, 0:2, :], mv_sb)
                m_T_copy(l, 1)
                rg_tanh(l, 0)
                hi_of(ybuf, ret_y32, 2, l, 0, 0.5 * A_SCALE * UNSCALE, ret_hi)
                m_stage(l, 0, 0)
                from_unit(l, POOL, 1, ubuf[:, :, 16 + HALF:16 + S], pool_u)
                m_stage(l, 0, 1)
                conv_tanh(l, 1)
                m_stage(l, 0, 2)
                hi_of(ybuf, conv_y32, 0, l, 1, 0.5 * A_SCALE, conv_hi)
                m_stage(l, 0, 3)
                hi_of(ybuf, pool_y32, 6, l, 1, A_SCALE, pool_hi)
                m_stage(l, 0, 4)
                m_qk(l, 1)
                hi_of(b256(5), mY_ps, 4, l, 0, A_SCALE, moba_hi)
                from_unit(l, MV, 1, mv[:, 2:4, :], mv_sb)
                m_T_copy(l, 2)
                rg_tanh(l, 1)
                m_T_copy(l, 3)
                m_stage(l, 1, 0)
                hi_of(ybuf, ret_y32, 2, l, 1, 0.5 * A_SCALE * UNSCALE, ret_hi)
                for k in range(1, 5):
                    m_stage(l, 1, k)
                hi_of(b256(5), mY_ps, 4, l, 1, A_SCALE, moba_hi)
                for s in range(2):
                    squares_of_y("post", l, s)
                    squares_of_x("fpre", l, s)
                    if s:
                        hidden_steps(l, 0, GU_EARLY)
                    h_split_hi("fpre", l, s)
                hidden_steps(l, GU_EARLY, 2 * FT)
                hidden_hi(l, *HIDDEN[-1])
                squares_of_y("fpost", l, 0)
                if l + 1 < L:
                    squares_of_x("pre", l + 1, 0)
                    h_split_hi("pre", l + 1, 0)
            for t in range(NT):
                if t == 2:
                    squares_of_y("fpost", L - 1, 1)
                for i in range(2):
                    act.wait_ge(xo_ps, 2 * t + i + 1)
                    copy(xout[:, t, 4 * P * i:4 * P * (i + 1)],
                         bank[i + 2 * (t % 2)][:, :]).then_inc(xo_sb, 1)

        @block.vector
        def _(dve):
            V = nc.vector
            ticks = [0]

            def tick(ins):
                ins.then_inc(dve_tick, 1)
                ticks[0] += 1
                return ticks[0]

            def after(n=None):
                dve.wait_ge(dve_tick, ticks[0] if n is None else n)

            def rsqrt(n):
                xx, tt, yy = rsx[:, 0:n], rst[:, 0:n], rsy[:, 0:n]
                after()
                tick(V.tensor_scalar(tt.bitcast(I32), xx.bitcast(I32), 1, None, ALU.logical_shift_right))
                after()
                tick(V.tensor_scalar(yy.bitcast(I32), tt.bitcast(I32), -1.0, RSQRT_MAGIC, ALU.mult, ALU.add))
                for _ in range(3):
                    after()
                    tick(V.scalar_tensor_tensor(out=tt, in0=yy, scalar=-0.5, in1=yy, op0=ALU.mult, op1=ALU.mult))
                    after()
                    tick(V.tensor_tensor(tt, tt, xx, ALU.mult))
                    after()
                    tick(V.scalar_tensor_tensor(out=yy, in0=tt, scalar=1.5, in1=yy, op0=ALU.add, op1=ALU.mult))
                after()

            def split_lo(slot):
                if slot >= L * SLOTS:
                    return
                assert dve_splits(slot)
                for part in range(2):
                    n = 2 * slot + part
                    dve.wait_ge(hi_split, n + 1)
                    V.scalar_tensor_tensor(out=ring[:, slot % RING, 1, raw_part(part)], in0=raw[:, n % NRAW, :],
                                           scalar=W_SCALE, in1=ring[:, slot % RING, 0, raw_part(part)],
                                           op0=ALU.mult, op1=ALU.subtract).then_inc(lo_dve, 1)

            def norm_reduce(kind, l, s):
                n = norm_no(kind, l, s)
                dve.wait_ge(sq_done, 4 * (n + 1))
                if n:
                    dve.wait_ge(nsum_ps, n)
                V.reduce_sum(ssq, sq[:, :, :].rearrange("p k t -> p t k"), axis=AX_X).then_inc(ssq_done, 1)

            def norm_diag(kind, l, s):
                n, b = norm_no(kind, l, s), norm_bank(kind, l, s)
                dve.wait_ge(nsum_ps, n + 1)
                tick(V.tensor_scalar(rsx[:, 0:2], bank[b][:, 0:2], 1.0 / DM, 1e-6, ALU.mult, ALU.add))
                rsqrt(2)
                if n:
                    dve.wait_ge(rstd_ps, n)
                tick(V.tensor_scalar(diag[:, 0:P], ident, rsy[:, 0:1], None, ALU.mult))
                V.tensor_scalar(diag[:, P:2 * P], ident, rsy[:, 1:2], None, ALU.mult).then_inc(diag_done, 1)

            def norm_scale(kind, l, s):
                n, b = norm_no(kind, l, s), norm_bank(kind, l, s)
                pre = kind in ("pre", "fpre")
                dve.wait_ge(rstd_ps, n + 1)
                if not pre:
                    dve.wait_ge(y_sb, 4 * (post_no(kind, l, s) + 1))
                elif n < 2:
                    dve.wait_ge(xt_ps, KT)
                src = xT[:, :, half(s)] if pre else yT[:, s, :, :]
                V.tensor_tensor(yT[:, s, :, :], src,
                                bank[b][:, HALF:2 * HALF].unsqueeze(1).to_broadcast([P, KT, HALF]),
                                ALU.mult).then_inc(xr_done, 1)

            def residual(kind, l, s):
                n = norm_no(kind, l, s)
                dve.wait_ge(xr_done, n + 1)
                name = {"post": "post", "fpost": "fpost"}[kind]
                for k in range(KT):
                    V.scalar_tensor_tensor(out=xT[:, k, half(s)], in0=yT[:, s, k, :],
                                           scalar=par_col(l, name, k), in1=xT[:, k, half(s)],
                                           op0=ALU.mult, op1=ALU.add).then_inc(x_upd, 1)

            def h_split_lo(kind, l, s):
                m = pre_no(kind, l, s)
                for k in range(KT):
                    dve.wait_ge(h_hi, KT * m + k + 1)
                    V.scalar_tensor_tensor(out=hT[:, 1, k, half(s)], in0=yT[:, s, k, :],
                                           scalar=gain(kind, l, k), in1=hT[:, 0, k, half(s)],
                                           op0=ALU.mult, op1=ALU.subtract).then_inc(h_lo, 1)

            def lo_of(src, ready, kt, l, s, scale, done):
                dve.wait_ge(ready, hs(l, s))
                V.scalar_tensor_tensor(out=ycat[:, 1, kt:kt + 2, half(s)], in0=src, scalar=scale,
                                       in1=ycat[:, 0, kt:kt + 2, half(s)], op0=ALU.mult,
                                       op1=ALU.subtract).then_inc(done, 1)

            def glu(l, s):
                dve.wait_ge(unit_done, unit_no(l, CONV_A, s))
                dve.wait_ge(glu_th, hs(l, s))
                at = CW - 1 + HALF * s
                V.scalar_tensor_tensor(out=hbuf[:, :, at:at + HALF], in0=th, scalar=1.0,
                                       in1=b256(unit_bank(CONV_A, s)), op0=ALU.add,
                                       op1=ALU.mult).then_inc(hb_sb, 1)

            conv_at = [0, 0]

            def conv(l, s, k0, k1):
                if k0 == 0:
                    dve.wait_ge(hb_sb, hs(l, s))
                    if hs(l, s) > 1:
                        dve.wait_ge(convT_ps, hs(l, s) - 1)
                for k in range(k0, k1):
                    for c in range(2):
                        src = hbuf[:, c, HALF * s + k:HALF * s + k + HALF]
                        w = px(l, "cw", 2 * k + c)
                        if k == 0:
                            ins = V.tensor_scalar(cacc[:, c, :], src, w, par_col(l, "cb", c), ALU.mult, ALU.add)
                        else:
                            after(conv_at[c])
                            ins = V.scalar_tensor_tensor(out=cacc[:, c, :], in0=src, scalar=w,
                                                         in1=cacc[:, c, :], op0=ALU.mult, op1=ALU.add)
                        if k == CW - 1 and c == 1:
                            ins.then_inc(conv_sb, 1)
                        else:
                            conv_at[c] = tick(ins)

            def conv_norm(l, s):
                dve.wait_ge(convT_ps, hs(l, s))
                for t in range(2):
                    tick(V.bn_stats(cst_st[:, 6 * t:6 * t + 6], b256(5)[:, t, :]))
                after()
                for t in range(2):
                    tick(V.bn_aggr(cmv[:, 2 * t:2 * t + 2], cst_st[:, 6 * t:6 * t + 6]))
                after()
                tick(V.tensor_scalar(rsx[:, 0:2], cmv.rearrange("p (t v) -> p t v", v=2)[:, :, 1], 1e-5, None,
                                     ALU.add))
                rsqrt(2)
                if hs(l, s) > 1:
                    dve.wait_ge(convY_ps, hs(l, s) - 1)
                for t in range(2):
                    ins = V.tensor_scalar(cn[:, t, :], b256(5)[:, t, :], cmv[:, 2 * t:2 * t + 1],
                                          rsy[:, t:t + 1], ALU.subtract, ALU.mult)
                    if t == 0:
                        tick(ins)
                    else:
                        ins.then_inc(convN_sb, 1)

            def conv_out(l, s):
                dve.wait_ge(convY_ps, hs(l, s))
                dve.wait_ge(conv_th, 2 * hs(l, s))
                if l or s:
                    dve.wait_ge(ret_y, hs(l, s) - 1)
                tick(V.tensor_scalar(ybuf[:, 0, :], b256(5)[:, 0, :], par_col(l, "lng", 0),
                                     par_col(l, "lnb", 0), ALU.mult, ALU.add))
                V.tensor_scalar(ybuf[:, 1, :], b256(5)[:, 1, :], par_col(l, "lng", 1),
                                par_col(l, "lnb", 1), ALU.mult, ALU.add).then_inc(conv_z, 1)
                dve.wait_ge(conv_z, hs(l, s))
                V.scalar_tensor_tensor(out=ybuf, in0=th, scalar=1.0, in1=ybuf, op0=ALU.add,
                                       op1=ALU.mult).then_inc(conv_y32, 1)

            scratch_read = []

            def rotate(out_, u, cos, sin, n, w):
                ma = m1[:, 0:2 * n * w].rearrange("p (a h d) -> p a h d", a=n, h=2)
                mb = m2[:, 0:2 * n * w].rearrange("p (a h d) -> p a h d", a=n, h=2)
                for sem_, value in scratch_read:
                    dve.wait_ge(sem_, value)
                tick(V.tensor_tensor(ma, u, cos.unsqueeze(2).to_broadcast([P, n, 2, w]), ALU.mult))
                tick(V.scalar_tensor_tensor(out=mb[:, :, 0, :], in0=u[:, :, 1, :], scalar=-1.0, in1=sin,
                                            op0=ALU.mult, op1=ALU.mult))
                tick(V.tensor_tensor(mb[:, :, 1, :], u[:, :, 0, :], sin, ALU.mult))
                after()
                return V.tensor_tensor(out_, ma, mb, ALU.add)

            def table(name, s, w):
                n = 2 * NH * w
                return C(name)[:, s * n:(s + 1) * n].rearrange("p (a d) -> p a d", d=w)

            def ret_rotate(l, s, q):
                slot = (RQ, RK)[q]
                dve.wait_ge(unit_done, unit_no(l, slot, s))
                if l or s:
                    dve.wait_ge(retO_ps, ts(l, 2 * s) - 1)
                u = bank[unit_bank(slot, s)][:, :].rearrange("p (a h d) -> p a h d", h=2, d=32)
                dst = qk[:, q, :, :].rearrange("p t (a h d) -> p (t a) h d", h=2, d=32)
                rotate(dst, u, table(("rqc", "rkc")[q], s, 32), table(("rqs", "rks")[q], s, 32), 2 * NH,
                       32).then_inc(rot_done, 1)
                scratch_read[:] = [(rot_done, 2 * hs(l, s) - 1 + q)]

            def moba_rotate(l, s):
                dve.wait_ge(mq_sb, hs(l, s))
                dve.wait_ge(mk_sb, hs(l, s))
                for q in range(2):
                    u = mqk[:, q, :, :].rearrange("p t (a d) -> p (t a) d", d=HD)[:, :, 0:16].rearrange(
                        "p a (h d) -> p a h d", h=2)
                    ins = rotate(u, u, table("mc", s, 8), table("ms", s, 8), 2 * NH, 8)
                    if q == 0:
                        scratch_read[:] = [(dve_tick, tick(ins))]
                    else:
                        ins.then_inc(mrot, 1)
                        scratch_read[:] = [(mrot, hs(l, s))]

            def ret_mask(l, t):
                dve.wait_ge(retS_ps, ts(l, t))
                if l or t:
                    dve.wait_ge(retO_ps, ts(l, t) - 1)
                smv = sm.rearrange("p (c two) t -> p two c t", two=2)
                for e, b in ((0, 6), (1, 4)):
                    V.tensor_tensor(smv[:, e, :, :], b128(b)[:, 0:2, :],
                                    tri.unsqueeze(1).to_broadcast([P, 2, P]), ALU.mult).then_inc(retS_sb, 1)

            def ret_state(l, t):
                dve.wait_ge(retO_ps, ts(l, t))
                if t == 0:
                    after(zeroed[0])
                else:
                    dve.wait_ge(state_sb, (NT - 1) * l + t)
                for i in range(2):
                    r = slice(HD * i, HD * i + HD)
                    ins = V.tensor_tensor(state[r, :, r], state[r, :, r], b128(6)[r, 0:2, r], ALU.add)
                    if i == 0:
                        tick(ins)
                    else:
                        ins.then_inc(state_sb, 1)

            def ret_norm(l, s):
                dve.wait_ge(retO_sb, ts(l, 2 * s + 1))
                for i in range(8):
                    o = osb[:, i // NH, HD * (i % NH):HD * (i % NH + 1)]
                    tick(V.bn_stats(bst[:, 6 * i:6 * i + 6], o))
                for i in range(8):
                    after(ticks[0] - 7)
                    tick(V.bn_aggr(mvr[:, 2 * i:2 * i + 2], bst[:, 6 * i:6 * i + 6]))
                after()
                tick(V.tensor_scalar(rsx[:, 0:8], mvr.rearrange("p (i v) -> p i v", v=2)[:, :, 1], 1e-5, None,
                                     ALU.add))
                rsqrt(8)
                for i in range(8):
                    o = osb[:, i // NH, HD * (i % NH):HD * (i % NH + 1)]
                    ins = V.tensor_scalar(o, o, mvr[:, 2 * i:2 * i + 1], rsy[:, i:i + 1], ALU.subtract, ALU.mult)
                    if i < 7:
                        tick(ins)
                    else:
                        ins.then_inc(retN_sb, 1)

            def ret_affine(l, s):
                dve.wait_ge(retY_ps, hs(l, s))
                for c in range(2):
                    ins = V.tensor_scalar(rz[:, c, :], b256(5)[:, c, :], par_col(l, "gng", c),
                                          par_col(l, "gnb", c), ALU.mult, ALU.add)
                    if c == 0:
                        tick(ins)
                    else:
                        ins.then_inc(ret_z, 1)

            def ret_out(l, s):
                dve.wait_ge(rg_th, hs(l, s))
                dve.wait_ge(ret_z, hs(l, s))
                V.scalar_tensor_tensor(out=rz, in0=th, scalar=1.0, in1=rz, op0=ALU.add,
                                       op1=ALU.mult).then_inc(ret_g, 1)
                dve.wait_ge(ret_g, hs(l, s))
                dve.wait_ge(pool_y, hs(l, s))
                V.tensor_tensor(ybuf, rz, b256(unit_bank(RG, s)), ALU.mult).then_inc(ret_y32, 1)

            def pool_windows(l, s):
                dve.wait_ge(pool_u, hs(l, s))
                if hs(l, s) > 1:
                    dve.wait_ge(poolY_ps, hs(l, s) - 1)
                if s == 0:
                    after(zeroed[0])
                at = 16 + HALF * s
                tick(V.tensor_tensor(t2, ubuf[:, :, at - 14:at + HALF], ubuf[:, :, at - 15:at + HALF - 1],
                                     ALU.add))
                after()
                tick(V.tensor_tensor(t4, t2[:, :, 2:], t2[:, :, 0:HALF + 12], ALU.add))
                after()
                tick(V.tensor_tensor(t8, t4[:, 1, 4:], t4[:, 1, 0:HALF + 8], ALU.add))
                after()
                lo, hi_ = slice(0, HD), slice(HD, P)
                w16 = m1[:, 0:HALF]
                tick(V.tensor_tensor(w16[hi_, :], t8[hi_, 8:], t8[hi_, 0:HALF], ALU.add))
                after()
                sums_ = [(lo, 0, t2[lo, 0, 14:]), (hi_, 0, t4[hi_, 0, 12:]), (lo, 1, t8[lo, 8:]),
                         (hi_, 1, w16[hi_, :])]
                if s == 0:
                    for r, c, v in sums_:
                        tick(V.tensor_tensor(v[:, 0:16], v[:, 0:16], C("adj")[r, 16 * c:16 * c + 16], ALU.mult))
                    after()
                for i, (r, c, v) in enumerate(sums_):
                    ins = V.scalar_tensor_tensor(out=pooled[r, c, :], in0=v, scalar=1.0 / WINDOWS[i],
                                                 in1=ubuf[r, c, at:at + HALF], op0=ALU.mult, op1=ALU.subtract)
                    if i < 3:
                        tick(ins)
                    else:
                        ins.then_inc(pool_sb, 1)

            def pool_out(l, s):
                dve.wait_ge(poolY_ps, hs(l, s))
                dve.wait_ge(conv_y, hs(l, s))
                tick(V.tensor_scalar(ybuf[:, 0, :], b256(6)[:, 0, :], par_col(l, "pb", 0),
                                     par_col(l, "ps", 0), ALU.add, ALU.mult))
                V.tensor_scalar(ybuf[:, 1, :], b256(6)[:, 1, :], par_col(l, "pb", 1),
                                par_col(l, "ps", 1), ALU.add, ALU.mult).then_inc(pool_y32, 1)

            def m_max(l, t, h):
                i = ths(l, t, h)
                dve.wait_ge(mS_ps, i)
                if i > 8:
                    dve.wait_ge(mP, i - 8)
                c = (i - 1) % 8
                V.tensor_reduce(nms[:, c:c + 1], bank[(4, 6)[h % 2]][:, 0:P * (t + 1)], AX_X, ALU.max,
                                negate=True).then_inc(mM, 1)

            def m_norm(l, t):
                dve.wait_ge(mPV, ths(l, t, NH - 1))
                dve.wait_ge(mP, ths(l, t, NH - 1))
                c = NH * (t % 2)
                tick(V.reciprocal(rinv[:, c:c + NH], sums[:, c:c + NH]))
                after()
                if hs(l, t // 2) > 1:
                    dve.wait_ge(mY_ps, hs(l, t // 2) - 1)
                V.tensor_tensor(mo[:, t % 2, :].rearrange("p (h e) -> p h e", h=NH),
                                bank[7][:, 0:G].rearrange("p (h e) -> p h e", h=NH),
                                rinv[:, c:c + NH].unsqueeze(2).to_broadcast([P, NH, HD]),
                                ALU.mult).then_inc(mO_sb, 1)

            def hidden(l, f, s):
                n = fno(l, f, s)
                dve.wait_ge(sil_done, n)
                if n > 2:
                    dve.wait_ge(f_lo, n - 2)
                V.scalar_tensor_tensor(out=fbuf[:, n % 2, :], in0=b256(unit_bank(GU0 + f, s))[:, 1, :],
                                       scalar=UNSCALE * A_SCALE, in1=sil[:, n % 2, :], op0=ALU.mult,
                                       op1=ALU.mult).then_inc(f_sb, 1)

            def hidden_lo(l, f, s):
                n = fno(l, f, s)
                dve.wait_ge(f_hi, n)
                V.tensor_tensor(fT[:, 1, f, half(s)], fbuf[:, n % 2, :], fT[:, 0, f, half(s)],
                                ALU.subtract).then_inc(f_lo, 1)

            def hidden_steps(l, i0, i1):
                for i in range(i0, i1):
                    f, s = HIDDEN[i]
                    hidden(l, f, s)
                    if i:
                        hidden_lo(l, *HIDDEN[i - 1])
                    if s:
                        split_lo(l * SLOTS + GU0 + f + RING)

            zeroed = [0]
            tick(V.memset(bd[:, :, :, :], 0.0))
            tick(V.memset(hbuf[:, :, 0:CW - 1], 0.0))
            dve.wait_ge(consts_in, 16)
            dve.wait_ge(params_in, 16)
            for l in range(L):
                for name, cols, scale in PARX_FROM:
                    last = V.tensor_scalar(parx[:, l, PARX[name]:PARX[name] + cols],
                                           par[:, l, PAR[name]:PAR[name] + cols], scale, None, ALU.mult)
                    if (l, name) != (L - 1, PARX_FROM[-1][0]):
                        tick(last)
            last.then_inc(setup_done, 1)
            dve.wait_ge(setup_done, 1)
            after()
            for slot in FIRST_BY_DVE:
                split_lo(slot)
            norm_reduce("pre", 0, 0)
            norm_diag("pre", 0, 0)
            norm_scale("pre", 0, 0)
            h_split_lo("pre", 0, 0)
            for l in range(L):
                if l:
                    norm_reduce("fpost", l - 1, 1)
                    norm_diag("fpost", l - 1, 1)
                    glu(l, 0)
                    norm_scale("fpost", l - 1, 1)
                    residual("fpost", l - 1, 1)
                norm_reduce("pre", l, 1)
                norm_diag("pre", l, 1)
                if not l:
                    norm_scale("pre", l, 1)
                    h_split_lo("pre", l, 1)
                    glu(l, 0)
                ret_rotate(l, 0, 0)
                ret_rotate(l, 0, 1)
                if l:
                    norm_scale("pre", l, 1)
                    h_split_lo("pre", l, 1)
                dve.wait_ge(unit_done, unit_no(l, CONV_A, 0))
                tick(V.memset(state, 0.0))
                zeroed[0] = tick(V.memset(ubuf[:, :, 0:16], 0.0))
                conv(l, 0, 0, 3)
                ret_mask(l, 0)
                conv(l, 0, 3, 6)
                ret_state(l, 0)
                conv(l, 0, 6, 9)
                glu(l, 1)
                ret_mask(l, 1)
                conv(l, 0, 9, 12)
                ret_state(l, 1)
                conv(l, 0, 12, 16)
                ret_norm(l, 0)
                conv(l, 0, 16, 20)
                ret_affine(l, 0)
                conv(l, 0, 20, 24)
                ret_rotate(l, 1, 0)
                conv(l, 0, 24, CW)
                ret_rotate(l, 1, 1)
                conv_norm(l, 0)
                ret_mask(l, 2)
                conv(l, 1, 0, 3)
                conv_out(l, 0)
                ret_state(l, 2)
                pool_windows(l, 0)
                lo_of(ybuf, conv_hi, 0, l, 0, 0.5 * A_SCALE, conv_y)
                ret_mask(l, 3)
                conv(l, 1, 3, 8)
                pool_out(l, 0)
                conv(l, 1, 8, 12)
                lo_of(ybuf, pool_hi, 6, l, 0, A_SCALE, pool_y)
                moba_rotate(l, 0)
                conv(l, 1, 12, 26)
                ret_out(l, 0)
                conv(l, 1, 26, CW)
                lo_of(ybuf, ret_hi, 2, l, 0, 0.5 * A_SCALE * UNSCALE, ret_y)
                m_max(l, 0, 0)
                m_max(l, 0, 1)
                conv_norm(l, 1)
                m_max(l, 0, 2)
                m_max(l, 0, 3)
                pool_windows(l, 1)
                conv_out(l, 1)
                m_max(l, 1, 0)
                m_max(l, 1, 1)
                lo_of(ybuf, conv_hi, 0, l, 1, 0.5 * A_SCALE, conv_y)
                pool_out(l, 1)
                m_norm(l, 0)
                m_max(l, 1, 2)
                m_max(l, 1, 3)
                lo_of(ybuf, pool_hi, 6, l, 1, A_SCALE, pool_y)
                m_norm(l, 1)
                ret_norm(l, 1)
                lo_of(b256(5), moba_hi, 4, l, 0, A_SCALE, moba_y)
                moba_rotate(l, 1)
                ret_affine(l, 1)
                m_max(l, 2, 0)
                m_max(l, 2, 1)
                ret_out(l, 1)
                m_max(l, 2, 2)
                m_max(l, 2, 3)
                lo_of(ybuf, ret_hi, 2, l, 1, 0.5 * A_SCALE * UNSCALE, ret_y)
                m_max(l, 3, 0)
                m_max(l, 3, 1)
                m_norm(l, 2)
                m_max(l, 3, 2)
                m_max(l, 3, 3)
                m_norm(l, 3)
                lo_of(b256(5), moba_hi, 4, l, 1, A_SCALE, moba_y)
                for s in range(2):
                    norm_reduce("post", l, s)
                    norm_diag("post", l, s)
                    norm_scale("post", l, s)
                    residual("post", l, s)
                    norm_reduce("fpre", l, s)
                    if s:
                        hidden_steps(l, 0, GU_EARLY)
                    norm_diag("fpre", l, s)
                    norm_scale("fpre", l, s)
                    h_split_lo("fpre", l, s)
                hidden_steps(l, GU_EARLY, 2 * FT)
                hidden_lo(l, *HIDDEN[-1])
                for c in range(N_DN - DN_TAIL):
                    split_lo(l * SLOTS + DN0 + c + RING)
                norm_reduce("fpost", l, 0)
                norm_diag("fpost", l, 0)
                norm_scale("fpost", l, 0)
                residual("fpost", l, 0)
                if l + 1 < L:
                    norm_reduce("pre", l + 1, 0)
                    norm_diag("pre", l + 1, 0)
                    norm_scale("pre", l + 1, 0)
                    h_split_lo("pre", l + 1, 0)
            norm_reduce("fpost", L - 1, 1)
            norm_diag("fpost", L - 1, 1)
            norm_scale("fpost", L - 1, 1)
            residual("fpost", L - 1, 1)


def rotary_table(dim, theta, np):
    inv = 1.0 / (theta ** (np.arange(0, dim, 2, dtype=np.float32) / np.float32(dim)))
    ang = (np.arange(S, dtype=np.float32)[:, None] * inv[None, :].astype(np.float32)).astype(np.float32)
    return np.cos(ang), np.sin(ang)


def constants():
    import numpy as np
    c = np.zeros((P, CST_COLS), np.float32)

    def put(name, a):
        c[:, CST[name]:CST[name] + a.shape[1]] = a

    i = np.arange(P)
    put("ident", np.eye(P))
    put("ones", np.ones((P, P)))
    put("tri", (i[:, None] <= i[None, :]))
    put("neg", np.where(i[None, :] > i[:, None], -1e30, 0.0))
    pos = np.arange(S, dtype=np.float64)
    gamma = 1.0 - 2.0 ** (-5.0 - np.arange(NH))
    grow = gamma[None, :] ** (pos[:, None] + 1.0)
    cos, sin = rotary_table(HD, 10000.0, np)

    def tiles(a):
        return a.reshape(NT, P, -1).transpose(1, 0, 2).reshape(P, -1)

    for name, trig, decay in (("rqc", cos, grow * UNSCALE), ("rqs", sin, grow * UNSCALE),
                              ("rkc", cos, UNSCALE * HD ** -0.5 / grow),
                              ("rks", sin, UNSCALE * HD ** -0.5 / grow)):
        put(name, tiles(trig[:, None, :] * decay[:, :, None]))
    mcos, msin = rotary_table(HD // 4, 500000.0, np)
    for name, trig in (("mc", mcos), ("ms", msin)):
        put(name, tiles(np.repeat(trig[:, None, :], NH, axis=1)))
    adj = np.ones((P, 2, 16))
    for g, w in enumerate(WINDOWS):
        rows = slice(HD * (g % 2), HD * (g % 2) + HD)
        adj[rows, g // 2, :] = w / np.minimum(np.arange(16) + 1.0, w)
    put("adj", adj.reshape(P, 32))
    return c


def kernel(x, attn_pre_g, w_in, conv_w, conv_b, conv_ln_g, conv_ln_b, ret_gn_g, ret_gn_b, pool_w, pool_b,
           pool_scale, w_out, attn_post_g, ffn_pre_g, w_gate, w_up, w_down, ffn_post_g):
    import numpy as np
    import concourse.bacc as bacc
    from concourse.bass_utils import run_bass_kernel_spmd

    w_in, w_out, w_gate, w_up, w_down = map(np.asarray, (w_in, w_out, w_gate, w_up, w_down))
    weights = np.empty((L, SLOTS, P, SLOT), np.float32)
    by_col = w_in.reshape(L, KT, P, N_IN, G)
    for slot, blk in BLOCK_OF.items():
        weights[:, slot] = by_col[:, :, :, blk].transpose(0, 2, 1, 3).reshape(L, P, SLOT)
    weights[:, OUT0:GU0] = w_out.reshape(L, KT, P, N_OUT, 2 * P).transpose(0, 3, 2, 1, 4).reshape(
        L, N_OUT, P, SLOT)
    gu = np.stack([w_gate.reshape(L, KT, P, FT, P), w_up.reshape(L, KT, P, FT, P)], axis=4)
    weights[:, GU0:DN0] = gu.transpose(0, 3, 2, 1, 4, 5).reshape(L, N_GU, P, SLOT)
    weights[:, DN0:] = w_down.reshape(L, N_DN, 2, P, DM).transpose(0, 1, 3, 2, 4).reshape(L, N_DN, P, SLOT)

    params = np.empty((P, L, PAR_COLS), np.float32)
    for name, a in (("pre", attn_pre_g), ("post", attn_post_g), ("fpre", ffn_pre_g), ("fpost", ffn_post_g),
                    ("cw", conv_w), ("cb", conv_b), ("lng", conv_ln_g), ("lnb", conv_ln_b),
                    ("gng", ret_gn_g), ("gnb", ret_gn_b), ("pb", pool_b), ("ps", pool_scale)):
        a = np.asarray(a).reshape(L, -1, P)
        params[:, :, PAR[name]:PAR[name] + a.shape[1]] = a.transpose(2, 0, 1)

    arrays = {"x": np.ascontiguousarray(np.asarray(x).reshape(S, DM)),
              "weights": weights.reshape(L * SLOTS, P, SLOT), "params": params,
              "pool_w": np.ascontiguousarray(pool_w), "consts": constants()}
    nc = bacc.Bacc("TRN2", target_bir_lowering=False, num_devices=1)
    aps = [nc.dram_tensor(f"{n}_dram", a.shape, mybir.dt.from_np(a.dtype), kind="ExternalInput").ap()
           for n, a in arrays.items()]
    out = nc.dram_tensor("out_dram", (S, DM), F32, kind="ExternalOutput").ap()
    trunk_program(nc, *aps, out)
    got = run_bass_kernel_spmd(nc, [{f"{n}_dram": a for n, a in arrays.items()}], core_ids=[0])
    return got.results[0]["out_dram"].reshape(1, S, DM)
```

```python
import math
from contextlib import ExitStack

import concourse.bass as bass
from concourse import mybir

F32 = mybir.dt.float32
F16 = mybir.dt.float16
I32 = mybir.dt.int32
ALU = mybir.AluOpType
ACT = mybir.ActivationFunctionType
AX_X = mybir.AxisListType.X

P = 128
DM = 1024
S = 512
L = 2
KT = DM // P
HALF = S // 2
NT = S // P
G = DM // 4
HD = 64
NH = G // HD
CW = 31
FF = 2816
FT = FF // P
WINDOWS = (2, 4, 8, 16)

SLOT = 2048
RAW = SLOT // 2
NRAW = 2
RING = 8

W_SCALE = 1024.0
A_SCALE = 32.0
UNSCALE = 1.0 / (W_SCALE * A_SCALE)
RSQRT_MAGIC = float(0x5F3759DF)
RS = -8192.0

CONV_A, CONV_G, RQ, RK, RV, POOL, MQ, MK, MV, RG = range(10)
BLOCK_OF = {CONV_A: 0, CONV_G: 1, RQ: 2, RK: 3, RV: 4, POOL: 9, MQ: 6, MK: 7, MV: 8, RG: 5}
TOKEN_MAJOR = (RQ, RK, RV, MQ, MK, MV)
IN_GROUPS = (range(0, 7), range(7, 10))
N_IN, N_OUT, N_GU, N_DN = 10, 4, FT, FT // 2
OUT0 = N_IN
GU0 = OUT0 + N_OUT
DN0 = GU0 + N_GU
SLOTS = DN0 + N_DN
GU_HEAD = 6
DN_TAIL = 6
FIRST_BY_DVE = (0, 1)

UNITS = []
for group in IN_GROUPS:
    UNITS += [(c, (s,)) for s in range(2) for c in group]
UNITS += [(OUT0 + c, (s,)) for s in range(2) for c in range(N_OUT)]
UNITS += [(GU0 + c, (s,)) for s in range(2) for c in range(GU_HEAD)]
UNITS += [(GU0 + c, (0, 1)) for c in range(GU_HEAD, N_GU)]
UNITS += [(DN0 + c, (s,)) for c in range(N_DN - DN_TAIL) for s in range(2)]
UNITS += [(DN0 + c, (s,)) for s in range(2) for c in range(N_DN - DN_TAIL, N_DN)]
NU = len(UNITS)
UNIT_AT = {(slot, s): i for i, (slot, halves) in enumerate(UNITS) for s in halves}
HIDDEN = [(slot - GU0, halves) for slot, halves in UNITS if GU0 <= slot < DN0]
HIDDEN_AT = {(f, s): i for i, (f, halves) in enumerate(HIDDEN) for s in halves}
GU_EARLY = 2
assert len(UNIT_AT) == 2 * SLOTS and UNIT_AT[(GU0 + GU_HEAD, 0)] % 4 == 0

AT = {
    ("fpost_sum", 1): 12,
    ("fpost_bcast", 1): 24,
    ("pre_sum", 1): 51,
    ("pre_bcast", 1): 64,
    ("first_pre_sum", 1): 8,
    ("first_pre_bcast", 1): 24,
    ("ret_T", 0): 88,
    ("ret_S", 0): 96,
    ("ret_O", 0): 104,
    ("ret_T", 1): 112,
    ("ret_S", 1): 120,
    ("ret_O", 1): 128,
    ("ret_T", 2): 184,
    ("ret_S", 2): 192,
    ("ret_O", 2): 200,
    ("ret_T", 3): 208,
    ("ret_S", 3): 213,
    ("ret_O", 3): 219,
    ("ret_Y", 0): 160,
    ("ret_Y", 1): 312,
    ("conv_T", 0): 221,
    ("conv_Y", 0): 232,
    ("pool_Y", 0): 240,
    ("moba_T", 0): 250,
    ("moba_T", 1): 253,
    ("conv_T", 1): 320,
    ("conv_Y", 1): 333,
    ("pool_Y", 1): 339,
    ("moba_stage", 0): 258,
    ("moba_stage", 1): 266,
    ("moba_stage", 2): 274,
    ("moba_stage", 3): 282,
    ("moba_stage", 4): 290,
    ("moba_stage", 5): 298,
    ("moba_stage", 6): 310,
    ("moba_stage", 7): 318,
    ("moba_stage", 8): 326,
    ("moba_stage", 9): 334,
    ("moba_stage", 10): 342,
    ("moba_stage", 11): 350,
    ("moba_Y", 0): 306,
    ("moba_T", 2): 300,
    ("moba_T", 3): 302,
    ("moba_Y", 1): 358,
    ("post_sum", 0): 392,
    ("post_bcast", 0): 400,
    ("fpre_sum", 0): 421,
    ("fpre_bcast", 0): 432,
    ("post_sum", 1): 456,
    ("post_bcast", 1): 464,
    ("fpre_sum", 1): 496,
    ("fpre_bcast", 1): 507,
    ("fpost_sum", 0): 1160,
    ("fpost_bcast", 0): 1168,
    ("pre_sum", 0): 1192,
    ("pre_bcast", 0): 1203,
    ("x_out_T", 0): 1200,
    ("x_out_T", 1): 1208,
}

PAR = {}
PAR_COLS = 0
for name, cols in (("pre", KT), ("post", KT), ("fpre", KT), ("fpost", KT), ("cw", 2 * CW), ("cb", 2),
                   ("lng", 2), ("lnb", 2), ("gng", 2), ("gnb", 2), ("pb", 2), ("ps", 2)):
    PAR[name] = PAR_COLS
    PAR_COLS += cols

PARX = {}
PARX_COLS = 0
PARX_FROM = (("pre", "pre", KT, A_SCALE), ("fpre", "fpre", KT, A_SCALE), ("cw", "cw", 2 * CW, 0.5 * UNSCALE),
             ("lng", "lng", 2, 1.0 / RS), ("lng_half", "lng", 2, 0.5 / RS), ("lnb_half", "lnb", 2, 0.5),
             ("gng", "gng", 2, 1.0 / RS), ("pbs", "pb", 2, 1.0))
for name, _, cols, _ in PARX_FROM:
    PARX[name] = PARX_COLS
    PARX_COLS += cols

CST = {}
CST_COLS = 0
for name, cols in (("ident", P), ("ident_x", P), ("ident_y", P), ("tri", P), ("neg", P), ("ones", P), ("rqc", NT * NH * 32),
                   ("rqs", NT * NH * 32), ("rkc", NT * NH * 32), ("rks", NT * NH * 32),
                   ("mc", NT * NH * 8), ("ms", NT * NH * 8), ("adj", 2 * 16)):
    CST[name] = CST_COLS
    CST_COLS += cols


def trunk_program(nc, x, weights, params, pool_w, consts, out):
    with ExitStack() as ctx:
        def sb(name, shape, dt=F32):
            return ctx.enter_context(nc.sbuf_tensor(name, shape, dt))

        def sem(name):
            return ctx.enter_context(nc.semaphore(name))

        xT = sb("xT", [P, KT, S])
        hT = sb("hT", [P, 2, KT, S], F16)
        yT = sb("yT", [P, 2, KT, HALF])
        sq = sb("sq", [P, KT, HALF])
        raw = sb("raw", [P, NRAW, RAW])
        ring = sb("ring", [P, RING, 2, SLOT], F16)
        U = sb("U", [P, FT * S])
        E = sb("E", [P, 4672])
        cst = sb("cst", [P, CST_COLS])
        par = sb("par", [P, L, PAR_COLS])
        parx = sb("parx", [P, L, PARX_COLS])
        bd = sb("bd", [P, L, 2, P])
        small = sb("small", [P, 142])
        bank = [ctx.enter_context(nc.psum_tensor(f"bank{i}", [P, 512], F32)) for i in range(8)]

        def C(name):
            at = CST[name]
            nxt = min([v for v in CST.values() if v > at] + [CST_COLS])
            return cst[:, at:nxt]

        ident, ident_x, ident_y, tri, neg, ones = map(C, ("ident", "ident_x", "ident_y", "tri", "neg", "ones"))

        fT = U[:, :].bitcast(F16).rearrange("p (h f t) -> p h f t", h=2, f=FT)

        def carve(buf, sizes):
            at, got = 0, []
            for n in sizes:
                got.append(buf[:, at:at + n])
                at += n
            return got

        (ycat_w, ubuf_w, rv_w, mv_w, mqk_w, mkT_w, mqT_w, o_w, th_w, state_w) = carve(
            U, [KT * S, 2 * (16 + S), NT * G, NT * G, 2 * 2 * G, 2 * S, 2 * 2 * P, 2 * G, 2 * HALF, 2 * P])
        ycat = ycat_w.bitcast(F16).rearrange("p (h k t) -> p h k t", h=2, k=KT)
        ubuf = ubuf_w.rearrange("p (c t) -> p c t", c=2)
        rv = rv_w.rearrange("p (t c) -> p t c", t=NT)
        mv = mv_w.rearrange("p (t c) -> p t c", t=NT)
        mqk = mqk_w.rearrange("p (q t c) -> p q t c", q=2, t=2)
        mkT = mkT_w.rearrange("p (c t) -> p c t", c=2)
        mqT = mqT_w.rearrange("p (b c t) -> p b c t", b=2, c=2)
        osb = o_w.rearrange("p (t c) -> p t c", t=2)
        th = th_w.rearrange("p (c t) -> p c t", c=2)
        yA = yT[:, 0, :, :].rearrange("p k t -> p (k t)")
        yB = yT[:, 1, :, :].rearrange("p k t -> p (k t)")
        qk_w, rT_w, sm_w = carve(yA, [2 * 2 * G, 4 * P, 4 * P])
        qk = qk_w.rearrange("p (q t c) -> p q t c", q=2, t=2)
        rT = rT_w.rearrange("p (c t) -> p c t", c=4)
        sm = sm_w.rearrange("p (h t) -> p h t", h=4)
        pr_w, pT_w = carve(yB, [2 * S, 2 * S])
        pr = pr_w.rearrange("p (b t) -> p b t", b=2)
        pT = pT_w.rearrange("p (b j t) -> p b j t", b=2, j=NT)
        sqf = sq[:, :, :].rearrange("p k t -> p (k t)")
        t2_w, t4_w, t8, pooled_w = carve(sqf, [2 * (HALF + 14), 2 * (HALF + 12), HALF + 8, 2 * HALF])
        t2 = t2_w.rearrange("p (c t) -> p c t", c=2)
        t4 = t4_w.rearrange("p (c t) -> p c t", c=2)
        pooled = pooled_w.rearrange("p (c t) -> p c t", c=2)
        (rz_w, cn_w, yb_w, m1, m2, hb_w, ca_w, mo_w) = carve(
            E, [2 * HALF, 2 * G, 2 * HALF, 2 * HALF, 2 * HALF, 2 * (CW - 1 + S), 2 * HALF, 2 * G])
        mo = mo_w.rearrange("p (t c) -> p t c", t=2)
        rz = rz_w.rearrange("p (c t) -> p c t", c=2)
        cn = cn_w.rearrange("p (t c) -> p t c", t=2)
        ybuf = yb_w.rearrange("p (c t) -> p c t", c=2)
        hbuf = hb_w.rearrange("p (c t) -> p c t", c=2)
        cacc = ca_w.rearrange("p (c t) -> p c t", c=2)
        state = state_w.rearrange("p (c e) -> p c e", c=2)
        sil = E[:, 0:2 * S].rearrange("p (b t) -> p b t", b=2)
        fbuf = E[:, 2 * S:4 * S].rearrange("p (b t) -> p b t", b=2)
        xin = yT[:, :, :, :].rearrange("p s k t -> p (s k t)").rearrange("p (t c) -> p t c", t=NT)
        xout = hT[:, :, :, :].rearrange("p h k t -> p (h k t)").bitcast(F32).rearrange(
            "p (t c) -> p t c", t=NT)
        (rsx, rst, rsy, nmr, nms, sums, rinv, bst, mvr, cst_st, cmv) = carve(
            small, [10, 10, 10, 8, 8, 8, 8, 48, 16, 12, 4])

        def half(s):
            return slice(HALF * s, HALF * (s + 1))

        def span(halves):
            return slice(HALF * halves[0], HALF * (halves[-1] + 1))

        def tok(t):
            return slice(P * t, P * (t + 1))

        def b256(b):
            return bank[b][:, :].rearrange("p (c t) -> p c t", c=2)

        def b128(b):
            return bank[b][:, :].rearrange("p (c t) -> p c t", c=4)

        def par_col(l, name, c):
            return par[:, l, PAR[name] + c:PAR[name] + c + 1]

        def px(l, name, c):
            return parx[:, l, PARX[name] + c:PARX[name] + c + 1]

        def gain(kind, l, k):
            return px(l, kind, k)

        ident_in = sem("ident_in")
        consts_in = sem("consts_in")
        params_in = sem("params_in")
        maps_in = sem("maps_in")
        x_in = [sem(f"x_in{s}") for s in range(2)]
        hi_split = sem("hi_split")
        raw_scaled = sem("raw_scaled")
        lo_pool = sem("lo_pool")
        lo_dve = sem("lo_dve")
        unit_done = sem("unit_done")
        act_tick = sem("act_tick")
        dve_tick = sem("dve_tick")
        setup_done = sem("setup_done")
        xt_ps = sem("xt_ps")
        xt_sb = sem("xt_sb")
        y_sb = sem("y_sb")
        sq_done = sem("sq_done")
        ssq_done = sem("ssq_done")
        nsum_ps = sem("nsum_ps")
        rs_done = sem("rs_done")
        rstd_ps = sem("rstd_ps")
        dn_bank = sem("dn_bank")
        xr_done = sem("xr_done")
        x_upd = sem("x_upd")
        h_hi = sem("h_hi")
        h_lo = sem("h_lo")
        glu_th = sem("glu_th")
        hb_sb = sem("hb_sb")
        rot_done = sem("rot_done")
        rv_sb = sem("rv_sb")
        retT_ps = sem("retT_ps")
        retT_sb = sem("retT_sb")
        retS_ps = sem("retS_ps")
        retS_sb = sem("retS_sb")
        retO_ps = sem("retO_ps")
        retO_sb = sem("retO_sb")
        state_sb = sem("state_sb")
        ret_rs = sem("ret_rs")
        retN_sb = sem("retN_sb")
        retY_ps = sem("retY_ps")
        ret_z = sem("ret_z")
        rg_th = sem("rg_th")
        ret_g = sem("ret_g")
        ret_y32 = sem("ret_y32")
        ret_hi = sem("ret_hi")
        ret_y = sem("ret_y")
        conv_sb = sem("conv_sb")
        convT_ps = sem("convT_ps")
        conv_rs = sem("conv_rs")
        convN_sb = sem("convN_sb")
        convY_ps = sem("convY_ps")
        conv_th = sem("conv_th")
        conv_z = sem("conv_z")
        conv_y32 = sem("conv_y32")
        conv_hi = sem("conv_hi")
        conv_y = sem("conv_y")
        pool_u = sem("pool_u")
        pool_sb = sem("pool_sb")
        poolY_ps = sem("poolY_ps")
        pool_y32 = sem("pool_y32")
        pool_hi = sem("pool_hi")
        pool_y = sem("pool_y")
        mq_sb = sem("mq_sb")
        mk_sb = sem("mk_sb")
        mrot = sem("mrot")
        mv_sb = sem("mv_sb")
        mT_ps = sem("mT_ps")
        mT_sb = sem("mT_sb")
        mS_ps = sem("mS_ps")
        mM = sem("mM")
        mP = sem("mP")
        mPT_ps = sem("mPT_ps")
        mPT_sb = sem("mPT_sb")
        mPV = sem("mPV")
        mO_sb = sem("mO_sb")
        mY_ps = sem("mY_ps")
        moba_hi = sem("moba_hi")
        moba_y = sem("moba_y")
        sil_done = sem("sil_done")
        f_sb = sem("f_sb")
        f_hi = sem("f_hi")
        f_lo = sem("f_lo")
        xo_ps = sem("xo_ps")
        xo_sb = sem("xo_sb")
        stored = sem("stored")
        raw_in = [sem(f"raw_in{i}") for i in range(NRAW)]

        def dve_splits(n):
            return n in FIRST_BY_DVE or (n >= RING and GU0 <= (n - RING) % SLOTS < SLOTS - DN_TAIL)

        def split_count(n):
            by_dve = dve_splits(n // 2)
            count = sum(dve_splits(i // 2) == by_dve for i in range(n + 1))
            return (lo_dve if by_dve else lo_pool), count

        def unit_no(l, slot, s):
            return l * NU + UNIT_AT[(slot, s)] + 1

        def hs(l, s):
            return 2 * l + s + 1

        def ts(l, t):
            return NT * l + t + 1

        def ths(l, t, h):
            return NH * (NT * l + t) + h + 1

        def fno(l, f, s):
            return len(HIDDEN) * l + HIDDEN_AT[(f, s)] + 1

        def unit_bank(slot, s):
            return UNIT_AT[(slot, s)] % 4

        def gu_tiles(f, halves):
            if len(halves) == 1:
                b = unit_bank(GU0 + f, halves[0])
                return b256(b)[:, 0, :], b256(b)[:, 1, :]
            b = 2 * (f % 2)
            return bank[b][:, :], bank[b + 1][:, :]

        NORMS = [("pre", 0, 0), ("pre", 0, 1)]
        for l in range(L):
            for s in range(2):
                NORMS += [("post", l, s), ("fpre", l, s)]
            for s in range(2):
                NORMS += [("fpost", l, s)] + ([("pre", l + 1, s)] if l + 1 < L else [])
        PRES = [n for n in NORMS if n[0] in ("pre", "fpre")]
        POSTS = [n for n in NORMS if n[0] in ("post", "fpost")]

        def norm_no(*n):
            return NORMS.index(n)

        def pre_no(*n):
            return PRES.index(n)

        def post_no(*n):
            return POSTS.index(n)

        def norm_bank(kind, l, s):
            return 3 if s == 0 and (kind == "fpost" or (kind == "pre" and l)) else 7

        def raw_part(i):
            return slice(RAW * i, RAW * (i + 1))

        block = ctx.enter_context(nc.Block())

        @block.sync
        def _(sp):
            sp.dma_start(cst[:, 0:P], consts[:, 0:P]).then_inc(ident_in, 16)
            for t in range(2):
                sp.dma_start(xin[:, t, :], x[tok(t), :]).then_inc(x_in[0], 16)
            for n in range(2 * L * SLOTS):
                if n >= NRAW:
                    sp.wait_ge(*split_count(n - NRAW))
                sp.dma_start(raw[:, n % NRAW, :], weights[n // 2, :, raw_part(n % 2)]).then_inc(
                    raw_in[n % NRAW], 16)
                if n == 1:
                    sp.dma_start(par[:, :, :], params).then_inc(params_in, 16)
                    sp.dma_start(cst[:, P:], consts[:, P:]).then_inc(consts_in, 16)
                    for t in range(2, NT):
                        sp.dma_start(xin[:, t, :], x[tok(t), :]).then_inc(x_in[1], 16)
                    sp.wait_ge(dve_tick, 1)
                    for l in range(L):
                        for g in range(4):
                            r = slice(HD * (g % 2), HD * (g % 2) + HD)
                            sp.dma_start(bd[r, l, g // 2, r], pool_w[l, g, :, :]).then_inc(maps_in, 16)
            for t in range(NT):
                sp.wait_ge(xo_sb, 2 * (t + 1))
                sp.dma_start(out[tok(t), :], xout[:, t, :]).then_inc(stored, 16)
            sp.wait_ge(stored, 16 * NT)

        @block.gpsimd
        def _(pool):
            for n in range(2 * L * SLOTS):
                slot, part = n // 2, n % 2
                hi = ring[:, slot % RING, 0, raw_part(part)]
                lo = ring[:, slot % RING, 1, raw_part(part)]
                pool.wait_ge(raw_in[n % NRAW], 16 * (n // NRAW + 1))
                if slot >= RING:
                    old = slot - RING
                    pool.wait_ge(unit_done, unit_no(old // SLOTS, old % SLOTS, 1))
                src = raw[:, n % NRAW, :]
                nc.gpsimd.tensor_scalar(hi, src, W_SCALE, 1.0, ALU.mult, ALU.mult).then_inc(hi_split, 1)
                if not dve_splits(slot):
                    pool.wait_ge(hi_split, n + 1)
                    nc.gpsimd.tensor_scalar(src, src, W_SCALE, 1.0, ALU.mult, ALU.mult).then_inc(raw_scaled, 1)
                    pool.wait_ge(raw_scaled, split_count(n)[1])
                    nc.gpsimd.tensor_tensor(lo, src, hi, ALU.subtract).then_inc(lo_pool, 1)

        @block.tensor
        def _(pe):
            mm = nc.tensor.matmul
            freed_by = [None] * 8

            def take(b, sem, value):
                if freed_by[b] is not None:
                    pe.wait_ge(*freed_by[b])
                freed_by[b] = (sem, value)

            def split3(dst, w, a, first, last, weights_still, **kw):
                for i, (pw, pa) in enumerate(((0, 0), (0, 1), (1, 0))):
                    st, mv_ = (w[pw], a[pa]) if weights_still else (a[pa], w[pw])
                    ins = mm(dst, st, mv_, start=first and i == 0, stop=last and i == 2, **kw)
                return ins

            def transpose(dst, src):
                return nc.tensor.transpose(dst, src, ident)

            def last_read(l, slot, s):
                if slot >= GU0:
                    return f_sb, fno(l, slot - GU0, s)
                if slot >= OUT0:
                    return y_sb, 4 * post_no("post", l, s) + slot - OUT0 + 1
                return {CONV_A: (hb_sb, hs(l, s)), CONV_G: (glu_th, hs(l, s)), RQ: (rot_done, 2 * hs(l, s) - 1),
                        RK: (rot_done, 2 * hs(l, s)), RV: (rv_sb, hs(l, s)), POOL: (pool_u, hs(l, s)),
                        MQ: (mq_sb, hs(l, s)), MK: (mk_sb, hs(l, s)), MV: (mv_sb, hs(l, s)),
                        RG: (ret_y32, hs(l, s))}[slot]

            def unit(l, slot, halves, between):
                s = halves[0]
                if s == 0:
                    pe.wait_ge(*split_count(2 * (l * SLOTS + slot) + 1))
                w = [ring[:, (l * SLOTS + slot) % RING, i, :].rearrange(
                    "p (k n) -> p k n", k=KT if slot < DN0 else 2) for i in range(2)]
                pre = {0: "pre", GU0: "fpre"}.get(slot)
                if slot < OUT0:
                    b = unit_bank(slot, s)
                    take(b, *last_read(l, slot, s))
                    for c in range(2):
                        for k in range(KT):
                            between(KT * c + k)
                            if pre and c == 0:
                                pe.wait_ge(h_lo, KT * pre_no(pre, l, s) + k + 1)
                            if slot in TOKEN_MAJOR:
                                cols, rows = slice(0, G), tok(2 * s + c)
                            else:
                                cols, rows = slice(P * c, P * (c + 1)), half(s)
                            last = split3(b256(b)[:, c, :], [w[0][:, k, cols], w[1][:, k, cols]],
                                          [hT[:, 0, k, rows], hT[:, 1, k, rows]],
                                          k == 0, k == KT - 1, slot not in TOKEN_MAJOR)
                elif slot < GU0:
                    b = unit_bank(slot, s)
                    take(b, *last_read(l, slot, s))
                    order = [6, 7, 0, 1, 2, 3, 4, 5]
                    for c in range(2):
                        for i, k in enumerate(order):
                            between(KT * c + i)
                            if slot == OUT0 and c == 0 and i % 2 == 0:
                                pe.wait_ge((pool_y, conv_y, ret_y, moba_y)[i // 2], hs(l, s))
                            cols = slice(P * c, P * (c + 1))
                            last = split3(b256(b)[:, c, :], [w[0][:, k, cols], w[1][:, k, cols]],
                                          [ycat[:, 0, k, half(s)], ycat[:, 1, k, half(s)]],
                                          i == 0, i == KT - 1, True)
                elif slot < DN0:
                    f = slot - GU0
                    dst = gu_tiles(f, halves)
                    for b in ([unit_bank(slot, s)] if len(halves) == 1 else [2 * (f % 2), 2 * (f % 2) + 1]):
                        take(b, *last_read(l, slot, s))
                    for c in range(2):
                        for k in range(KT):
                            between(KT * c + k)
                            if pre and c == 0:
                                pe.wait_ge(h_lo, KT * pre_no(pre, l, s) + k + 1)
                            cols = slice(P * c, P * (c + 1))
                            last = split3(dst[c], [w[0][:, k, cols], w[1][:, k, cols]],
                                          [hT[:, 0, k, span(halves)], hT[:, 1, k, span(halves)]],
                                          k == 0, k == KT - 1, True)
                else:
                    final = slot == SLOTS - 1
                    parts = [(m, c) for m in range(KT) for c in range(2)] if final else \
                        [(m, c) for c in range(2) for m in range(KT)]
                    for i, (m, c) in enumerate(parts):
                        between(i)
                        f, b = 2 * (slot - DN0) + c, 4 * s + m // 2
                        if i % KT == 0 or (final and i == 1):
                            pe.wait_ge(f_lo, fno(l, f, s))
                        if f == 0 and m % 2 == 0:
                            take(b, y_sb, 4 * post_no("fpost", l, s) + m // 2 + 1)
                        ms = slice(P * m, P * (m + 1))
                        last = split3(b256(b)[:, m % 2, :], [w[0][:, c, ms], w[1][:, c, ms]],
                                      [fT[:, 0, f, half(s)], fT[:, 1, f, half(s)]],
                                      f == 0 and m % 2 == 0, f == FT - 1 and m % 2 == 1, True,
                                      skip_group_check=True)
                        if final and i in (3, 7, 11):
                            last.then_inc(dn_bank, 1)
                last.then_inc(unit_done, 1)

            def norm_sum(kind, l, s):
                n, b = norm_no(kind, l, s), norm_bank(kind, l, s)
                take(b, xr_done, 4 * (n + 1))
                pe.wait_ge(ssq_done, n + 1)
                for t in range(2):
                    for i in range(2):
                        last = mm(bank[b][:, t:t + 1], sq[:, i, tok(t)], ones[:, 0:1], start=i == 0, stop=i == 1)
                last.then_inc(nsum_ps, 1)

            def norm_bcast(kind, l, s):
                n, b = norm_no(kind, l, s), norm_bank(kind, l, s)
                pe.wait_ge(rs_done, n + 1)
                for t in range(2):
                    last = mm(bank[b][:, HALF + P * t:HALF + P * (t + 1)],
                              rsy[:, 8 + t:9 + t].to_broadcast([P, P]),
                              ident_y if kind in ("post", "fpost") else ident_x, start=True, stop=True)
                last.then_inc(rstd_ps, 1)

            def rows_of(h):
                return slice(HD * (h % 2), HD * (h % 2) + HD)

            def ret_T(l, t):
                pe.wait_ge(rot_done, 2 * hs(l, t // 2))
                take(4, retT_sb, ts(l, t))
                for q in range(2):
                    for c in range(2):
                        last = transpose(b128(4)[:, 2 * q + c, :], qk[:, q, t % 2, P * c:P * (c + 1)])
                last.then_inc(retT_ps, 1)

            def ret_S(l, t):
                pe.wait_ge(retT_sb, ts(l, t))
                take(6, retS_sb, 2 * ts(l, t) - 1)
                take(4, retS_sb, 2 * ts(l, t))
                for h in range(NH):
                    r = rows_of(h)
                    last = mm(b128((6, 4)[h % 2])[:, h // 2, :], rT[r, 2 + h // 2, :], rT[r, h // 2, :],
                              start=True, stop=True)
                last.then_inc(retS_ps, 1)

            def ret_O(l, t):
                pe.wait_ge(retS_sb, 2 * ts(l, t))
                pe.wait_ge(rv_sb, hs(l, t // 2))
                if t:
                    pe.wait_ge(state_sb, (NT - 1) * l + t)
                take(5, retO_sb, ts(l, t))
                o = bank[5][:, 0:NH * HD].rearrange("p (h e) -> p h e", h=NH)
                for c in range(2):
                    for h in (2 * c, 2 * c + 1):
                        last = mm(o[:, h, :], sm[:, h, :], rv[:, t, HD * h:HD * (h + 1)], start=h == 0,
                                  stop=t == 0 and h == NH - 1, skip_group_check=True)
                    if t:
                        last = mm(bank[5][:, P * c:P * (c + 1)], rT[:, c, :], state[:, c, :], start=False,
                                  stop=c == 1, skip_group_check=True)
                if t < NT - 1:
                    take(6, state_sb, (NT - 1) * l + t + 1)
                    for c in range(2):
                        pc = slice(P * c, P * (c + 1))
                        last = mm(b128(6)[:, c, :], qk[:, 1, t % 2, pc], rv[:, t, pc], start=True, stop=True)
                last.then_inc(retO_ps, 1)

            def to_channels(b, src, done):
                for c in range(2):
                    for t in range(2):
                        last = transpose(b256(b)[:, c, tok(t)], src[:, t, P * c:P * (c + 1)])
                last.then_inc(done, 1)

            def ret_Y(l, s):
                pe.wait_ge(retN_sb, 8 * hs(l, s))
                take(5, ret_z, 2 * hs(l, s))
                to_channels(5, osb, retY_ps)

            def conv_T(l, s):
                pe.wait_ge(conv_sb, hs(l, s))
                take(5, convN_sb, 2 * hs(l, s))
                for t in range(2):
                    for c in range(2):
                        last = transpose(b256(5)[:, t, P * c:P * (c + 1)], cacc[:, c, tok(t)])
                last.then_inc(convT_ps, 1)

            def conv_Y(l, s):
                pe.wait_ge(convN_sb, 2 * hs(l, s))
                take(5, conv_z, 2 * hs(l, s))
                to_channels(5, cn, convY_ps)

            def pool_Y(l, s):
                pe.wait_ge(pool_sb, hs(l, s))
                pe.wait_ge(maps_in, 16 * 4 * L)
                take(6, pool_y32, 2 * hs(l, s))
                for c in range(2):
                    last = mm(b256(6)[:, c, :], bd[:, l, c, :], pooled[:, c, :], start=True, stop=True)
                last.then_inc(poolY_ps, 1)

            def moba_T(l, t):
                pe.wait_ge(mrot, hs(l, t // 2))
                take(4, mT_sb, ts(l, t))
                for q in range(2):
                    for c in range(2):
                        last = transpose(b128(4)[:, 2 * q + c, :], mqk[:, q, t % 2, P * c:P * (c + 1)])
                last.then_inc(mT_ps, 1)

            def moba_S(l, t, h):
                if h == 0:
                    pe.wait_ge(mT_sb, ts(l, t))
                b, r = (4, 6)[h % 2], rows_of(h)
                take(b, mP, ths(l, t, h))
                q = mqT[r, t % 2, h // 2, :]
                mm(bank[b][:, tok(t)], ident, neg, start=True, stop=False)
                last = mm(bank[b][:, tok(t)], q, mkT[r, h // 2, tok(t)], start=False, stop=True)
                if t:
                    last = mm(bank[b][:, 0:P * t], q, mkT[r, h // 2, 0:P * t], start=True, stop=True)
                last.then_inc(mS_ps, 1)

            def moba_PT(l, t, h):
                pe.wait_ge(mP, ths(l, t, h))
                take(5, mPT_sb, ths(l, t, h))
                for j in range(t + 1):
                    last = transpose(b128(5)[:, j, :], pr[:, h % 2, tok(j)])
                last.then_inc(mPT_ps, 1)

            def moba_O(l, t, h):
                if h == 0:
                    take(7, mO_sb, ts(l, t))
                    pe.wait_ge(mv_sb, hs(l, t // 2))
                pe.wait_ge(mPT_sb, ths(l, t, h))
                for j in range(t + 1):
                    last = mm(bank[7][:, HD * h:HD * (h + 1)], pT[:, h % 2, j, :],
                              mv[:, j, HD * h:HD * (h + 1)], start=j == 0, stop=j == t)
                last.then_inc(mPV, 1)

            def moba_Y(l, s):
                pe.wait_ge(mO_sb, ts(l, 2 * s + 1))
                take(5, moba_y, hs(l, s))
                to_channels(5, mo, mY_ps)

            def moba_stage(l, s, k):
                def th_of(g, i):
                    return 2 * s + g // 2, 2 * (g % 2) + i
                if 1 <= k <= 4:
                    moba_PT(l, *th_of(k - 1, 0))
                if k <= 3:
                    moba_S(l, *th_of(k, 0))
                    moba_S(l, *th_of(k, 1))
                if k >= 2:
                    moba_O(l, *th_of(k - 2, 0))
                    moba_O(l, *th_of(k - 2, 1))
                if 1 <= k <= 4:
                    moba_PT(l, *th_of(k - 1, 1))

            def x_in_T(s):
                pe.wait_ge(x_in[s], 32)
                for c in range(4):
                    take(c, xt_sb, 4 * s + c + 1)
                    for k in range(2):
                        for t in range(2):
                            last = transpose(b256(c)[:, k, tok(t)], xin[:, 2 * s + t, P * (2 * c + k):P * (2 * c + k + 1)])
                    last.then_inc(xt_ps, 1)

            def x_out_T(t):
                pe.wait_ge(x_upd, KT * (post_no("fpost", L - 1, t // 2) + 1))
                for i in range(2):
                    b = i + 2 * (t % 2)
                    take(b, xo_sb, 2 * t + i + 1)
                    for k in range(4):
                        last = transpose(b128(b)[:, k, :], xT[:, 4 * i + k, tok(t)])
                    last.then_inc(xo_ps, 1)

            def small_products(l, at):
                for s in range(2):
                    first, last_l = ("first_" if l == 0 else ""), l == L - 1
                    if l and s and at == AT["fpost_sum", s]: norm_sum("fpost", l - 1, s)
                    if l and s and at == AT["fpost_bcast", s]: norm_bcast("fpost", l - 1, s)
                    if s and at == AT[first + "pre_sum", s]: norm_sum("pre", l, s)
                    if s and at == AT[first + "pre_bcast", s]: norm_bcast("pre", l, s)
                    for i in range(2):
                        t = 2 * s + i
                        if at == AT["ret_T", t]: ret_T(l, t)
                        if at == AT["ret_S", t]: ret_S(l, t)
                        if at == AT["ret_O", t]: ret_O(l, t)
                    if at == AT["ret_Y", s]: ret_Y(l, s)
                    if at == AT["conv_T", s]: conv_T(l, s)
                    if at == AT["conv_Y", s]: conv_Y(l, s)
                    if at == AT["pool_Y", s]: pool_Y(l, s)
                    for i in range(2):
                        if at == AT["moba_T", 2 * s + i]: moba_T(l, 2 * s + i)
                    for k in range(6):
                        if at == AT["moba_stage", 6 * s + k]: moba_stage(l, s, k)
                    if at == AT["moba_Y", s]: moba_Y(l, s)
                    for kind in ("post", "fpre"):
                        if at == AT[kind + "_sum", s]: norm_sum(kind, l, s)
                        if at == AT[kind + "_bcast", s]: norm_bcast(kind, l, s)
                if at == AT["fpost_sum", 0]: norm_sum("fpost", l, 0)
                if at == AT["fpost_bcast", 0]: norm_bcast("fpost", l, 0)
                if at == AT["pre_sum", 0] and l < L - 1: norm_sum("pre", l + 1, 0)
                if at == AT["pre_bcast", 0] and l < L - 1: norm_bcast("pre", l + 1, 0)
                for t in range(2):
                    if at == AT["x_out_T", t] and l == L - 1: x_out_T(t)

            pe.wait_ge(ident_in, 16)
            x_in_T(0)
            pe.wait_ge(consts_in, 16)
            norm_sum("pre", 0, 0)
            x_in_T(1)
            norm_bcast("pre", 0, 0)
            for l in range(L):
                for i, (slot, halves) in enumerate(UNITS):
                    unit(l, slot, halves, lambda part: small_products(l, 16 * i + part))
            norm_sum("fpost", L - 1, 1)
            norm_bcast("fpost", L - 1, 1)
            x_out_T(2)
            x_out_T(3)

        @block.scalar
        def _(act):
            A = nc.scalar.activation

            def copy(dst, src, scale=1.0):
                return A(dst, src, ACT.Copy, scale=scale)

            def squares_of_x(kind, l, s):
                n = norm_no(kind, l, s)
                if n:
                    act.wait_ge(nsum_ps, n)
                upd = post_no("post" if kind == "fpre" else "fpost", l if kind == "fpre" else l - 1, s) \
                    if kind == "fpre" or l else None
                for c in range(4):
                    if upd is None:
                        act.wait_ge(xt_sb, 4 * s + c + 1)
                    else:
                        act.wait_ge(x_upd, KT * upd + 2 * c + 2)
                    A(sq[:, 2 * c:2 * c + 2, :], xT[:, 2 * c:2 * c + 2, half(s)],
                      ACT.Square).then_inc(sq_done, 1)

            def squares_of_y(kind, l, s):
                n = norm_no(kind, l, s)
                act.wait_ge(nsum_ps, n)
                if kind == "post":
                    act.wait_ge(poolY_ps, hs(l, 1))
                    act.wait_ge((retO_ps, mPV)[s], (ts(l, 3), ths(l, 3, 3))[s])
                else:
                    act.wait_ge(h_lo, KT * (pre_no("fpre", l, s) + 1))
                for c in range(4):
                    if kind == "post":
                        act.wait_ge(unit_done, unit_no(l, OUT0 + c, s))
                        b = unit_bank(OUT0 + c, s)
                    else:
                        b = 4 * s + c
                        if c < 3:
                            act.wait_ge(dn_bank, 3 * (2 * l + s) + c + 1)
                        else:
                            act.wait_ge(unit_done, unit_no(l, SLOTS - 1, s))
                    A(sq[:, 2 * c:2 * c + 2, :], b256(b), ACT.Square, scale=UNSCALE).then_inc(sq_done, 1)
                    copy(yT[:, s, 2 * c:2 * c + 2, :], b256(b)).then_inc(y_sb, 1)

            def h_split_hi(kind, l, s):
                n = norm_no(kind, l, s)
                if kind == "fpre":
                    act.wait_ge(unit_done, unit_no(l, RG, s))
                elif l:
                    act.wait_ge(unit_done, unit_no(l - 1, GU0 + N_GU - 1, s))
                for k in range(KT):
                    act.wait_ge(xr_done, 4 * n + k // 2 + 1)
                    copy(hT[:, 0, k, half(s)], yT[:, s, k, :], gain(kind, l, k)).then_inc(h_hi, 1)

            def hi_of(src, ready, kt, l, s, scale, done):
                act.wait_ge(ready, hs(l, s) * (2 if ready is pool_y32 else 1))
                copy(ycat[:, 0, kt:kt + 2, half(s)], src, scale).then_inc(done, 1)

            def glu_tanh(l, s):
                act.wait_ge(unit_done, unit_no(l, CONV_G, s))
                if l or s:
                    act.wait_ge(hb_sb, hs(l, s) - 1)
                if l and s == 0:
                    act.wait_ge(ret_g, 2 * l)
                A(th, b256(unit_bank(CONV_G, s)), ACT.Tanh, scale=0.5 * UNSCALE).then_inc(glu_th, 1)

            def rg_tanh(l, s):
                act.wait_ge(unit_done, unit_no(l, RG, s))
                act.wait_ge(hb_sb, hs(l, 1))
                act.wait_ge(conv_y32, hs(l, s))
                if s:
                    act.wait_ge(ret_g, hs(l, 0))
                A(th, b256(unit_bank(RG, s)), ACT.Tanh, scale=0.5 * UNSCALE).then_inc(rg_th, 1)

            def affine(dst, src, scale, bias):
                return A(dst, src, ACT.Identity, scale=scale, bias=bias)

            def conv_scale(l, s):
                act.wait_ge(conv_rs, hs(l, s))
                if hs(l, s) > 1:
                    act.wait_ge(convY_ps, hs(l, s) - 1)
                for t in range(2):
                    affine(cn[:, t, :], b256(5)[:, t, :], rsy[:, t:t + 1], nmr[:, t:t + 1]).then_inc(convN_sb, 1)

            def ret_scale(l, s):
                act.wait_ge(ret_rs, hs(l, s))
                for i in range(8):
                    o = osb[:, i // NH, HD * (i % NH):HD * (i % NH + 1)]
                    affine(o, o, rsy[:, i:i + 1], nmr[:, i:i + 1]).then_inc(retN_sb, 1)

            def ret_affine(l, s):
                act.wait_ge(retY_ps, hs(l, s))
                if hs(l, s) > 1:
                    act.wait_ge(ret_y32, hs(l, s) - 1)
                for c in range(2):
                    affine(rz[:, c, :], b256(5)[:, c, :], px(l, "gng", c), par_col(l, "gnb", c)).then_inc(ret_z, 1)

            def pool_affine(l, s):
                act.wait_ge(poolY_ps, hs(l, s))
                act.wait_ge(conv_y, hs(l, s))
                for c in range(2):
                    affine(ybuf[:, c, :], b256(6)[:, c, :], par_col(l, "ps", c),
                           px(l, "pbs", c)).then_inc(pool_y32, 1)

            def conv_affine(l, s):
                act.wait_ge(convY_ps, hs(l, s))
                act.wait_ge(hb_sb, hs(l, 1))
                if s:
                    act.wait_ge(ret_g, hs(l, 0))
                if l or s:
                    act.wait_ge(ret_y, hs(l, s) - 1)
                for c in range(2):
                    A(th[:, c, :], b256(5)[:, c, :], ACT.Tanh, scale=px(l, "lng_half", c),
                      bias=px(l, "lnb_half", c)).then_inc(conv_th, 1)
                for c in range(2):
                    affine(ybuf[:, c, :], b256(5)[:, c, :], px(l, "lng", c),
                           par_col(l, "lnb", c)).then_inc(conv_z, 1)

            def from_unit(l, slot, s, dst, done):
                act.wait_ge(unit_done, unit_no(l, slot, s))
                copy(dst, b256(unit_bank(slot, s)), UNSCALE).then_inc(done, 1)

            def ret_T_copy(l, t):
                act.wait_ge(retT_ps, ts(l, t))
                if l or t:
                    act.wait_ge(retO_ps, ts(l, t) - 1)
                copy(rT, b128(4)).then_inc(retT_sb, 1)

            def ret_O_copy(l, t):
                act.wait_ge(retO_ps, ts(l, t))
                if hs(l, t // 2) > 1:
                    act.wait_ge(retY_ps, hs(l, t // 2) - 1)
                copy(osb[:, t % 2, :], bank[5][:, 0:G]).then_inc(retO_sb, 1)

            def moba_in(l, s, q):
                slot, done = ((MQ, mq_sb), (MK, mk_sb))[q]
                act.wait_ge(unit_done, unit_no(l, slot, s))
                if l or s:
                    act.wait_ge(mT_ps, ts(l, 2 * s) - 1)
                copy(mqk[:, q, :, :], b256(unit_bank(slot, s)),
                     UNSCALE * (HD ** -0.5 if q == 0 else 1.0)).then_inc(done, 1)

            def m_T_copy(l, t):
                act.wait_ge(mT_ps, ts(l, t))
                if ts(l, t) > 2:
                    act.wait_ge(mS_ps, ths(l, t, 3) - 2 * NH)
                if l:
                    act.wait_ge(mS_ps, ths(l - 1, NT - 1, NH - 1))
                copy(mqT[:, t % 2, :, :], b128(4)[:, 0:2, :]).then_inc(act_tick, 1)
                copy(mkT[:, :, tok(t)], b128(4)[:, 2:4, :]).then_inc(mT_sb, 1)

            def m_exp(l, t, h):
                i = ths(l, t, h)
                act.wait_ge(mM, i)
                if i > 2:
                    act.wait_ge(mPT_ps, i - 2)
                if ts(l, t) > 2:
                    act.wait_ge(mO_sb, ts(l, t) - 2)
                c = (i - 1) % 8
                w = P * (t + 1)
                A(pr[:, h % 2, 0:w], bank[(4, 6)[h % 2]][:, 0:w], ACT.Exp, bias=nms[:, c:c + 1],
                  accum_out=sums[:, c:c + 1]).then_inc(mP, 1)

            def m_PT_copy(l, t, h):
                i = ths(l, t, h)
                act.wait_ge(mPT_ps, i)
                if i > 2:
                    act.wait_ge(mPV, i - 2)
                copy(pT[:, h % 2, 0:t + 1, :], b128(5)[:, 0:t + 1, :]).then_inc(mPT_sb, 1)

            def m_stage(l, s, k):
                def th_of(g, i):
                    return 2 * s + g // 2, 2 * (g % 2) + i
                if 1 <= k <= 4:
                    m_PT_copy(l, *th_of(k - 1, 0))
                if k <= 3:
                    m_exp(l, *th_of(k, 0))
                    m_exp(l, *th_of(k, 1))
                if 1 <= k <= 4:
                    m_PT_copy(l, *th_of(k - 1, 1))

            def silu(l, f, halves):
                n = fno(l, f, halves[0])
                act.wait_ge(unit_done, unit_no(l, GU0 + f, halves[0]))
                if n > 2:
                    act.wait_ge(f_sb, n - 2)
                A(sil[:, n % 2, 0:HALF * len(halves)], gu_tiles(f, halves)[0], ACT.Silu,
                  scale=UNSCALE).then_inc(sil_done, 1)

            def hidden_hi(l, f, halves):
                n = fno(l, f, halves[0])
                act.wait_ge(f_sb, n)
                copy(fT[:, 0, f, span(halves)], fbuf[:, n % 2, 0:HALF * len(halves)]).then_inc(f_hi, 1)

            def hidden_steps(l, i0, i1):
                for i in range(i0, i1):
                    silu(l, *HIDDEN[i])
                    if i:
                        hidden_hi(l, *HIDDEN[i - 1])

            def x_copy(s):
                for c in range(4):
                    act.wait_ge(xt_ps, 4 * s + c + 1)
                    copy(xT[:, 2 * c:2 * c + 2, half(s)], b256(c)).then_inc(xt_sb, 1)

            x_copy(0)
            squares_of_x("pre", 0, 0)
            x_copy(1)
            act.wait_ge(setup_done, 1 + L)
            h_split_hi("pre", 0, 0)
            for l in range(L):
                if l:
                    squares_of_y("fpost", l - 1, 1)
                    glu_tanh(l, 0)
                    squares_of_x("pre", l, 1)
                else:
                    squares_of_x("pre", l, 1)
                    glu_tanh(l, 0)
                h_split_hi("pre", l, 1)
                from_unit(l, RV, 0, rv[:, 0:2, :], rv_sb)
                from_unit(l, POOL, 0, ubuf[:, :, 16:16 + HALF], pool_u)
                ret_T_copy(l, 0)
                ret_O_copy(l, 0)
                moba_in(l, 0, 0)
                ret_T_copy(l, 1)
                ret_O_copy(l, 1)
                glu_tanh(l, 1)
                ret_scale(l, 0)
                ret_affine(l, 0)
                ret_T_copy(l, 2)
                from_unit(l, RV, 1, rv[:, 2:4, :], rv_sb)
                ret_O_copy(l, 2)
                from_unit(l, POOL, 1, ubuf[:, :, 16 + HALF:16 + S], pool_u)
                ret_T_copy(l, 3)
                ret_O_copy(l, 3)
                conv_scale(l, 0)
                conv_affine(l, 0)
                hi_of(ybuf, conv_y32, 0, l, 0, 0.5 * A_SCALE, conv_hi)
                moba_in(l, 0, 1)
                pool_affine(l, 0)
                hi_of(ybuf, pool_y32, 6, l, 0, A_SCALE, pool_hi)
                m_T_copy(l, 0)
                m_T_copy(l, 1)
                moba_in(l, 1, 0)
                from_unit(l, MV, 0, mv[:, 0:2, :], mv_sb)
                m_stage(l, 0, 0)
                m_stage(l, 0, 1)
                rg_tanh(l, 0)
                hi_of(ybuf, ret_y32, 2, l, 0, 0.5 * A_SCALE * UNSCALE, ret_hi)
                m_stage(l, 0, 2)
                m_stage(l, 0, 3)
                moba_in(l, 1, 1)
                m_stage(l, 0, 4)
                m_T_copy(l, 2)
                from_unit(l, MV, 1, mv[:, 2:4, :], mv_sb)
                m_T_copy(l, 3)
                hi_of(b256(5), mY_ps, 4, l, 0, A_SCALE, moba_hi)
                ret_scale(l, 1)
                m_stage(l, 1, 0)
                ret_affine(l, 1)
                m_stage(l, 1, 1)
                conv_scale(l, 1)
                m_stage(l, 1, 2)
                conv_affine(l, 1)
                hi_of(ybuf, conv_y32, 0, l, 1, 0.5 * A_SCALE, conv_hi)
                rg_tanh(l, 1)
                m_stage(l, 1, 3)
                pool_affine(l, 1)
                hi_of(ybuf, pool_y32, 6, l, 1, A_SCALE, pool_hi)
                m_stage(l, 1, 4)
                hi_of(ybuf, ret_y32, 2, l, 1, 0.5 * A_SCALE * UNSCALE, ret_hi)
                hi_of(b256(5), mY_ps, 4, l, 1, A_SCALE, moba_hi)
                for s in range(2):
                    squares_of_y("post", l, s)
                    squares_of_x("fpre", l, s)
                    if s:
                        hidden_steps(l, 0, GU_EARLY)
                    h_split_hi("fpre", l, s)
                hidden_steps(l, GU_EARLY, len(HIDDEN))
                hidden_hi(l, *HIDDEN[-1])
                squares_of_y("fpost", l, 0)
                if l + 1 < L:
                    squares_of_x("pre", l + 1, 0)
                    h_split_hi("pre", l + 1, 0)
            for t in range(NT):
                if t == 2:
                    squares_of_y("fpost", L - 1, 1)
                for i in range(2):
                    act.wait_ge(xo_ps, 2 * t + i + 1)
                    copy(xout[:, t, 4 * P * i:4 * P * (i + 1)],
                         bank[i + 2 * (t % 2)][:, :]).then_inc(xo_sb, 1)

        @block.vector
        def _(dve):
            V = nc.vector
            ticks = [0]

            def tick(ins):
                ins.then_inc(dve_tick, 1)
                ticks[0] += 1
                return ticks[0]

            def after(n=None):
                dve.wait_ge(dve_tick, ticks[0] if n is None else n)

            def rsqrt(cols, fill=None):
                xx, tt, yy = rsx[:, cols], rst[:, cols], rsy[:, cols]
                after()
                tick(V.tensor_scalar(yy.bitcast(I32), xx.bitcast(I32), -0.5, RSQRT_MAGIC * 1.0, ALU.mult, ALU.add))
                for step, c in enumerate((-3.0, -12.0, -768.0)):
                    n = ticks[0]
                    if fill:
                        fill()
                    after(n)
                    if cols.stop - cols.start == 2:
                        for i in (cols.start, cols.start + 1):
                            n = tick(V.tensor_scalar(rst[:, i:i + 1], rsy[:, i:i + 1], rsy[:, i:i + 1],
                                                     rsx[:, i:i + 1], ALU.mult, ALU.mult))
                    else:
                        n = tick(V.tensor_tensor(tt, yy, yy, ALU.mult))
                        if fill:
                            fill()
                        after(n)
                        n = tick(V.tensor_tensor(tt, tt, xx, ALU.mult))
                    if fill:
                        fill()
                    after(n)
                    ins = V.scalar_tensor_tensor(out=yy, in0=tt, scalar=c, in1=yy, op0=ALU.add, op1=ALU.mult)
                    if step < 2:
                        tick(ins)
                return ins

            def split_lo(slot):
                if slot >= L * SLOTS:
                    return
                assert dve_splits(slot)
                for part in range(2):
                    n = 2 * slot + part
                    dve.wait_ge(hi_split, n + 1)
                    V.scalar_tensor_tensor(out=ring[:, slot % RING, 1, raw_part(part)], in0=raw[:, n % NRAW, :],
                                           scalar=W_SCALE, in1=ring[:, slot % RING, 0, raw_part(part)],
                                           op0=ALU.mult, op1=ALU.subtract).then_inc(lo_dve, 1)

            def norm_reduce(kind, l, s):
                n = norm_no(kind, l, s)
                for c in range(1, 4):
                    dve.wait_ge(sq_done, 4 * n + c + 1)
                    if c > 1:
                        after()
                    ins = V.tensor_tensor(sq[:, 0:2, :], sq[:, 0:2, :], sq[:, 2 * c:2 * c + 2, :], ALU.add)
                    if c < 3:
                        tick(ins)
                    else:
                        ins.then_inc(ssq_done, 1)

            def norm_rsqrt(kind, l, s):
                n, b = norm_no(kind, l, s), norm_bank(kind, l, s)
                dve.wait_ge(nsum_ps, n + 1)
                if n:
                    dve.wait_ge(rstd_ps, n)
                tick(V.tensor_scalar(rsx[:, 8:10], bank[b][:, 0:2], 1.0 / DM, 1e-6, ALU.mult, ALU.add))
                rsqrt(slice(8, 10)).then_inc(rs_done, 1)

            def norm_scale(kind, l, s, c):
                n, b = norm_no(kind, l, s), norm_bank(kind, l, s)
                k2 = slice(2 * c, 2 * c + 2)
                dst = yT[:, s, k2, :]
                if c == 0:
                    dve.wait_ge(rstd_ps, n + 1)
                if kind in ("pre", "fpre"):
                    src = xT[:, k2, half(s)]
                    if n < 2:
                        dve.wait_ge(xt_ps, 8)
                        dve.wait_ge(xt_sb, 4 * s + 4)
                else:
                    src = dst
                    dve.wait_ge(y_sb, 4 * post_no(kind, l, s) + c + 1)
                V.tensor_tensor(dst, src, bank[b][:, HALF:2 * HALF].unsqueeze(1).to_broadcast([P, 2, HALF]),
                                ALU.mult).then_inc(xr_done, 1)

            def residual(kind, l, s):
                n = norm_no(kind, l, s)
                for c in range(5):
                    if c < 4:
                        norm_scale(kind, l, s, c)
                    if c:
                        dve.wait_ge(xr_done, 4 * n + c)
                        for k in (2 * c - 2, 2 * c - 1):
                            V.scalar_tensor_tensor(out=xT[:, k, half(s)], in0=yT[:, s, k, :],
                                                   scalar=par_col(l, kind, k), in1=xT[:, k, half(s)],
                                                   op0=ALU.mult, op1=ALU.add).then_inc(x_upd, 1)

            def h_split(kind, l, s):
                m = pre_no(kind, l, s)
                for c in range(6):
                    if c < 4:
                        norm_scale(kind, l, s, c)
                    if c > 1:
                        for k in (2 * c - 4, 2 * c - 3):
                            dve.wait_ge(h_hi, KT * m + k + 1)
                            V.scalar_tensor_tensor(out=hT[:, 1, k, half(s)], in0=yT[:, s, k, :],
                                                   scalar=gain(kind, l, k), in1=hT[:, 0, k, half(s)],
                                                   op0=ALU.mult, op1=ALU.subtract).then_inc(h_lo, 1)

            def lo_of(src, ready, kt, l, s, scale, done):
                dve.wait_ge(ready, hs(l, s))
                V.scalar_tensor_tensor(out=ycat[:, 1, kt:kt + 2, half(s)], in0=src, scalar=scale,
                                       in1=ycat[:, 0, kt:kt + 2, half(s)], op0=ALU.mult,
                                       op1=ALU.subtract).then_inc(done, 1)

            def glu(l, s):
                dve.wait_ge(unit_done, unit_no(l, CONV_A, s))
                dve.wait_ge(glu_th, hs(l, s))
                at = CW - 1 + HALF * s
                V.scalar_tensor_tensor(out=hbuf[:, :, at:at + HALF], in0=th, scalar=1.0,
                                       in1=b256(unit_bank(CONV_A, s)), op0=ALU.add,
                                       op1=ALU.mult).then_inc(hb_sb, 1)

            tap_tick = [0, 0]
            taps_done = {}

            def conv(l, s, n):
                if (l, s) not in taps_done:
                    taps_done[(l, s)] = 0
                    dve.wait_ge(hb_sb, hs(l, s))
                    if hs(l, s) > 1:
                        dve.wait_ge(convT_ps, hs(l, s) - 1)
                for i in range(taps_done[(l, s)], min(taps_done[(l, s)] + n, 2 * CW)):
                    k, c = i // 2, i % 2
                    src = hbuf[:, c, HALF * s + k:HALF * s + k + HALF]
                    w = px(l, "cw", 2 * k + c)
                    if k == 0:
                        ins = V.tensor_scalar(cacc[:, c, :], src, w, par_col(l, "cb", c), ALU.mult, ALU.add)
                    else:
                        after(tap_tick[c])
                        ins = V.scalar_tensor_tensor(out=cacc[:, c, :], in0=src, scalar=w,
                                                     in1=cacc[:, c, :], op0=ALU.mult, op1=ALU.add)
                    if i == 2 * CW - 1:
                        ins.then_inc(conv_sb, 1)
                    else:
                        tap_tick[c] = tick(ins)
                    taps_done[(l, s)] = i + 1

            def norm_rows_free(l, s, ret):
                if not ret:
                    dve.wait_ge(retN_sb, 8 * hs(l, s))
                elif l or s:
                    dve.wait_ge(convN_sb, 2 * hs(l, s) - 2)

            def conv_norm(l, s, fill=None):
                dve.wait_ge(convT_ps, hs(l, s))
                for t in range(2):
                    tick(V.bn_stats(cst_st[:, 6 * t:6 * t + 6], b256(5)[:, t, :]))
                after()
                for t in range(2):
                    tick(V.bn_aggr(cmv[:, 2 * t:2 * t + 2], cst_st[:, 6 * t:6 * t + 6]))
                after()
                norm_rows_free(l, s, 0)
                tick(V.tensor_scalar(rsx[:, 0:2], cmv.rearrange("p (t v) -> p t v", v=2)[:, :, 1], 1e-5, None,
                                     ALU.add))
                n = tick(rsqrt(slice(0, 2), fill))
                if fill:
                    fill()
                after(n)
                V.scalar_tensor_tensor(out=nmr[:, 0:2], in0=cmv.rearrange("p (t v) -> p t v", v=2)[:, :, 0],
                                       scalar=-1.0, in1=rsy[:, 0:2], op0=ALU.mult,
                                       op1=ALU.mult).then_inc(conv_rs, 1)

            def conv_out(l, s):
                dve.wait_ge(conv_th, 2 * hs(l, s))
                dve.wait_ge(conv_z, 2 * hs(l, s))
                V.scalar_tensor_tensor(out=ybuf, in0=th, scalar=1.0, in1=ybuf, op0=ALU.add,
                                       op1=ALU.mult).then_inc(conv_y32, 1)

            scratch_read = []

            def rotate(out_, u, cos, sin, n, w):
                ma = m1[:, 0:2 * n * w].rearrange("p (a h d) -> p a h d", a=n, h=2)
                mb = m2[:, 0:2 * n * w].rearrange("p (a h d) -> p a h d", a=n, h=2)
                for sem_, value in scratch_read:
                    dve.wait_ge(sem_, value)
                tick(V.tensor_tensor(ma, u, cos.unsqueeze(2).to_broadcast([P, n, 2, w]), ALU.mult))
                tick(V.scalar_tensor_tensor(out=mb[:, :, 0, :], in0=u[:, :, 1, :], scalar=-1.0, in1=sin,
                                            op0=ALU.mult, op1=ALU.mult))
                tick(V.tensor_tensor(mb[:, :, 1, :], u[:, :, 0, :], sin, ALU.mult))
                after()
                return V.tensor_tensor(out_, ma, mb, ALU.add)

            def table(name, s, w):
                n = 2 * NH * w
                return C(name)[:, s * n:(s + 1) * n].rearrange("p (a d) -> p a d", d=w)

            def ret_rotate(l, s, q):
                slot = (RQ, RK)[q]
                dve.wait_ge(unit_done, unit_no(l, slot, s))
                if l or s:
                    dve.wait_ge(retO_ps, ts(l, 2 * s) - 1)
                u = bank[unit_bank(slot, s)][:, :].rearrange("p (a h d) -> p a h d", h=2, d=32)
                dst = qk[:, q, :, :].rearrange("p t (a h d) -> p (t a) h d", h=2, d=32)
                rotate(dst, u, table(("rqc", "rkc")[q], s, 32), table(("rqs", "rks")[q], s, 32), 2 * NH,
                       32).then_inc(rot_done, 1)
                scratch_read[:] = [(rot_done, 2 * hs(l, s) - 1 + q)]

            def moba_rotate(l, s):
                dve.wait_ge(mq_sb, hs(l, s))
                dve.wait_ge(mk_sb, hs(l, s))
                for q in range(2):
                    u = mqk[:, q, :, :].rearrange("p t (a d) -> p (t a) d", d=HD)[:, :, 0:16].rearrange(
                        "p a (h d) -> p a h d", h=2)
                    ins = rotate(u, u, table("mc", s, 8), table("ms", s, 8), 2 * NH, 8)
                    if q == 0:
                        scratch_read[:] = [(dve_tick, tick(ins))]
                    else:
                        ins.then_inc(mrot, 1)
                        scratch_read[:] = [(mrot, hs(l, s))]

            def ret_mask(l, t):
                dve.wait_ge(retS_ps, ts(l, t))
                if l or t:
                    dve.wait_ge(retO_ps, ts(l, t) - 1)
                smv = sm.rearrange("p (c two) t -> p two c t", two=2)
                for e, b in ((0, 6), (1, 4)):
                    V.tensor_tensor(smv[:, e, :, :], b128(b)[:, 0:2, :],
                                    tri.unsqueeze(1).to_broadcast([P, 2, P]), ALU.mult).then_inc(retS_sb, 1)

            def ret_state(l, t):
                dve.wait_ge(retO_ps, ts(l, t))
                if t == 0:
                    after(zeroed[0])
                else:
                    dve.wait_ge(state_sb, (NT - 1) * l + t)
                for i in range(2):
                    r = slice(HD * i, HD * i + HD)
                    ins = V.tensor_tensor(state[r, :, r], state[r, :, r], b128(6)[r, 0:2, r], ALU.add)
                    if i == 0:
                        tick(ins)
                    else:
                        ins.then_inc(state_sb, 1)

            def ret_norm(l, s, fill=None):
                dve.wait_ge(retO_sb, ts(l, 2 * s + 1))
                for i in range(8):
                    o = osb[:, i // NH, HD * (i % NH):HD * (i % NH + 1)]
                    tick(V.bn_stats(bst[:, 6 * i:6 * i + 6], o))
                for i in range(8):
                    after(ticks[0] - 7)
                    tick(V.bn_aggr(mvr[:, 2 * i:2 * i + 2], bst[:, 6 * i:6 * i + 6]))
                after()
                norm_rows_free(l, s, 1)
                tick(V.tensor_scalar(rsx[:, 0:8], mvr.rearrange("p (i v) -> p i v", v=2)[:, :, 1], 1e-5, None,
                                     ALU.add))
                n = tick(rsqrt(slice(0, 8), fill))
                if fill:
                    fill()
                after(n)
                V.scalar_tensor_tensor(out=nmr, in0=mvr.rearrange("p (i v) -> p i v", v=2)[:, :, 0],
                                       scalar=-1.0, in1=rsy[:, 0:8], op0=ALU.mult,
                                       op1=ALU.mult).then_inc(ret_rs, 1)

            def ret_out(l, s):
                dve.wait_ge(rg_th, hs(l, s))
                dve.wait_ge(ret_z, 2 * hs(l, s))
                V.scalar_tensor_tensor(out=rz, in0=th, scalar=1.0, in1=rz, op0=ALU.add,
                                       op1=ALU.mult).then_inc(ret_g, 1)
                dve.wait_ge(ret_g, hs(l, s))
                dve.wait_ge(pool_y, hs(l, s))
                V.tensor_tensor(ybuf, rz, b256(unit_bank(RG, s)), ALU.mult).then_inc(ret_y32, 1)

            def pool_windows(l, s):
                dve.wait_ge(pool_u, hs(l, s))
                if hs(l, s) > 1:
                    dve.wait_ge(poolY_ps, hs(l, s) - 1)
                if s == 0:
                    after(zeroed[0])
                at = 16 + HALF * s
                tick(V.tensor_tensor(t2, ubuf[:, :, at - 14:at + HALF], ubuf[:, :, at - 15:at + HALF - 1],
                                     ALU.add))
                after()
                tick(V.tensor_tensor(t4, t2[:, :, 2:], t2[:, :, 0:HALF + 12], ALU.add))
                after()
                tick(V.tensor_tensor(t8, t4[:, 1, 4:], t4[:, 1, 0:HALF + 8], ALU.add))
                after()
                lo, hi_ = slice(0, HD), slice(HD, P)
                w16 = m1[:, 0:HALF]
                tick(V.tensor_tensor(w16[hi_, :], t8[hi_, 8:], t8[hi_, 0:HALF], ALU.add))
                after()
                sums_ = [(lo, 0, t2[lo, 0, 14:]), (hi_, 0, t4[hi_, 0, 12:]), (lo, 1, t8[lo, 8:]),
                         (hi_, 1, w16[hi_, :])]
                if s == 0:
                    for r, c, v in sums_:
                        tick(V.tensor_tensor(v[:, 0:16], v[:, 0:16], C("adj")[r, 16 * c:16 * c + 16], ALU.mult))
                    after()
                for i, (r, c, v) in enumerate(sums_):
                    ins = V.scalar_tensor_tensor(out=pooled[r, c, :], in0=v, scalar=1.0 / WINDOWS[i],
                                                 in1=ubuf[r, c, at:at + HALF], op0=ALU.mult, op1=ALU.subtract)
                    if i < 3:
                        tick(ins)
                    else:
                        ins.then_inc(pool_sb, 1)

            def m_max(l, t, h):
                i = ths(l, t, h)
                dve.wait_ge(mS_ps, i)
                if i > 8:
                    dve.wait_ge(mP, i - 8)
                c = (i - 1) % 8
                V.tensor_reduce(nms[:, c:c + 1], bank[(4, 6)[h % 2]][:, 0:P * (t + 1)], AX_X, ALU.max,
                                negate=True).then_inc(mM, 1)

            def m_norm(l, t):
                dve.wait_ge(mPV, ths(l, t, NH - 1))
                dve.wait_ge(mP, ths(l, t, NH - 1))
                c = NH * (t % 2)
                tick(V.reciprocal(rinv[:, c:c + NH], sums[:, c:c + NH]))
                after()
                if hs(l, t // 2) > 1:
                    dve.wait_ge(mY_ps, hs(l, t // 2) - 1)
                V.tensor_tensor(mo[:, t % 2, :].rearrange("p (h e) -> p h e", h=NH),
                                bank[7][:, 0:G].rearrange("p (h e) -> p h e", h=NH),
                                rinv[:, c:c + NH].unsqueeze(2).to_broadcast([P, NH, HD]),
                                ALU.mult).then_inc(mO_sb, 1)

            def hidden(l, f, halves):
                n, w = fno(l, f, halves[0]), HALF * len(halves)
                dve.wait_ge(sil_done, n)
                if n > 2:
                    dve.wait_ge(f_lo, n - 2)
                V.scalar_tensor_tensor(out=fbuf[:, n % 2, 0:w], in0=gu_tiles(f, halves)[1],
                                       scalar=UNSCALE * A_SCALE, in1=sil[:, n % 2, 0:w], op0=ALU.mult,
                                       op1=ALU.mult).then_inc(f_sb, 1)

            def hidden_lo(l, f, halves):
                n, w = fno(l, f, halves[0]), HALF * len(halves)
                dve.wait_ge(f_hi, n)
                V.tensor_tensor(fT[:, 1, f, span(halves)], fbuf[:, n % 2, 0:w], fT[:, 0, f, span(halves)],
                                ALU.subtract).then_inc(f_lo, 1)

            def hidden_steps(l, i0, i1):
                for i in range(i0, i1):
                    f, halves = HIDDEN[i]
                    hidden(l, f, halves)
                    if i:
                        hidden_lo(l, *HIDDEN[i - 1])
                    if 1 in halves:
                        split_lo(l * SLOTS + GU0 + f + RING)

            zeroed = [0]
            tick(V.memset(bd[:, :, :, :], 0.0))
            tick(V.memset(hbuf[:, :, 0:CW - 1], 0.0))
            dve.wait_ge(consts_in, 16)
            dve.wait_ge(params_in, 16)
            for l in range(L):
                for name, source, cols, scale in PARX_FROM:
                    last = V.tensor_scalar(parx[:, l, PARX[name]:PARX[name] + cols],
                                           par[:, l, PAR[source]:PAR[source] + cols], scale, None, ALU.mult)
                    if (l, name) != (L - 1, PARX_FROM[-1][0]):
                        tick(last)
            last.then_inc(setup_done, 1)
            dve.wait_ge(setup_done, 1)
            after()
            for l in range(L):
                V.tensor_tensor(parx[:, l, PARX["pbs"]:PARX["pbs"] + 2], parx[:, l, PARX["pbs"]:PARX["pbs"] + 2],
                                par[:, l, PAR["ps"]:PAR["ps"] + 2], ALU.mult).then_inc(setup_done, 1)
            norm_reduce("pre", 0, 0)
            norm_rsqrt("pre", 0, 0)
            for slot in FIRST_BY_DVE:
                split_lo(slot)
            h_split("pre", 0, 0)
            for l in range(L):
                if l:
                    norm_reduce("fpost", l - 1, 1)
                    norm_rsqrt("fpost", l - 1, 1)
                    glu(l, 0)
                    residual("fpost", l - 1, 1)
                norm_reduce("pre", l, 1)
                norm_rsqrt("pre", l, 1)
                if not l:
                    h_split("pre", l, 1)
                    glu(l, 0)
                ret_rotate(l, 0, 0)
                ret_rotate(l, 0, 1)
                if l:
                    h_split("pre", l, 1)
                dve.wait_ge(unit_done, unit_no(l, CONV_A, 0))
                tick(V.memset(state, 0.0))
                zeroed[0] = tick(V.memset(ubuf[:, :, 0:16], 0.0))
                conv(l, 0, 3)
                ret_mask(l, 0)
                conv(l, 0, 5)
                ret_state(l, 0)
                conv(l, 0, 8)
                ret_mask(l, 1)
                conv(l, 0, 5)
                ret_state(l, 1)
                ret_norm(l, 0, lambda: conv(l, 0, 1))
                conv(l, 0, 2)
                glu(l, 1)
                conv(l, 0, 4)
                ret_rotate(l, 1, 0)
                conv(l, 0, 6)
                ret_rotate(l, 1, 1)
                conv(l, 0, 4)
                ret_mask(l, 2)
                conv(l, 0, 5)
                ret_state(l, 2)
                conv(l, 0, 4)
                ret_mask(l, 3)
                conv(l, 0, 2 * CW)
                pool_windows(l, 0)
                conv_norm(l, 0, lambda: conv(l, 1, 1))
                conv(l, 1, 4)
                conv_out(l, 0)
                lo_of(ybuf, conv_hi, 0, l, 0, 0.5 * A_SCALE, conv_y)
                moba_rotate(l, 0)
                conv(l, 1, 4)
                lo_of(ybuf, pool_hi, 6, l, 0, A_SCALE, pool_y)
                conv(l, 1, 4)
                m_max(l, 0, 0)
                m_max(l, 0, 1)
                conv(l, 1, 5)
                m_max(l, 0, 2)
                m_max(l, 0, 3)
                conv(l, 1, 3)
                ret_out(l, 0)
                m_max(l, 1, 0)
                m_max(l, 1, 1)
                lo_of(ybuf, ret_hi, 2, l, 0, 0.5 * A_SCALE * UNSCALE, ret_y)
                conv(l, 1, 4)
                m_norm(l, 0)
                m_max(l, 1, 2)
                m_max(l, 1, 3)
                moba_rotate(l, 1)
                conv(l, 1, 5)
                m_norm(l, 1)
                ret_norm(l, 1, lambda: conv(l, 1, 1))
                lo_of(b256(5), moba_hi, 4, l, 0, A_SCALE, moba_y)
                conv(l, 1, 3)
                m_max(l, 2, 0)
                m_max(l, 2, 1)
                conv(l, 1, 2 * CW)
                m_max(l, 2, 2)
                m_max(l, 2, 3)
                conv_norm(l, 1)
                pool_windows(l, 1)
                m_max(l, 3, 0)
                m_max(l, 3, 1)
                conv_out(l, 1)
                m_norm(l, 2)
                m_max(l, 3, 2)
                m_max(l, 3, 3)
                lo_of(ybuf, conv_hi, 0, l, 1, 0.5 * A_SCALE, conv_y)
                lo_of(ybuf, pool_hi, 6, l, 1, A_SCALE, pool_y)
                ret_out(l, 1)
                m_norm(l, 3)
                lo_of(ybuf, ret_hi, 2, l, 1, 0.5 * A_SCALE * UNSCALE, ret_y)
                lo_of(b256(5), moba_hi, 4, l, 1, A_SCALE, moba_y)
                for s in range(2):
                    norm_reduce("post", l, s)
                    norm_rsqrt("post", l, s)
                    residual("post", l, s)
                    norm_reduce("fpre", l, s)
                    if s:
                        hidden_steps(l, 0, GU_EARLY)
                    norm_rsqrt("fpre", l, s)
                    h_split("fpre", l, s)
                hidden_steps(l, GU_EARLY, len(HIDDEN))
                hidden_lo(l, *HIDDEN[-1])
                for c in range(N_DN - DN_TAIL):
                    split_lo(l * SLOTS + DN0 + c + RING)
                norm_reduce("fpost", l, 0)
                norm_rsqrt("fpost", l, 0)
                residual("fpost", l, 0)
                if l + 1 < L:
                    norm_reduce("pre", l + 1, 0)
                    norm_rsqrt("pre", l + 1, 0)
                    h_split("pre", l + 1, 0)
            norm_reduce("fpost", L - 1, 1)
            norm_rsqrt("fpost", L - 1, 1)
            residual("fpost", L - 1, 1)


def rotary_table(dim, theta, np):
    inv = 1.0 / (theta ** (np.arange(0, dim, 2, dtype=np.float32) / np.float32(dim)))
    ang = (np.arange(S, dtype=np.float32)[:, None] * inv[None, :].astype(np.float32)).astype(np.float32)
    return np.cos(ang), np.sin(ang)


def constants():
    import numpy as np
    c = np.zeros((P, CST_COLS), np.float32)

    def put(name, a):
        c[:, CST[name]:CST[name] + a.shape[1]] = a

    i = np.arange(P)
    put("ident", np.eye(P))
    put("ident_x", np.eye(P) / RS)
    put("ident_y", np.eye(P) * UNSCALE / RS)
    put("ones", np.ones((P, P)))
    put("tri", (i[:, None] <= i[None, :]))
    put("neg", np.where(i[None, :] > i[:, None], -1e30, 0.0))
    pos = np.arange(S, dtype=np.float64)
    gamma = 1.0 - 2.0 ** (-5.0 - np.arange(NH))
    grow = gamma[None, :] ** (pos[:, None] + 1.0)
    cos, sin = rotary_table(HD, 10000.0, np)

    def tiles(a):
        return a.reshape(NT, P, -1).transpose(1, 0, 2).reshape(P, -1)

    for name, trig, decay in (("rqc", cos, grow * UNSCALE), ("rqs", sin, grow * UNSCALE),
                              ("rkc", cos, UNSCALE * HD ** -0.5 / grow),
                              ("rks", sin, UNSCALE * HD ** -0.5 / grow)):
        put(name, tiles(trig[:, None, :] * decay[:, :, None]))
    mcos, msin = rotary_table(HD // 4, 500000.0, np)
    for name, trig in (("mc", mcos), ("ms", msin)):
        put(name, tiles(np.repeat(trig[:, None, :], NH, axis=1)))
    adj = np.ones((P, 2, 16))
    for g, w in enumerate(WINDOWS):
        rows = slice(HD * (g % 2), HD * (g % 2) + HD)
        adj[rows, g // 2, :] = w / np.minimum(np.arange(16) + 1.0, w)
    put("adj", adj.reshape(P, 32))
    return c


def kernel(x, attn_pre_g, w_in, conv_w, conv_b, conv_ln_g, conv_ln_b, ret_gn_g, ret_gn_b, pool_w, pool_b,
           pool_scale, w_out, attn_post_g, ffn_pre_g, w_gate, w_up, w_down, ffn_post_g):
    import numpy as np
    import concourse.bacc as bacc
    from concourse.bass_utils import run_bass_kernel_spmd

    w_in, w_out, w_gate, w_up, w_down = map(np.asarray, (w_in, w_out, w_gate, w_up, w_down))
    weights = np.empty((L, SLOTS, P, SLOT), np.float32)
    by_col = w_in.reshape(L, KT, P, N_IN, G)
    for slot, blk in BLOCK_OF.items():
        weights[:, slot] = by_col[:, :, :, blk].transpose(0, 2, 1, 3).reshape(L, P, SLOT)
    weights[:, OUT0:GU0] = w_out.reshape(L, KT, P, N_OUT, 2 * P).transpose(0, 3, 2, 1, 4).reshape(
        L, N_OUT, P, SLOT)
    gu = np.stack([w_gate.reshape(L, KT, P, FT, P), w_up.reshape(L, KT, P, FT, P)], axis=4)
    weights[:, GU0:DN0] = gu.transpose(0, 3, 2, 1, 4, 5).reshape(L, N_GU, P, SLOT)
    weights[:, DN0:] = w_down.reshape(L, N_DN, 2, P, DM).transpose(0, 1, 3, 2, 4).reshape(L, N_DN, P, SLOT)

    params = np.empty((P, L, PAR_COLS), np.float32)
    for name, a in (("pre", attn_pre_g), ("post", attn_post_g), ("fpre", ffn_pre_g), ("fpost", ffn_post_g),
                    ("cw", conv_w), ("cb", conv_b), ("lng", conv_ln_g), ("lnb", conv_ln_b),
                    ("gng", ret_gn_g), ("gnb", ret_gn_b), ("pb", pool_b), ("ps", pool_scale)):
        a = np.asarray(a).reshape(L, -1, P)
        params[:, :, PAR[name]:PAR[name] + a.shape[1]] = a.transpose(2, 0, 1)

    arrays = {"x": np.ascontiguousarray(np.asarray(x).reshape(S, DM)),
              "weights": weights.reshape(L * SLOTS, P, SLOT), "params": params,
              "pool_w": np.ascontiguousarray(pool_w), "consts": constants()}
    nc = bacc.Bacc("TRN2", target_bir_lowering=False, num_devices=1)
    aps = [nc.dram_tensor(f"{n}_dram", a.shape, mybir.dt.from_np(a.dtype), kind="ExternalInput").ap()
           for n, a in arrays.items()]
    out = nc.dram_tensor("out_dram", (S, DM), F32, kind="ExternalOutput").ap()
    trunk_program(nc, *aps, out)
    got = run_bass_kernel_spmd(nc, [{f"{n}_dram": a for n, a in arrays.items()}], core_ids=[0])
    return got.results[0]["out_dram"].reshape(1, S, DM)
```

```python
import math
from contextlib import ExitStack

import concourse.bass as bass
from concourse import mybir

F32 = mybir.dt.float32
F16 = mybir.dt.float16
BF16 = mybir.dt.bfloat16
I32 = mybir.dt.int32
ALU = mybir.AluOpType
ACT = mybir.ActivationFunctionType
AX_X = mybir.AxisListType.X

P = 128
DM = 1024
S = 512
L = 2
KT = DM // P
HALF = S // 2
NT = S // P
G = DM // 4
HD = 64
NH = G // HD
CW = 31
FF = 2816
FT = FF // P
WINDOWS = (2, 4, 8, 16)

SLOT = 2048
PARTS = 4
RAW = SLOT // PARTS
NRAW = 4
RING = 8

W_SCALE = 1024.0
A_SCALE = 32.0
UNSCALE = 1.0 / (W_SCALE * A_SCALE)
RSQRT_MAGIC = float(0x5F3759DF)
RS = -8192.0

CONV_A, CONV_G, RQ, RK, RV, POOL, MQ, MK, MV, RG = range(10)
BLOCK_OF = {CONV_A: 0, CONV_G: 1, RQ: 2, RK: 3, RV: 4, POOL: 9, MQ: 6, MK: 7, MV: 8, RG: 5}
TOKEN_MAJOR = (RQ, RK, RV, MQ, MK, MV)
IN_GROUPS = (range(0, 6), range(6, 10))
N_IN, N_OUT, N_GU, N_DN = 10, 4, FT, FT // 2
OUT0 = N_IN
GU0 = OUT0 + N_OUT
DN0 = GU0 + N_GU
SLOTS = DN0 + N_DN
GU_HEAD = 6
DN_TAIL = 6
FIRST_BY_DVE = (0, 1, 2, 3, 4, 5)

UNITS = []
for group in IN_GROUPS:
    UNITS += [(c, (s,)) for s in range(2) for c in group]
UNITS += [(OUT0 + c, (s,)) for s in range(2) for c in range(N_OUT)]
UNITS += [(GU0 + c, (s,)) for s in range(2) for c in range(GU_HEAD)]
UNITS += [(GU0 + c, (0, 1)) for c in range(GU_HEAD, N_GU)]
UNITS += [(DN0 + c, (s,)) for c in range(N_DN - DN_TAIL) for s in range(2)]
UNITS += [(DN0 + c, (s,)) for s in range(2) for c in range(N_DN - DN_TAIL, N_DN)]
NU = len(UNITS)
UNIT_AT = {(slot, s): i for i, (slot, halves) in enumerate(UNITS) for s in halves}
HIDDEN = [(slot - GU0, halves) for slot, halves in UNITS if GU0 <= slot < DN0]
HIDDEN_AT = {(f, s): i for i, (f, halves) in enumerate(HIDDEN) for s in halves}
GU_EARLY = 2
assert len(UNIT_AT) == 2 * SLOTS and UNIT_AT[(GU0 + GU_HEAD, 0)] % 4 == 0

AT = {
    ("fpost_sum", 1): 8,
    ("fpost_bcast", 1): 20,
    ("first_bcast", 1): 29,
    ("pre_sum", 1): 63,
    ("pre_bcast", 1): 72,
    ("ret_T", 0): 101,
    ("ret_S", 0): 105,
    ("ret_O", 0): 109,
    ("ret_T", 1): 109,
    ("ret_S", 1): 114,
    ("ret_O", 1): 120,
    ("ret_Y", 0): 156,
    ("ret_T", 2): 180,
    ("ret_S", 2): 183,
    ("ret_O", 2): 190,
    ("ret_T", 3): 193,
    ("ret_S", 3): 200,
    ("ret_O", 3): 205,
    ("conv_T", 0): 213,
    ("conv_Y", 0): 238,
    ("pool_Y", 0): 246,
    ("moba_T", 0): 256,
    ("moba_T", 1): 259,
    ("moba_stage", 0): 261,
    ("moba_stage", 1): 271,
    ("moba_stage", 2): 283,
    ("moba_stage", 3): 285,
    ("moba_stage", 4): 291,
    ("moba_stage", 5): 296,
    ("moba_T", 2): 300,
    ("moba_Y", 0): 311,
    ("moba_T", 3): 312,
    ("moba_stage", 6): 316,
    ("moba_stage", 7): 322,
    ("ret_Y", 1): 327,
    ("conv_T", 1): 331,
    ("moba_stage", 8): 346,
    ("moba_stage", 9): 350,
    ("conv_Y", 1): 355,
    ("pool_Y", 1): 357,
    ("moba_stage", 10): 360,
    ("moba_stage", 11): 363,
    ("moba_Y", 1): 370,
    ("post_sum", 0): 391,
    ("post_bcast", 0): 400,
    ("fpre_sum", 0): 422,
    ("fpre_bcast", 0): 431,
    ("post_sum", 1): 461,
    ("post_bcast", 1): 472,
    ("fpre_sum", 1): 499,
    ("fpre_bcast", 1): 514,
    ("fpost_sum", 0): 1160,
    ("fpost_bcast", 0): 1170,
    ("pre_sum", 0): 1196,
    ("x_out_T", 0): 1199,
    ("pre_bcast", 0): 1205,
}

PAR = {}
PAR_COLS = 0
for name, cols in (("pre", KT), ("post", KT), ("fpre", KT), ("fpost", KT), ("cw", 2 * CW), ("cb", 2),
                   ("lng", 2), ("lnb", 2), ("gng", 2), ("gnb", 2), ("pb", 2), ("ps", 2)):
    PAR[name] = PAR_COLS
    PAR_COLS += cols

PARX = {}
PARX_COLS = 0
PARX_FROM = (("pre", "pre", KT, A_SCALE), ("fpre", "fpre", KT, A_SCALE), ("cw", "cw", 2 * CW, 0.5 * UNSCALE),
             ("lng", "lng", 2, 1.0 / RS), ("lng_half", "lng", 2, 0.5 / RS), ("lnb_half", "lnb", 2, 0.5),
             ("gng", "gng", 2, 1.0 / RS), ("pbs", "pb", 2, 1.0))
for name, _, cols, _ in PARX_FROM:
    PARX[name] = PARX_COLS
    PARX_COLS += cols

CST = {}
CST_COLS = 0
for name, cols in (("ident", P), ("ident_x", P), ("ident_y", P), ("tri", P), ("ident16", P // 2),
                   ("neg16", P // 2), ("ones", 1), ("rqc", NT * NH * 32), ("rqs", NT * NH * 32),
                   ("rkc", NT * NH * 32), ("rks", NT * NH * 32), ("mc", NT * NH * 8), ("ms", NT * NH * 8),
                   ("adj", 2 * 16)):
    CST[name] = CST_COLS
    CST_COLS += cols


def trunk_program(nc, x, weights, params, pool_w, consts, out):
    with ExitStack() as ctx:
        def sb(name, shape, dt=F32):
            return ctx.enter_context(nc.sbuf_tensor(name, shape, dt))

        def sem(name):
            return ctx.enter_context(nc.semaphore(name))

        xT = sb("xT", [P, KT, S])
        hT = sb("hT", [P, 2, KT, S], F16)
        yT = sb("yT", [P, 2, KT, HALF])
        sq = sb("sq", [P, KT, HALF])
        raw = sb("raw", [P, NRAW, RAW])
        ring = sb("ring", [P, RING, 2, SLOT], F16)
        U = sb("U", [P, FT * S])
        E = sb("E", [P, 4672])
        cst = sb("cst", [P, CST_COLS])
        par = sb("par", [P, L, PAR_COLS])
        parx = sb("parx", [P, L, PARX_COLS])
        bd = sb("bd", [P, L, 2, P])
        small = sb("small", [P, 142])
        bank = [ctx.enter_context(nc.psum_tensor(f"bank{i}", [P, 512], F32)) for i in range(8)]

        def C(name):
            at = CST[name]
            nxt = min([v for v in CST.values() if v > at] + [CST_COLS])
            return cst[:, at:nxt]

        ident, ident_x, ident_y, tri, ones = map(C, ("ident", "ident_x", "ident_y", "tri", "ones"))
        ident16, neg16 = C("ident16").bitcast(BF16), C("neg16").bitcast(BF16)

        fT = U[:, :].bitcast(F16).rearrange("p (h f t) -> p h f t", h=2, f=FT)

        def carve(buf, sizes):
            at, got = 0, []
            for n in sizes:
                got.append(buf[:, at:at + n])
                at += n
            return got

        (ycat_w, ubuf_w, rv_w, mv_w, mqk_w, mkT_w, mqT_w, o_w, th_w, state_w) = carve(
            U, [KT * S, 2 * (16 + S), NT * G, NT * G, 2 * 2 * G, 2 * S, 2 * 2 * P, 2 * G, 2 * HALF, 2 * P])
        ycat = ycat_w.bitcast(F16).rearrange("p (h k t) -> p h k t", h=2, k=KT)
        ubuf = ubuf_w.rearrange("p (c t) -> p c t", c=2)
        rv = rv_w.rearrange("p (t c) -> p t c", t=NT)
        mv = mv_w.rearrange("p (t c) -> p t c", t=NT)
        mqk = mqk_w.rearrange("p (q t c) -> p q t c", q=2, t=2)
        mkT = mkT_w.rearrange("p (c t) -> p c t", c=2)
        mqT = mqT_w.rearrange("p (b c t) -> p b c t", b=2, c=2)
        osb = o_w.rearrange("p (t c) -> p t c", t=2)
        th = th_w.rearrange("p (c t) -> p c t", c=2)
        yA = yT[:, 0, :, :].rearrange("p k t -> p (k t)")
        yB = yT[:, 1, :, :].rearrange("p k t -> p (k t)")
        qk_w, rT_w, sm_w = carve(yA, [2 * 2 * G, 4 * P, 4 * P])
        qk = qk_w.rearrange("p (q t c) -> p q t c", q=2, t=2)
        rT = rT_w.rearrange("p (c t) -> p c t", c=4)
        sm = sm_w.rearrange("p (h t) -> p h t", h=4)
        pr_w, pT_w = carve(yB, [2 * S, 2 * S])
        pr = pr_w.rearrange("p (b t) -> p b t", b=2)
        pT = pT_w.rearrange("p (b j t) -> p b j t", b=2, j=NT)
        sqf = sq[:, :, :].rearrange("p k t -> p (k t)")
        t2_w, t4_w, t8, pooled_w = carve(sqf, [2 * (HALF + 14), 2 * (HALF + 12), HALF + 8, 2 * HALF])
        t2 = t2_w.rearrange("p (c t) -> p c t", c=2)
        t4 = t4_w.rearrange("p (c t) -> p c t", c=2)
        pooled = pooled_w.rearrange("p (c t) -> p c t", c=2)
        (rz_w, cn_w, yb_w, m1, m2, hb_w, ca_w, mo_w) = carve(
            E, [2 * HALF, 2 * G, 2 * HALF, 2 * HALF, 2 * HALF, 2 * (CW - 1 + S), 2 * HALF, 2 * G])
        mo = mo_w.rearrange("p (t c) -> p t c", t=2)
        rz = rz_w.rearrange("p (c t) -> p c t", c=2)
        cn = cn_w.rearrange("p (t c) -> p t c", t=2)
        ybuf = yb_w.rearrange("p (c t) -> p c t", c=2)
        hbuf = hb_w.rearrange("p (c t) -> p c t", c=2)
        cacc = ca_w.rearrange("p (c t) -> p c t", c=2)
        state = state_w.rearrange("p (c e) -> p c e", c=2)
        sil = E[:, 0:2 * S].rearrange("p (b t) -> p b t", b=2)
        fbuf = E[:, 2 * S:4 * S].rearrange("p (b t) -> p b t", b=2)
        xsq = sqf[:, 0:DM]
        xin = yT[:, :, :, :].rearrange("p s k t -> p (s k t)").rearrange("p (t c) -> p t c", t=NT)
        xout = hT[:, :, :, :].rearrange("p h k t -> p (h k t)").bitcast(F32).rearrange(
            "p (t c) -> p t c", t=NT)
        (rsx, rst, rsy, nmr, nms, sums, rinv, bst, mvr, cst_st, cmv) = carve(
            small, [10, 10, 10, 8, 8, 8, 8, 48, 16, 12, 4])

        def half(s):
            return slice(HALF * s, HALF * (s + 1))

        def span(halves):
            return slice(HALF * halves[0], HALF * (halves[-1] + 1))

        def tok(t):
            return slice(P * t, P * (t + 1))

        def b256(b):
            return bank[b][:, :].rearrange("p (c t) -> p c t", c=2)

        def b128(b):
            return bank[b][:, :].rearrange("p (c t) -> p c t", c=4)

        def par_col(l, name, c):
            return par[:, l, PAR[name] + c:PAR[name] + c + 1]

        def px(l, name, c):
            return parx[:, l, PARX[name] + c:PARX[name] + c + 1]

        def gain(kind, l, k):
            return px(l, kind, k)

        ident_in = sem("ident_in")
        idents_in = sem("idents_in")
        consts_in = sem("consts_in")
        params_in = sem("params_in")
        maps_in = sem("maps_in")
        x_in = [sem(f"x_in{t}") for t in range(NT)]
        hi_split = sem("hi_split")
        raw_scaled = sem("raw_scaled")
        lo_pool = sem("lo_pool")
        lo_dve = sem("lo_dve")
        unit_done = sem("unit_done")
        mqT_sb = sem("mqT_sb")
        dve_tick = sem("dve_tick")
        setup_done = sem("setup_done")
        xt_ps = sem("xt_ps")
        x_sq = sem("x_sq")
        xt_sb = sem("xt_sb")
        y_sb = sem("y_sb")
        sq_done = sem("sq_done")
        ssq_done = sem("ssq_done")
        nsum_ps = sem("nsum_ps")
        rs_done = sem("rs_done")
        rstd_ps = sem("rstd_ps")
        dn_bank = sem("dn_bank")
        xr_done = sem("xr_done")
        x_upd = sem("x_upd")
        h_hi = sem("h_hi")
        h_lo = sem("h_lo")
        glu_th = sem("glu_th")
        hb_sb = sem("hb_sb")
        rot_done = sem("rot_done")
        rv_sb = sem("rv_sb")
        retT_ps = sem("retT_ps")
        retT_sb = sem("retT_sb")
        retS_ps = sem("retS_ps")
        retS_sb = sem("retS_sb")
        retO_ps = sem("retO_ps")
        retO_sb = sem("retO_sb")
        state_sb = sem("state_sb")
        ret_rs = sem("ret_rs")
        retN_sb = sem("retN_sb")
        retY_ps = sem("retY_ps")
        ret_z = sem("ret_z")
        rg_th = sem("rg_th")
        ret_g = sem("ret_g")
        ret_y32 = sem("ret_y32")
        ret_hi = sem("ret_hi")
        ret_y = sem("ret_y")
        conv_sb = sem("conv_sb")
        convT_ps = sem("convT_ps")
        conv_rs = sem("conv_rs")
        convN_sb = sem("convN_sb")
        convY_ps = sem("convY_ps")
        conv_th = sem("conv_th")
        conv_z = sem("conv_z")
        conv_y32 = sem("conv_y32")
        conv_hi = sem("conv_hi")
        conv_y = sem("conv_y")
        pool_u = sem("pool_u")
        pool_sb = sem("pool_sb")
        poolY_ps = sem("poolY_ps")
        pool_y32 = sem("pool_y32")
        pool_hi = sem("pool_hi")
        pool_y = sem("pool_y")
        mq_sb = sem("mq_sb")
        mk_sb = sem("mk_sb")
        mrot = sem("mrot")
        mv_sb = sem("mv_sb")
        mT_ps = sem("mT_ps")
        mkT_sb = sem("mkT_sb")
        mS_ps = sem("mS_ps")
        mM = sem("mM")
        mP = sem("mP")
        mPT_ps = sem("mPT_ps")
        mPT_sb = sem("mPT_sb")
        mPV = sem("mPV")
        mO_sb = sem("mO_sb")
        mY_ps = sem("mY_ps")
        moba_hi = sem("moba_hi")
        moba_y = sem("moba_y")
        sil_done = sem("sil_done")
        f_sb = sem("f_sb")
        f_hi = sem("f_hi")
        f_lo = sem("f_lo")
        xo_ps = sem("xo_ps")
        xo_sb = sem("xo_sb")
        stored = sem("stored")
        raw_in = [sem(f"raw_in{i}") for i in range(NRAW)]

        def dve_splits(n):
            return n in FIRST_BY_DVE or (n >= RING and GU0 <= (n - RING) % SLOTS < SLOTS - DN_TAIL)

        def split_count(n):
            by_dve = dve_splits(n // PARTS)
            count = sum(dve_splits(i // PARTS) == by_dve for i in range(n + 1))
            return (lo_dve if by_dve else lo_pool), count

        def unit_no(l, slot, s):
            return l * NU + UNIT_AT[(slot, s)] + 1

        def hs(l, s):
            return 2 * l + s + 1

        def ts(l, t):
            return NT * l + t + 1

        def ths(l, t, h):
            return NH * (NT * l + t) + h + 1

        def fno(l, f, s):
            return len(HIDDEN) * l + HIDDEN_AT[(f, s)] + 1

        def unit_bank(slot, s):
            return UNIT_AT[(slot, s)] % 4

        def gu_tiles(f, halves):
            if len(halves) == 1:
                b = unit_bank(GU0 + f, halves[0])
                return b256(b)[:, 0, :], b256(b)[:, 1, :]
            b = 2 * (f % 2)
            return bank[b][:, :], bank[b + 1][:, :]

        NORMS = [("pre", 0, 0), ("pre", 0, 1)]
        for l in range(L):
            for s in range(2):
                NORMS += [("post", l, s), ("fpre", l, s)]
            for s in range(2):
                NORMS += [("fpost", l, s)] + ([("pre", l + 1, s)] if l + 1 < L else [])
        PRES = [n for n in NORMS if n[0] in ("pre", "fpre")]
        POSTS = [n for n in NORMS if n[0] in ("post", "fpost")]

        def norm_no(*n):
            return NORMS.index(n)

        def pre_no(*n):
            return PRES.index(n)

        def post_no(*n):
            return POSTS.index(n)

        def norm_bank(kind, l, s):
            return 3 if s == 0 and (kind == "fpost" or (kind == "pre" and l)) else 7

        X_BANKS = ((0, 1, 2, 3), (4, 5, 6, 3))

        def raw_part(i):
            return slice(RAW * i, RAW * (i + 1))

        block = ctx.enter_context(nc.Block())

        @block.sync
        def _(sp):
            sp.dma_start(ident, consts[:, 0:P]).then_inc(ident_in, 16)
            for t in range(2):
                sp.dma_start(xin[:, t, :], x[tok(t), :]).then_inc(x_in[t], 16)
            sp.dma_start(cst[:, P:3 * P], consts[:, P:3 * P]).then_inc(idents_in, 16)
            for n in range(PARTS * L * SLOTS):
                if n == 0:
                    sp.dma_start(par[:, :, :], params).then_inc(params_in, 16)
                if n >= NRAW:
                    sp.wait_ge(*split_count(n - NRAW))
                sp.dma_start(raw[:, n % NRAW, :], weights[n, :, :]).then_inc(
                    raw_in[n % NRAW], 16)
                if n == PARTS - 1:
                    for t in range(2, NT):
                        sp.dma_start(xin[:, t, :], x[tok(t), :]).then_inc(x_in[t], 16)
                if n == 2 * PARTS - 1:
                    sp.dma_start(cst[:, 3 * P:], consts[:, 3 * P:]).then_inc(consts_in, 16)
                    sp.wait_ge(dve_tick, 1)
                    for l in range(L):
                        for g in range(4):
                            r = slice(HD * (g % 2), HD * (g % 2) + HD)
                            sp.dma_start(bd[r, l, g // 2, r], pool_w[l, g, :, :]).then_inc(maps_in, 16)
            for n in range(2 * NT):
                s, i, t = n // 4, n // 2 % 2, n % 2
                cols = slice(4 * P * i, 4 * P * (i + 1))
                sp.wait_ge(xo_sb, n + 1)
                sp.dma_start(out[tok(2 * s + t), cols], xout[:, 2 * s + t, cols]).then_inc(stored, 16)
            sp.wait_ge(stored, 32 * NT)

        SCALED = L * len(PARX_FROM)

        @block.gpsimd
        def _(pool):
            pool.wait_ge(params_in, 16)
            for l in range(L):
                for name, source, cols, scale in PARX_FROM:
                    nc.gpsimd.tensor_scalar(parx[:, l, PARX[name]:PARX[name] + cols],
                                            par[:, l, PAR[source]:PAR[source] + cols], scale, 1.0, ALU.mult,
                                            ALU.mult).then_inc(setup_done, 1)
            pool.wait_ge(setup_done, SCALED)
            for l in range(L):
                pbs = parx[:, l, PARX["pbs"]:PARX["pbs"] + 2]
                nc.gpsimd.tensor_tensor(pbs, pbs, par[:, l, PAR["ps"]:PAR["ps"] + 2],
                                        ALU.mult).then_inc(setup_done, 1)
            for n in range(PARTS * L * SLOTS):
                slot, part = n // PARTS, n % PARTS
                hi = ring[:, slot % RING, 0, raw_part(part)]
                lo = ring[:, slot % RING, 1, raw_part(part)]
                pool.wait_ge(raw_in[n % NRAW], 16 * (n // NRAW + 1))
                if slot >= RING:
                    old = slot - RING
                    pool.wait_ge(unit_done, unit_no(old // SLOTS, old % SLOTS, 1))
                src = raw[:, n % NRAW, :]
                nc.gpsimd.tensor_scalar(hi, src, W_SCALE, 1.0, ALU.mult, ALU.mult).then_inc(hi_split, 1)
                if not dve_splits(slot):
                    pool.wait_ge(hi_split, n + 1)
                    nc.gpsimd.tensor_scalar(src, src, W_SCALE, 1.0, ALU.mult, ALU.mult).then_inc(raw_scaled, 1)
                    pool.wait_ge(raw_scaled, split_count(n)[1])
                    nc.gpsimd.tensor_tensor(lo, src, hi, ALU.subtract).then_inc(lo_pool, 1)

        @block.tensor
        def _(pe):
            mm = nc.tensor.matmul
            freed_by = [None] * 8

            def take(b, sem, value):
                if freed_by[b] is not None:
                    pe.wait_ge(*freed_by[b])
                freed_by[b] = (sem, value)

            def split3(dst, w, a, first, last, weights_still, **kw):
                for i, (pw, pa) in enumerate(((0, 0), (0, 1), (1, 0))):
                    st, mv_ = (w[pw], a[pa]) if weights_still else (a[pa], w[pw])
                    ins = mm(dst, st, mv_, start=first and i == 0, stop=last and i == 2, **kw)
                return ins

            def transpose(dst, src):
                return nc.tensor.transpose(dst, src, ident)

            def last_read(l, slot, s):
                if slot >= GU0:
                    return f_sb, fno(l, slot - GU0, s)
                if slot >= OUT0:
                    return y_sb, KT * post_no("post", l, s) + 2 * (slot - OUT0) + 2
                return {CONV_A: (hb_sb, hs(l, s)), CONV_G: (glu_th, hs(l, s)), RQ: (rot_done, 2 * hs(l, s) - 1),
                        RK: (rot_done, 2 * hs(l, s)), RV: (rv_sb, hs(l, s)), POOL: (pool_u, hs(l, s)),
                        MQ: (mq_sb, hs(l, s)), MK: (mk_sb, hs(l, s)), MV: (mv_sb, hs(l, s)),
                        RG: (ret_y32, hs(l, s))}[slot]

            def unit(l, slot, halves, between):
                s = halves[0]
                if s == 0:
                    pe.wait_ge(*split_count(PARTS * (l * SLOTS + slot + 1) - 1))
                w = [ring[:, (l * SLOTS + slot) % RING, i, :].rearrange(
                    "p (k n) -> p k n", k=KT if slot < DN0 else 2) for i in range(2)]
                pre = {0: "pre", GU0: "fpre"}.get(slot)
                if slot < OUT0:
                    b = unit_bank(slot, s)
                    take(b, *last_read(l, slot, s))
                    for c in range(2):
                        for k in range(KT):
                            between(KT * c + k)
                            if pre and c == 0:
                                pe.wait_ge(h_lo, KT * pre_no(pre, l, s) + k + 1)
                            if slot in TOKEN_MAJOR:
                                cols, rows = slice(0, G), tok(2 * s + c)
                            else:
                                cols, rows = slice(P * c, P * (c + 1)), half(s)
                            last = split3(b256(b)[:, c, :], [w[0][:, k, cols], w[1][:, k, cols]],
                                          [hT[:, 0, k, rows], hT[:, 1, k, rows]],
                                          k == 0, k == KT - 1, slot not in TOKEN_MAJOR)
                elif slot < GU0:
                    b = unit_bank(slot, s)
                    take(b, *last_read(l, slot, s))
                    order = [6, 7, 0, 1, 2, 3, 4, 5]
                    for c in range(2):
                        for i, k in enumerate(order):
                            between(KT * c + i)
                            if slot == OUT0 and c == 0 and i % 2 == 0:
                                pe.wait_ge((pool_y, conv_y, ret_y, moba_y)[i // 2], hs(l, s))
                            cols = slice(P * c, P * (c + 1))
                            last = split3(b256(b)[:, c, :], [w[0][:, k, cols], w[1][:, k, cols]],
                                          [ycat[:, 0, k, half(s)], ycat[:, 1, k, half(s)]],
                                          i == 0, i == KT - 1, True)
                elif slot < DN0:
                    f = slot - GU0
                    dst = gu_tiles(f, halves)
                    for b in ([unit_bank(slot, s)] if len(halves) == 1 else [2 * (f % 2), 2 * (f % 2) + 1]):
                        take(b, *last_read(l, slot, s))
                    for c in range(2):
                        for k in range(KT):
                            between(KT * c + k)
                            if pre and c == 0:
                                pe.wait_ge(h_lo, KT * pre_no(pre, l, s) + k + 1)
                            cols = slice(P * c, P * (c + 1))
                            last = split3(dst[c], [w[0][:, k, cols], w[1][:, k, cols]],
                                          [hT[:, 0, k, span(halves)], hT[:, 1, k, span(halves)]],
                                          k == 0, k == KT - 1, True)
                else:
                    final = slot == SLOTS - 1
                    parts = [(m, c) for m in range(KT) for c in range(2)] if final else \
                        [(m, c) for c in range(2) for m in range(KT)]
                    for i, (m, c) in enumerate(parts):
                        between(i)
                        f, b = 2 * (slot - DN0) + c, 4 * s + m // 2
                        if i % KT == 0 or (final and i == 1):
                            pe.wait_ge(f_lo, fno(l, f, s))
                        if f == 0 and m % 2 == 0:
                            take(b, y_sb, KT * post_no("fpost", l, s) + m + 2)
                        ms = slice(P * m, P * (m + 1))
                        last = split3(b256(b)[:, m % 2, :], [w[0][:, c, ms], w[1][:, c, ms]],
                                      [fT[:, 0, f, half(s)], fT[:, 1, f, half(s)]],
                                      f == 0 and m % 2 == 0, f == FT - 1 and m % 2 == 1, True,
                                      skip_group_check=True)
                        if final and i in (3, 7, 11):
                            last.then_inc(dn_bank, 1)
                last.then_inc(unit_done, 1)

            def norm_sum(kind, l, s):
                n, b = norm_no(kind, l, s), norm_bank(kind, l, s)
                take(b, xr_done, 4 * (n + 1))
                pe.wait_ge(ssq_done, n - 1)
                for t in range(2):
                    last = mm(bank[b][:, t:t + 1], sq[:, 0, tok(t)], ones, start=True, stop=True)
                last.then_inc(nsum_ps, 1)

            def norm_bcast(kind, l, s):
                n, b = norm_no(kind, l, s), norm_bank(kind, l, s)
                if n < 2:
                    take(b, xr_done, 4 * (n + 1))
                    pe.wait_ge(idents_in, 16)
                pe.wait_ge(rs_done, n + 1)
                for t in range(2):
                    last = mm(bank[b][:, HALF + P * t:HALF + P * (t + 1)],
                              rsy[:, 8 + t:9 + t].to_broadcast([P, P]),
                              ident_y if kind in ("post", "fpost") else ident_x, start=True, stop=True)
                last.then_inc(rstd_ps, 1)

            def rows_of(h):
                return slice(HD * (h % 2), HD * (h % 2) + HD)

            def ret_T(l, t):
                pe.wait_ge(rot_done, 2 * hs(l, t // 2))
                take(4, retT_sb, ts(l, t))
                for q in range(2):
                    for c in range(2):
                        last = transpose(b128(4)[:, 2 * q + c, :], qk[:, q, t % 2, P * c:P * (c + 1)])
                last.then_inc(retT_ps, 1)

            def ret_S(l, t):
                pe.wait_ge(retT_sb, ts(l, t))
                take(6, retS_sb, 2 * ts(l, t) - 1)
                take(4, retS_sb, 2 * ts(l, t))
                for h in range(NH):
                    r = rows_of(h)
                    last = mm(b128((6, 4)[h % 2])[:, h // 2, :], rT[r, 2 + h // 2, :], rT[r, h // 2, :],
                              start=True, stop=True)
                last.then_inc(retS_ps, 1)

            def ret_O(l, t):
                pe.wait_ge(retS_sb, 2 * ts(l, t))
                pe.wait_ge(rv_sb, hs(l, t // 2))
                if t:
                    pe.wait_ge(state_sb, (NT - 1) * l + t)
                take(5, retO_sb, ts(l, t))
                o = bank[5][:, 0:NH * HD].rearrange("p (h e) -> p h e", h=NH)
                for c in range(2):
                    for h in (2 * c, 2 * c + 1):
                        last = mm(o[:, h, :], sm[:, h, :], rv[:, t, HD * h:HD * (h + 1)], start=h == 0,
                                  stop=t == 0 and h == NH - 1, skip_group_check=True)
                    if t:
                        last = mm(bank[5][:, P * c:P * (c + 1)], rT[:, c, :], state[:, c, :], start=False,
                                  stop=c == 1, skip_group_check=True)
                if t < NT - 1:
                    take(6, state_sb, (NT - 1) * l + t + 1)
                    for c in range(2):
                        pc = slice(P * c, P * (c + 1))
                        last = mm(b128(6)[:, c, :], qk[:, 1, t % 2, pc], rv[:, t, pc], start=True, stop=True)
                last.then_inc(retO_ps, 1)

            def to_channels(b, src, done):
                for c in range(2):
                    for t in range(2):
                        last = transpose(b256(b)[:, c, tok(t)], src[:, t, P * c:P * (c + 1)])
                last.then_inc(done, 1)

            def ret_Y(l, s):
                pe.wait_ge(retN_sb, 8 * hs(l, s))
                take(5, ret_z, 2 * hs(l, s))
                to_channels(5, osb, retY_ps)

            def conv_T(l, s):
                pe.wait_ge(conv_sb, hs(l, s))
                take(5, convN_sb, 2 * hs(l, s))
                for t in range(2):
                    for c in range(2):
                        last = transpose(b256(5)[:, t, P * c:P * (c + 1)], cacc[:, c, tok(t)])
                last.then_inc(convT_ps, 1)

            def conv_Y(l, s):
                pe.wait_ge(convN_sb, 2 * hs(l, s))
                take(5, conv_z, 2 * hs(l, s))
                to_channels(5, cn, convY_ps)

            def pool_Y(l, s):
                pe.wait_ge(pool_sb, hs(l, s))
                pe.wait_ge(maps_in, 16 * 4 * L)
                take(6, pool_y32, 2 * hs(l, s))
                for c in range(2):
                    last = mm(b256(6)[:, c, :], bd[:, l, c, :], pooled[:, c, :], start=True, stop=True)
                last.then_inc(poolY_ps, 1)

            def moba_T(l, t):
                pe.wait_ge(mrot, hs(l, t // 2))
                take(4, mkT_sb, ts(l, t))
                for q in range(2):
                    for c in range(2):
                        last = transpose(b128(4)[:, 2 * q + c, :], mqk[:, q, t % 2, P * c:P * (c + 1)])
                last.then_inc(mT_ps, 1)

            def moba_S(l, t, h):
                if h == 0:
                    pe.wait_ge(consts_in, 16)
                    pe.wait_ge(mqT_sb, ts(l, t))
                    pe.wait_ge(mkT_sb, ts(l, t))
                b, r = (4, 6)[h % 2], rows_of(h)
                take(b, mP, ths(l, t, h))
                q = mqT[r, t % 2, h // 2, :]
                mm(bank[b][:, tok(t)], ident16, neg16, start=True, stop=True)
                mm(bank[b][:, 0:P * (t + 1)], q, mkT[r, h // 2, 0:P * (t + 1)], start=False, stop=True,
                   skip_group_check=True).then_inc(mS_ps, 1)

            def moba_PT(l, t, h):
                pe.wait_ge(mP, ths(l, t, h))
                take(5, mPT_sb, ths(l, t, h))
                for j in range(t + 1):
                    last = transpose(b128(5)[:, j, :], pr[:, h % 2, tok(j)])
                last.then_inc(mPT_ps, 1)

            def moba_O(l, t, h):
                if h == 0:
                    take(7, mO_sb, ts(l, t))
                    pe.wait_ge(mv_sb, hs(l, t // 2))
                pe.wait_ge(mPT_sb, ths(l, t, h))
                for j in range(t + 1):
                    last = mm(bank[7][:, HD * h:HD * (h + 1)], pT[:, h % 2, j, :],
                              mv[:, j, HD * h:HD * (h + 1)], start=j == 0, stop=j == t)
                last.then_inc(mPV, 1)

            def moba_Y(l, s):
                pe.wait_ge(mO_sb, ts(l, 2 * s + 1))
                take(5, moba_y, hs(l, s))
                to_channels(5, mo, mY_ps)

            def moba_stage(l, s, k):
                def th_of(g, i):
                    return 2 * s + g // 2, 2 * (g % 2) + i
                if 1 <= k <= 4:
                    moba_PT(l, *th_of(k - 1, 0))
                if k <= 3:
                    moba_S(l, *th_of(k, 0))
                    moba_S(l, *th_of(k, 1))
                if k >= 2:
                    moba_O(l, *th_of(k - 2, 0))
                    moba_O(l, *th_of(k - 2, 1))
                if 1 <= k <= 4:
                    moba_PT(l, *th_of(k - 1, 1))

            def x_in_T(s):
                for t in range(2):
                    pe.wait_ge(x_in[2 * s + t], 16)
                    for c, b in enumerate(X_BANKS[s]):
                        if t == 0:
                            take(b, xt_sb, 4 * s + c + 1)
                        for k in range(2):
                            last = transpose(b256(b)[:, k, tok(t)],
                                             xin[:, 2 * s + t, P * (2 * c + k):P * (2 * c + k + 1)])
                        if t:
                            last.then_inc(xt_ps, 1)

            def x_out_T(s):
                for i in range(2):
                    pe.wait_ge(x_upd, 4 * post_no("fpost", L - 1, s) + 2 * (i + 1))
                    for t in range(2):
                        b = 2 * i + t
                        take(b, xo_sb, 4 * s + 2 * i + t + 1)
                        for k in range(4):
                            last = transpose(b128(b)[:, k, :], xT[:, 4 * i + k, tok(2 * s + t)])
                        last.then_inc(xo_ps, 1)

            def small_products(l, at):
                for s in range(2):
                    if l and s and at == AT["fpost_sum", s]: norm_sum("fpost", l - 1, s)
                    if l and s and at == AT["fpost_bcast", s]: norm_bcast("fpost", l - 1, s)
                    if l and s and at == AT["pre_sum", s]: norm_sum("pre", l, s)
                    if s and at == AT["pre_bcast" if l else "first_bcast", s]: norm_bcast("pre", l, s)
                    for i in range(2):
                        t = 2 * s + i
                        if at == AT["ret_T", t]: ret_T(l, t)
                        if at == AT["ret_S", t]: ret_S(l, t)
                        if at == AT["ret_O", t]: ret_O(l, t)
                    if at == AT["ret_Y", s]: ret_Y(l, s)
                    if at == AT["conv_T", s]: conv_T(l, s)
                    if at == AT["conv_Y", s]: conv_Y(l, s)
                    if at == AT["pool_Y", s]: pool_Y(l, s)
                    for i in range(2):
                        if at == AT["moba_T", 2 * s + i]: moba_T(l, 2 * s + i)
                    for k in range(6):
                        if at == AT["moba_stage", 6 * s + k]: moba_stage(l, s, k)
                    if at == AT["moba_Y", s]: moba_Y(l, s)
                    for kind in ("post", "fpre"):
                        if at == AT[kind + "_sum", s]: norm_sum(kind, l, s)
                        if at == AT[kind + "_bcast", s]: norm_bcast(kind, l, s)
                if at == AT["fpost_sum", 0]: norm_sum("fpost", l, 0)
                if at == AT["fpost_bcast", 0]: norm_bcast("fpost", l, 0)
                if at == AT["pre_sum", 0] and l < L - 1: norm_sum("pre", l + 1, 0)
                if at == AT["pre_bcast", 0] and l < L - 1: norm_bcast("pre", l + 1, 0)
                if at == AT["x_out_T", 0] and l == L - 1: x_out_T(0)

            pe.wait_ge(ident_in, 16)
            x_in_T(0)
            norm_bcast("pre", 0, 0)
            x_in_T(1)
            for l in range(L):
                for i, (slot, halves) in enumerate(UNITS):
                    unit(l, slot, halves, lambda part: small_products(l, 16 * i + part))
            norm_sum("fpost", L - 1, 1)
            norm_bcast("fpost", L - 1, 1)
            x_out_T(1)

        @block.scalar
        def _(act):
            A = nc.scalar.activation

            def copy(dst, src, scale=1.0):
                return A(dst, src, ACT.Copy, scale=scale)

            def squares_of_input(s):
                for t in range(2):
                    act.wait_ge(x_in[2 * s + t], 16)
                    A(xsq, xin[:, 2 * s + t, :], ACT.Square, accum_out=rsx[:, 8 + t:9 + t]).then_inc(x_sq, 1)
                    act.wait_ge(x_sq, 2 * s + t + 1)

            def squares_of_x(kind, l, s):
                n = norm_no(kind, l, s)
                if n > 2:
                    act.wait_ge(nsum_ps, n - 2)
                upd = post_no("post" if kind == "fpre" else "fpost", l if kind == "fpre" else l - 1, s)
                for c in range(4):
                    act.wait_ge(x_upd, 4 * upd + c + 1)
                    A(sq[:, 2 * c:2 * c + 2, :], xT[:, 2 * c:2 * c + 2, half(s)],
                      ACT.Square).then_inc(sq_done, 1)

            def squares_of_y(kind, l, s):
                n = norm_no(kind, l, s)
                if n > 2:
                    act.wait_ge(nsum_ps, n - 2)
                if kind == "post":
                    act.wait_ge(poolY_ps, hs(l, 1))
                    act.wait_ge((retO_ps, mPV)[s], (ts(l, 3), ths(l, 3, 3))[s])
                else:
                    act.wait_ge(h_lo, KT * (pre_no("fpre", l, s) + 1))
                for c in range(4):
                    if kind == "post":
                        act.wait_ge(unit_done, unit_no(l, OUT0 + c, s))
                        b = unit_bank(OUT0 + c, s)
                    else:
                        b = 4 * s + c
                        if c < 3:
                            act.wait_ge(dn_bank, 3 * (2 * l + s) + c + 1)
                        else:
                            act.wait_ge(unit_done, unit_no(l, SLOTS - 1, s))
                    A(sq[:, 2 * c:2 * c + 2, :], b256(b), ACT.Square, scale=UNSCALE).then_inc(sq_done, 1)
                    for i in range(2):
                        k = 2 * c + i
                        copy(yT[:, s, k, :], b256(b)[:, i, :], par_col(l, kind, k)).then_inc(y_sb, 1)

            def h_split_hi(kind, l, s):
                n = norm_no(kind, l, s)
                if kind == "fpre":
                    act.wait_ge(unit_done, unit_no(l, RG, s))
                elif l:
                    act.wait_ge(unit_done, unit_no(l - 1, GU0 + N_GU - 1, s))
                for k in range(KT):
                    act.wait_ge(xr_done, 4 * n + k // 2 + 1)
                    copy(hT[:, 0, k, half(s)], yT[:, s, k, :], gain(kind, l, k)).then_inc(h_hi, 1)

            def hi_of(src, ready, kt, l, s, scale, done):
                act.wait_ge(ready, hs(l, s) * (2 if ready is pool_y32 else 1))
                copy(ycat[:, 0, kt:kt + 2, half(s)], src, scale).then_inc(done, 1)

            def glu_tanh(l, s):
                act.wait_ge(unit_done, unit_no(l, CONV_G, s))
                if l or s:
                    act.wait_ge(hb_sb, hs(l, s) - 1)
                if l and s == 0:
                    act.wait_ge(ret_g, 2 * l)
                A(th, b256(unit_bank(CONV_G, s)), ACT.Tanh, scale=0.5 * UNSCALE).then_inc(glu_th, 1)

            def rg_tanh(l, s):
                act.wait_ge(unit_done, unit_no(l, RG, s))
                act.wait_ge(hb_sb, hs(l, 1))
                act.wait_ge(conv_y32, hs(l, s))
                if s:
                    act.wait_ge(ret_g, hs(l, 0))
                A(th, b256(unit_bank(RG, s)), ACT.Tanh, scale=0.5 * UNSCALE).then_inc(rg_th, 1)

            def affine(dst, src, scale, bias):
                return A(dst, src, ACT.Identity, scale=scale, bias=bias)

            def conv_scale(l, s):
                act.wait_ge(conv_rs, hs(l, s))
                if hs(l, s) > 1:
                    act.wait_ge(convY_ps, hs(l, s) - 1)
                for t in range(2):
                    affine(cn[:, t, :], b256(5)[:, t, :], rsy[:, t:t + 1], nmr[:, t:t + 1]).then_inc(convN_sb, 1)

            def ret_scale(l, s):
                act.wait_ge(ret_rs, hs(l, s))
                for i in range(8):
                    o = osb[:, i // NH, HD * (i % NH):HD * (i % NH + 1)]
                    affine(o, o, rsy[:, i:i + 1], nmr[:, i:i + 1]).then_inc(retN_sb, 1)

            def ret_affine(l, s):
                act.wait_ge(retY_ps, hs(l, s))
                if hs(l, s) > 1:
                    act.wait_ge(ret_y32, hs(l, s) - 1)
                for c in range(2):
                    affine(rz[:, c, :], b256(5)[:, c, :], px(l, "gng", c), par_col(l, "gnb", c)).then_inc(ret_z, 1)

            def pool_affine(l, s):
                act.wait_ge(poolY_ps, hs(l, s))
                act.wait_ge(conv_y, hs(l, s))
                for c in range(2):
                    affine(ybuf[:, c, :], b256(6)[:, c, :], par_col(l, "ps", c),
                           px(l, "pbs", c)).then_inc(pool_y32, 1)

            def conv_affine(l, s):
                act.wait_ge(convY_ps, hs(l, s))
                act.wait_ge(hb_sb, hs(l, 1))
                if s:
                    act.wait_ge(ret_g, hs(l, 0))
                if l or s:
                    act.wait_ge(ret_y, hs(l, s) - 1)
                for c in range(2):
                    A(th[:, c, :], b256(5)[:, c, :], ACT.Tanh, scale=px(l, "lng_half", c),
                      bias=px(l, "lnb_half", c)).then_inc(conv_th, 1)
                for c in range(2):
                    affine(ybuf[:, c, :], b256(5)[:, c, :], px(l, "lng", c),
                           par_col(l, "lnb", c)).then_inc(conv_z, 1)

            def from_unit(l, slot, s, dst, done):
                act.wait_ge(unit_done, unit_no(l, slot, s))
                copy(dst, b256(unit_bank(slot, s)), UNSCALE).then_inc(done, 1)

            def ret_T_copy(l, t):
                act.wait_ge(retT_ps, ts(l, t))
                if l or t:
                    act.wait_ge(retO_ps, ts(l, t) - 1)
                copy(rT, b128(4)).then_inc(retT_sb, 1)

            def ret_O_copy(l, t):
                act.wait_ge(retO_ps, ts(l, t))
                if hs(l, t // 2) > 1:
                    act.wait_ge(retY_ps, hs(l, t // 2) - 1)
                copy(osb[:, t % 2, :], bank[5][:, 0:G]).then_inc(retO_sb, 1)

            def moba_in(l, s, q):
                slot, done = ((MQ, mq_sb), (MK, mk_sb))[q]
                act.wait_ge(unit_done, unit_no(l, slot, s))
                if l or s:
                    act.wait_ge(mT_ps, ts(l, 2 * s) - 1)
                copy(mqk[:, q, :, :], b256(unit_bank(slot, s)),
                     UNSCALE * (HD ** -0.5 if q == 0 else 1.0)).then_inc(done, 1)

            def m_T_copy(l, t):
                act.wait_ge(mT_ps, ts(l, t))
                if ts(l, t) > 2:
                    act.wait_ge(mS_ps, ths(l, t, 3) - 2 * NH)
                if l:
                    act.wait_ge(mS_ps, ths(l - 1, NT - 1, NH - 1))
                copy(mqT[:, t % 2, :, :], b128(4)[:, 0:2, :]).then_inc(mqT_sb, 1)
                copy(mkT[:, :, tok(t)], b128(4)[:, 2:4, :]).then_inc(mkT_sb, 1)

            def m_exp(l, t, h):
                i = ths(l, t, h)
                act.wait_ge(mM, i)
                if i > 2:
                    act.wait_ge(mPT_ps, i - 2)
                if ts(l, t) > 2:
                    act.wait_ge(mO_sb, ts(l, t) - 2)
                c = (i - 1) % 8
                w = P * (t + 1)
                A(pr[:, h % 2, 0:w], bank[(4, 6)[h % 2]][:, 0:w], ACT.Exp, bias=nms[:, c:c + 1],
                  accum_out=sums[:, c:c + 1]).then_inc(mP, 1)

            def m_PT_copy(l, t, h):
                i = ths(l, t, h)
                act.wait_ge(mPT_ps, i)
                if i > 2:
                    act.wait_ge(mPV, i - 2)
                copy(pT[:, h % 2, 0:t + 1, :], b128(5)[:, 0:t + 1, :]).then_inc(mPT_sb, 1)

            def m_stage(l, s, k):
                def th_of(g, i):
                    return 2 * s + g // 2, 2 * (g % 2) + i
                if 1 <= k <= 4:
                    m_PT_copy(l, *th_of(k - 1, 0))
                if k <= 3:
                    m_exp(l, *th_of(k, 0))
                    m_exp(l, *th_of(k, 1))
                if 1 <= k <= 4:
                    m_PT_copy(l, *th_of(k - 1, 1))

            def silu(l, f, halves):
                n = fno(l, f, halves[0])
                act.wait_ge(unit_done, unit_no(l, GU0 + f, halves[0]))
                if n > 2:
                    act.wait_ge(f_sb, n - 2)
                A(sil[:, n % 2, 0:HALF * len(halves)], gu_tiles(f, halves)[0], ACT.Silu,
                  scale=UNSCALE).then_inc(sil_done, 1)

            def hidden_hi(l, f, halves):
                n = fno(l, f, halves[0])
                act.wait_ge(f_sb, n)
                copy(fT[:, 0, f, span(halves)], fbuf[:, n % 2, 0:HALF * len(halves)]).then_inc(f_hi, 1)

            def hidden_steps(l, i0, i1):
                for i in range(i0, i1):
                    silu(l, *HIDDEN[i])
                    if i:
                        hidden_hi(l, *HIDDEN[i - 1])

            def x_copy(s):
                for c, b in enumerate(X_BANKS[s]):
                    act.wait_ge(xt_ps, 4 * s + c + 1)
                    copy(xT[:, 2 * c:2 * c + 2, half(s)], b256(b)).then_inc(xt_sb, 1)

            squares_of_input(0)
            x_copy(0)
            act.wait_ge(setup_done, SCALED + L)
            h_split_hi("pre", 0, 0)
            act.wait_ge(rs_done, 1)
            squares_of_input(1)
            x_copy(1)
            for l in range(L):
                if l:
                    squares_of_y("fpost", l - 1, 1)
                    glu_tanh(l, 0)
                    squares_of_x("pre", l, 1)
                else:
                    glu_tanh(l, 0)
                h_split_hi("pre", l, 1)
                from_unit(l, RV, 0, rv[:, 0:2, :], rv_sb)
                ret_T_copy(l, 0)
                ret_O_copy(l, 0)
                ret_T_copy(l, 1)
                ret_O_copy(l, 1)
                from_unit(l, POOL, 0, ubuf[:, :, 16:16 + HALF], pool_u)
                ret_scale(l, 0)
                glu_tanh(l, 1)
                ret_T_copy(l, 2)
                ret_affine(l, 0)
                from_unit(l, RV, 1, rv[:, 2:4, :], rv_sb)
                ret_O_copy(l, 2)
                from_unit(l, POOL, 1, ubuf[:, :, 16 + HALF:16 + S], pool_u)
                ret_T_copy(l, 3)
                ret_O_copy(l, 3)
                conv_scale(l, 0)
                conv_affine(l, 0)
                hi_of(ybuf, conv_y32, 0, l, 0, 0.5 * A_SCALE, conv_hi)
                moba_in(l, 0, 0)
                moba_in(l, 0, 1)
                pool_affine(l, 0)
                hi_of(ybuf, pool_y32, 6, l, 0, A_SCALE, pool_hi)
                m_T_copy(l, 0)
                m_T_copy(l, 1)
                from_unit(l, MV, 0, mv[:, 0:2, :], mv_sb)
                m_stage(l, 0, 0)
                rg_tanh(l, 0)
                m_stage(l, 0, 1)
                moba_in(l, 1, 0)
                hi_of(ybuf, ret_y32, 2, l, 0, 0.5 * A_SCALE * UNSCALE, ret_hi)
                m_stage(l, 0, 2)
                m_stage(l, 0, 3)
                moba_in(l, 1, 1)
                m_stage(l, 0, 4)
                m_T_copy(l, 2)
                m_T_copy(l, 3)
                from_unit(l, MV, 1, mv[:, 2:4, :], mv_sb)
                hi_of(b256(5), mY_ps, 4, l, 0, A_SCALE, moba_hi)
                ret_scale(l, 1)
                m_stage(l, 1, 0)
                m_stage(l, 1, 1)
                ret_affine(l, 1)
                conv_scale(l, 1)
                m_stage(l, 1, 2)
                m_stage(l, 1, 3)
                conv_affine(l, 1)
                hi_of(ybuf, conv_y32, 0, l, 1, 0.5 * A_SCALE, conv_hi)
                rg_tanh(l, 1)
                m_stage(l, 1, 4)
                pool_affine(l, 1)
                hi_of(ybuf, pool_y32, 6, l, 1, A_SCALE, pool_hi)
                hi_of(ybuf, ret_y32, 2, l, 1, 0.5 * A_SCALE * UNSCALE, ret_hi)
                hi_of(b256(5), mY_ps, 4, l, 1, A_SCALE, moba_hi)
                for s in range(2):
                    squares_of_y("post", l, s)
                    squares_of_x("fpre", l, s)
                    if s:
                        hidden_steps(l, 0, GU_EARLY)
                    h_split_hi("fpre", l, s)
                hidden_steps(l, GU_EARLY, len(HIDDEN))
                hidden_hi(l, *HIDDEN[-1])
                squares_of_y("fpost", l, 0)
                if l + 1 < L:
                    squares_of_x("pre", l + 1, 0)
                    h_split_hi("pre", l + 1, 0)
            for s in range(2):
                if s:
                    squares_of_y("fpost", L - 1, 1)
                for i in range(2):
                    for t in range(2):
                        act.wait_ge(xo_ps, 4 * s + 2 * i + t + 1)
                        copy(xout[:, 2 * s + t, 4 * P * i:4 * P * (i + 1)],
                             bank[2 * i + t][:, :]).then_inc(xo_sb, 1)

        @block.vector
        def _(dve):
            V = nc.vector
            ticks = [0]

            def tick(ins):
                ins.then_inc(dve_tick, 1)
                ticks[0] += 1
                return ticks[0]

            def after(n=None):
                dve.wait_ge(dve_tick, ticks[0] if n is None else n)

            def rsqrt(cols, fill=None):
                xx, tt, yy = rsx[:, cols], rst[:, cols], rsy[:, cols]
                after()
                tick(V.tensor_scalar(yy.bitcast(I32), xx.bitcast(I32), -0.5, RSQRT_MAGIC, ALU.mult, ALU.add))
                for step, c in enumerate((-3.0, -12.0, -768.0)):
                    n = ticks[0]
                    if fill:
                        fill()
                    after(n)
                    if cols.stop - cols.start == 2:
                        for i in (cols.start, cols.start + 1):
                            n = tick(V.tensor_scalar(rst[:, i:i + 1], rsy[:, i:i + 1], rsy[:, i:i + 1],
                                                     rsx[:, i:i + 1], ALU.mult, ALU.mult))
                    else:
                        n = tick(V.tensor_tensor(tt, yy, yy, ALU.mult))
                        if fill:
                            fill()
                        after(n)
                        n = tick(V.tensor_tensor(tt, tt, xx, ALU.mult))
                    if fill:
                        fill()
                    after(n)
                    ins = V.scalar_tensor_tensor(out=yy, in0=tt, scalar=c, in1=yy, op0=ALU.add, op1=ALU.mult)
                    if step < 2:
                        tick(ins)
                return ins

            def split_lo(slot):
                if slot >= L * SLOTS:
                    return
                assert dve_splits(slot)
                for part in range(PARTS):
                    n = PARTS * slot + part
                    dve.wait_ge(hi_split, n + 1)
                    V.scalar_tensor_tensor(out=ring[:, slot % RING, 1, raw_part(part)], in0=raw[:, n % NRAW, :],
                                           scalar=W_SCALE, in1=ring[:, slot % RING, 0, raw_part(part)],
                                           op0=ALU.mult, op1=ALU.subtract).then_inc(lo_dve, 1)

            def norm_reduce(kind, l, s):
                n = norm_no(kind, l, s)
                for c in range(1, 4):
                    dve.wait_ge(sq_done, 4 * (n - 2) + c + 1)
                    if c > 1:
                        after()
                    tick(V.tensor_tensor(sq[:, 0:2, :], sq[:, 0:2, :], sq[:, 2 * c:2 * c + 2, :], ALU.add))
                after()
                V.tensor_tensor(sq[:, 0, :], sq[:, 0, :], sq[:, 1, :], ALU.add).then_inc(ssq_done, 1)

            def norm_rsqrt(kind, l, s):
                n, b = norm_no(kind, l, s), norm_bank(kind, l, s)
                if n:
                    dve.wait_ge(rstd_ps, n)
                if n < 2:
                    dve.wait_ge(x_sq, 2 * (n + 1))
                    src = rsx[:, 8:10]
                else:
                    dve.wait_ge(nsum_ps, n - 1)
                    src = bank[b][:, 0:2]
                tick(V.tensor_scalar(rsx[:, 8:10], src, 1.0 / DM, 1e-6, ALU.mult, ALU.add))
                rsqrt(slice(8, 10)).then_inc(rs_done, 1)

            def norm_scale(kind, l, s, c):
                n, b = norm_no(kind, l, s), norm_bank(kind, l, s)
                k2 = slice(2 * c, 2 * c + 2)
                dst = yT[:, s, k2, :]
                if c == 0:
                    dve.wait_ge(rstd_ps, n + 1)
                if kind in ("pre", "fpre"):
                    src = xT[:, k2, half(s)]
                    if n < 2:
                        dve.wait_ge(xt_sb, 4 * s + 4)
                        dve.wait_ge(x_sq, 2 * s + 2)
                else:
                    src = dst
                    dve.wait_ge(y_sb, KT * post_no(kind, l, s) + 2 * c + 2)
                V.tensor_tensor(dst, src, bank[b][:, HALF:2 * HALF].unsqueeze(1).to_broadcast([P, 2, HALF]),
                                ALU.mult).then_inc(xr_done, 1)

            def residual(kind, l, s):
                n = norm_no(kind, l, s)
                for c in range(5):
                    if c < 4:
                        norm_scale(kind, l, s, c)
                    if c:
                        dve.wait_ge(xr_done, 4 * n + c)
                        k2 = slice(2 * c - 2, 2 * c)
                        V.tensor_tensor(xT[:, k2, half(s)], xT[:, k2, half(s)], yT[:, s, k2, :],
                                        ALU.add).then_inc(x_upd, 1)

            def h_split(kind, l, s):
                m = pre_no(kind, l, s)
                for c in range(6):
                    if c < 4:
                        norm_scale(kind, l, s, c)
                    if c > 1:
                        for k in (2 * c - 4, 2 * c - 3):
                            dve.wait_ge(h_hi, KT * m + k + 1)
                            V.scalar_tensor_tensor(out=hT[:, 1, k, half(s)], in0=yT[:, s, k, :],
                                                   scalar=gain(kind, l, k), in1=hT[:, 0, k, half(s)],
                                                   op0=ALU.mult, op1=ALU.subtract).then_inc(h_lo, 1)

            def lo_of(src, ready, kt, l, s, scale, done):
                dve.wait_ge(ready, hs(l, s))
                V.scalar_tensor_tensor(out=ycat[:, 1, kt:kt + 2, half(s)], in0=src, scalar=scale,
                                       in1=ycat[:, 0, kt:kt + 2, half(s)], op0=ALU.mult,
                                       op1=ALU.subtract).then_inc(done, 1)

            def glu(l, s):
                dve.wait_ge(unit_done, unit_no(l, CONV_A, s))
                dve.wait_ge(glu_th, hs(l, s))
                at = CW - 1 + HALF * s
                V.scalar_tensor_tensor(out=hbuf[:, :, at:at + HALF], in0=th, scalar=1.0,
                                       in1=b256(unit_bank(CONV_A, s)), op0=ALU.add,
                                       op1=ALU.mult).then_inc(hb_sb, 1)

            tap_tick = [0, 0]
            taps_done = {}

            def conv(l, s, n):
                if (l, s) not in taps_done:
                    taps_done[(l, s)] = 0
                    dve.wait_ge(hb_sb, hs(l, s))
                    if hs(l, s) > 1:
                        dve.wait_ge(convT_ps, hs(l, s) - 1)
                for i in range(taps_done[(l, s)], min(taps_done[(l, s)] + n, 2 * CW)):
                    k, c = i // 2, i % 2
                    src = hbuf[:, c, HALF * s + k:HALF * s + k + HALF]
                    w = px(l, "cw", 2 * k + c)
                    if k == 0:
                        ins = V.tensor_scalar(cacc[:, c, :], src, w, par_col(l, "cb", c), ALU.mult, ALU.add)
                    else:
                        after(tap_tick[c])
                        ins = V.scalar_tensor_tensor(out=cacc[:, c, :], in0=src, scalar=w,
                                                     in1=cacc[:, c, :], op0=ALU.mult, op1=ALU.add)
                    if i == 2 * CW - 1:
                        ins.then_inc(conv_sb, 1)
                    else:
                        tap_tick[c] = tick(ins)
                    taps_done[(l, s)] = i + 1

            def norm_rows_free(l, s, ret):
                if not ret:
                    dve.wait_ge(retN_sb, 8 * hs(l, s))
                elif l or s:
                    dve.wait_ge(convN_sb, 2 * hs(l, s) - 2)

            def conv_norm(l, s, fill=None):
                dve.wait_ge(convT_ps, hs(l, s))
                for t in range(2):
                    tick(V.bn_stats(cst_st[:, 6 * t:6 * t + 6], b256(5)[:, t, :]))
                after()
                for t in range(2):
                    tick(V.bn_aggr(cmv[:, 2 * t:2 * t + 2], cst_st[:, 6 * t:6 * t + 6]))
                after()
                norm_rows_free(l, s, 0)
                tick(V.tensor_scalar(rsx[:, 0:2], cmv.rearrange("p (t v) -> p t v", v=2)[:, :, 1], 1e-5, None,
                                     ALU.add))
                n = tick(rsqrt(slice(0, 2), fill))
                if fill:
                    fill()
                after(n)
                V.scalar_tensor_tensor(out=nmr[:, 0:2], in0=cmv.rearrange("p (t v) -> p t v", v=2)[:, :, 0],
                                       scalar=-1.0, in1=rsy[:, 0:2], op0=ALU.mult,
                                       op1=ALU.mult).then_inc(conv_rs, 1)

            def conv_out(l, s):
                dve.wait_ge(conv_th, 2 * hs(l, s))
                dve.wait_ge(conv_z, 2 * hs(l, s))
                V.scalar_tensor_tensor(out=ybuf, in0=th, scalar=1.0, in1=ybuf, op0=ALU.add,
                                       op1=ALU.mult).then_inc(conv_y32, 1)

            scratch_read = []

            def rotate(out_, u, cos, sin, n, w):
                ma = m1[:, 0:2 * n * w].rearrange("p (a h d) -> p a h d", a=n, h=2)
                mb = m2[:, 0:2 * n * w].rearrange("p (a h d) -> p a h d", a=n, h=2)
                for sem_, value in scratch_read:
                    dve.wait_ge(sem_, value)
                tick(V.tensor_tensor(ma, u, cos.unsqueeze(2).to_broadcast([P, n, 2, w]), ALU.mult))
                tick(V.scalar_tensor_tensor(out=mb[:, :, 0, :], in0=u[:, :, 1, :], scalar=-1.0, in1=sin,
                                            op0=ALU.mult, op1=ALU.mult))
                tick(V.tensor_tensor(mb[:, :, 1, :], u[:, :, 0, :], sin, ALU.mult))
                after()
                return V.tensor_tensor(out_, ma, mb, ALU.add)

            def table(name, s, w):
                n = 2 * NH * w
                return C(name)[:, s * n:(s + 1) * n].rearrange("p (a d) -> p a d", d=w)

            def ret_rotate(l, s, q):
                slot = (RQ, RK)[q]
                dve.wait_ge(unit_done, unit_no(l, slot, s))
                if l or s:
                    dve.wait_ge(retO_ps, ts(l, 2 * s) - 1)
                u = bank[unit_bank(slot, s)][:, :].rearrange("p (a h d) -> p a h d", h=2, d=32)
                dst = qk[:, q, :, :].rearrange("p t (a h d) -> p (t a) h d", h=2, d=32)
                rotate(dst, u, table(("rqc", "rkc")[q], s, 32), table(("rqs", "rks")[q], s, 32), 2 * NH,
                       32).then_inc(rot_done, 1)
                scratch_read[:] = [(rot_done, 2 * hs(l, s) - 1 + q)]

            def moba_rotate(l, s):
                dve.wait_ge(mq_sb, hs(l, s))
                dve.wait_ge(mk_sb, hs(l, s))
                for q in range(2):
                    u = mqk[:, q, :, :].rearrange("p t (a d) -> p (t a) d", d=HD)[:, :, 0:16].rearrange(
                        "p a (h d) -> p a h d", h=2)
                    ins = rotate(u, u, table("mc", s, 8), table("ms", s, 8), 2 * NH, 8)
                    if q == 0:
                        scratch_read[:] = [(dve_tick, tick(ins))]
                    else:
                        ins.then_inc(mrot, 1)
                        scratch_read[:] = [(mrot, hs(l, s))]

            def ret_mask(l, t):
                dve.wait_ge(retS_ps, ts(l, t))
                if l or t:
                    dve.wait_ge(retO_ps, ts(l, t) - 1)
                smv = sm.rearrange("p (c two) t -> p two c t", two=2)
                for e, b in ((0, 6), (1, 4)):
                    V.tensor_tensor(smv[:, e, :, :], b128(b)[:, 0:2, :],
                                    tri.unsqueeze(1).to_broadcast([P, 2, P]), ALU.mult).then_inc(retS_sb, 1)

            def ret_state(l, t):
                dve.wait_ge(retO_ps, ts(l, t))
                if t == 0:
                    after(zeroed[0])
                else:
                    dve.wait_ge(state_sb, (NT - 1) * l + t)
                for i in range(2):
                    r = slice(HD * i, HD * i + HD)
                    ins = V.tensor_tensor(state[r, :, r], state[r, :, r], b128(6)[r, 0:2, r], ALU.add)
                    if i == 0:
                        tick(ins)
                    else:
                        ins.then_inc(state_sb, 1)

            def ret_norm(l, s, fill=None):
                dve.wait_ge(retO_sb, ts(l, 2 * s + 1))
                for i in range(8):
                    o = osb[:, i // NH, HD * (i % NH):HD * (i % NH + 1)]
                    tick(V.bn_stats(bst[:, 6 * i:6 * i + 6], o))
                for i in range(8):
                    after(ticks[0] - 7)
                    tick(V.bn_aggr(mvr[:, 2 * i:2 * i + 2], bst[:, 6 * i:6 * i + 6]))
                after()
                norm_rows_free(l, s, 1)
                tick(V.tensor_scalar(rsx[:, 0:8], mvr.rearrange("p (i v) -> p i v", v=2)[:, :, 1], 1e-5, None,
                                     ALU.add))
                n = tick(rsqrt(slice(0, 8), fill))
                if fill:
                    fill()
                after(n)
                V.scalar_tensor_tensor(out=nmr, in0=mvr.rearrange("p (i v) -> p i v", v=2)[:, :, 0],
                                       scalar=-1.0, in1=rsy[:, 0:8], op0=ALU.mult,
                                       op1=ALU.mult).then_inc(ret_rs, 1)

            def ret_out(l, s):
                dve.wait_ge(rg_th, hs(l, s))
                dve.wait_ge(ret_z, 2 * hs(l, s))
                V.scalar_tensor_tensor(out=rz, in0=th, scalar=1.0, in1=rz, op0=ALU.add,
                                       op1=ALU.mult).then_inc(ret_g, 1)
                dve.wait_ge(ret_g, hs(l, s))
                dve.wait_ge(pool_y, hs(l, s))
                V.tensor_tensor(ybuf, rz, b256(unit_bank(RG, s)), ALU.mult).then_inc(ret_y32, 1)

            def pool_windows(l, s):
                dve.wait_ge(pool_u, hs(l, s))
                if hs(l, s) > 1:
                    dve.wait_ge(poolY_ps, hs(l, s) - 1)
                if s == 0:
                    after(zeroed[0])
                at = 16 + HALF * s
                tick(V.tensor_tensor(t2, ubuf[:, :, at - 14:at + HALF], ubuf[:, :, at - 15:at + HALF - 1],
                                     ALU.add))
                after()
                tick(V.tensor_tensor(t4, t2[:, :, 2:], t2[:, :, 0:HALF + 12], ALU.add))
                after()
                tick(V.tensor_tensor(t8, t4[:, 1, 4:], t4[:, 1, 0:HALF + 8], ALU.add))
                after()
                lo, hi_ = slice(0, HD), slice(HD, P)
                w16 = m1[:, 0:HALF]
                tick(V.tensor_tensor(w16[hi_, :], t8[hi_, 8:], t8[hi_, 0:HALF], ALU.add))
                after()
                sums_ = [(lo, 0, t2[lo, 0, 14:]), (hi_, 0, t4[hi_, 0, 12:]), (lo, 1, t8[lo, 8:]),
                         (hi_, 1, w16[hi_, :])]
                if s == 0:
                    for r, c, v in sums_:
                        tick(V.tensor_tensor(v[:, 0:16], v[:, 0:16], C("adj")[r, 16 * c:16 * c + 16], ALU.mult))
                    after()
                for i, (r, c, v) in enumerate(sums_):
                    ins = V.scalar_tensor_tensor(out=pooled[r, c, :], in0=v, scalar=1.0 / WINDOWS[i],
                                                 in1=ubuf[r, c, at:at + HALF], op0=ALU.mult, op1=ALU.subtract)
                    if i < 3:
                        tick(ins)
                    else:
                        ins.then_inc(pool_sb, 1)

            def m_max(l, t, h):
                i = ths(l, t, h)
                dve.wait_ge(mS_ps, i)
                if i > 8:
                    dve.wait_ge(mP, i - 8)
                c = (i - 1) % 8
                V.tensor_reduce(nms[:, c:c + 1], bank[(4, 6)[h % 2]][:, 0:P * (t + 1)], AX_X, ALU.max,
                                negate=True).then_inc(mM, 1)

            def m_norm(l, t):
                dve.wait_ge(mPV, ths(l, t, NH - 1))
                dve.wait_ge(mP, ths(l, t, NH - 1))
                c = NH * (t % 2)
                tick(V.reciprocal(rinv[:, c:c + NH], sums[:, c:c + NH]))
                after()
                if hs(l, t // 2) > 1:
                    dve.wait_ge(mY_ps, hs(l, t // 2) - 1)
                V.tensor_tensor(mo[:, t % 2, :].rearrange("p (h e) -> p h e", h=NH),
                                bank[7][:, 0:G].rearrange("p (h e) -> p h e", h=NH),
                                rinv[:, c:c + NH].unsqueeze(2).to_broadcast([P, NH, HD]),
                                ALU.mult).then_inc(mO_sb, 1)

            def hidden(l, f, halves):
                n, w = fno(l, f, halves[0]), HALF * len(halves)
                dve.wait_ge(sil_done, n)
                if n > 2:
                    dve.wait_ge(f_lo, n - 2)
                V.scalar_tensor_tensor(out=fbuf[:, n % 2, 0:w], in0=gu_tiles(f, halves)[1],
                                       scalar=UNSCALE * A_SCALE, in1=sil[:, n % 2, 0:w], op0=ALU.mult,
                                       op1=ALU.mult).then_inc(f_sb, 1)

            def hidden_lo(l, f, halves):
                n, w = fno(l, f, halves[0]), HALF * len(halves)
                dve.wait_ge(f_hi, n)
                V.tensor_tensor(fT[:, 1, f, span(halves)], fbuf[:, n % 2, 0:w], fT[:, 0, f, span(halves)],
                                ALU.subtract).then_inc(f_lo, 1)

            def hidden_steps(l, i0, i1):
                for i in range(i0, i1):
                    f, halves = HIDDEN[i]
                    hidden(l, f, halves)
                    if i:
                        hidden_lo(l, *HIDDEN[i - 1])
                    if 1 in halves:
                        split_lo(l * SLOTS + GU0 + f + RING)

            zeroed = [0]
            tick(V.memset(bd[:, :, :, :], 0.0))
            tick(V.memset(hbuf[:, :, 0:CW - 1], 0.0))
            norm_rsqrt("pre", 0, 0)
            split_lo(0)
            dve.wait_ge(setup_done, SCALED + L)
            h_split("pre", 0, 0)
            split_lo(1)
            norm_rsqrt("pre", 0, 1)
            split_lo(2)
            split_lo(3)
            for l in range(L):
                if l:
                    norm_reduce("fpost", l - 1, 1)
                    norm_rsqrt("fpost", l - 1, 1)
                    glu(l, 0)
                    residual("fpost", l - 1, 1)
                    norm_reduce("pre", l, 1)
                    norm_rsqrt("pre", l, 1)
                else:
                    glu(l, 0)
                    split_lo(4)
                    split_lo(5)
                    dve.wait_ge(consts_in, 16)
                ret_rotate(l, 0, 0)
                h_split("pre", l, 1)
                ret_rotate(l, 0, 1)
                dve.wait_ge(unit_done, unit_no(l, CONV_A, 0))
                tick(V.memset(state, 0.0))
                zeroed[0] = tick(V.memset(ubuf[:, :, 0:16], 0.0))
                conv(l, 0, 5)
                ret_mask(l, 0)
                conv(l, 0, 7)
                ret_state(l, 0)
                ret_mask(l, 1)
                conv(l, 0, 8)
                ret_state(l, 1)
                ret_norm(l, 0, lambda: conv(l, 0, 1))
                conv(l, 0, 10)
                glu(l, 1)
                ret_rotate(l, 1, 0)
                conv(l, 0, 8)
                ret_rotate(l, 1, 1)
                ret_mask(l, 2)
                conv(l, 0, 10)
                ret_state(l, 2)
                conv(l, 0, 4)
                ret_mask(l, 3)
                conv(l, 0, 2 * CW)
                conv_norm(l, 0, lambda: conv(l, 1, 1))
                pool_windows(l, 0)
                conv_out(l, 0)
                lo_of(ybuf, conv_hi, 0, l, 0, 0.5 * A_SCALE, conv_y)
                moba_rotate(l, 0)
                conv(l, 1, 2)
                lo_of(ybuf, pool_hi, 6, l, 0, A_SCALE, pool_y)
                conv(l, 1, 6)
                m_max(l, 0, 0)
                m_max(l, 0, 1)
                conv(l, 1, 14)
                m_max(l, 0, 2)
                m_max(l, 0, 3)
                conv(l, 1, 3)
                ret_out(l, 0)
                m_max(l, 1, 0)
                m_max(l, 1, 1)
                lo_of(ybuf, ret_hi, 2, l, 0, 0.5 * A_SCALE * UNSCALE, ret_y)
                conv(l, 1, 4)
                m_max(l, 1, 2)
                m_norm(l, 0)
                m_max(l, 1, 3)
                moba_rotate(l, 1)
                conv(l, 1, 8)
                m_norm(l, 1)
                ret_norm(l, 1, lambda: conv(l, 1, 1))
                lo_of(b256(5), moba_hi, 4, l, 0, A_SCALE, moba_y)
                conv(l, 1, 2)
                m_max(l, 2, 0)
                m_max(l, 2, 1)
                conv(l, 1, 2 * CW)
                m_max(l, 2, 2)
                m_max(l, 2, 3)
                conv_norm(l, 1)
                pool_windows(l, 1)
                m_max(l, 3, 0)
                m_max(l, 3, 1)
                m_max(l, 3, 2)
                m_max(l, 3, 3)
                m_norm(l, 2)
                conv_out(l, 1)
                lo_of(ybuf, conv_hi, 0, l, 1, 0.5 * A_SCALE, conv_y)
                lo_of(ybuf, pool_hi, 6, l, 1, A_SCALE, pool_y)
                ret_out(l, 1)
                m_norm(l, 3)
                lo_of(ybuf, ret_hi, 2, l, 1, 0.5 * A_SCALE * UNSCALE, ret_y)
                lo_of(b256(5), moba_hi, 4, l, 1, A_SCALE, moba_y)
                for s in range(2):
                    norm_reduce("post", l, s)
                    norm_rsqrt("post", l, s)
                    residual("post", l, s)
                    norm_reduce("fpre", l, s)
                    if s:
                        hidden_steps(l, 0, GU_EARLY)
                    norm_rsqrt("fpre", l, s)
                    h_split("fpre", l, s)
                hidden_steps(l, GU_EARLY, len(HIDDEN))
                hidden_lo(l, *HIDDEN[-1])
                for c in range(N_DN - DN_TAIL):
                    split_lo(l * SLOTS + DN0 + c + RING)
                norm_reduce("fpost", l, 0)
                norm_rsqrt("fpost", l, 0)
                residual("fpost", l, 0)
                if l + 1 < L:
                    norm_reduce("pre", l + 1, 0)
                    norm_rsqrt("pre", l + 1, 0)
                    h_split("pre", l + 1, 0)
            norm_reduce("fpost", L - 1, 1)
            norm_rsqrt("fpost", L - 1, 1)
            residual("fpost", L - 1, 1)


def rotary_table(dim, theta, np):
    inv = 1.0 / (theta ** (np.arange(0, dim, 2, dtype=np.float32) / np.float32(dim)))
    ang = (np.arange(S, dtype=np.float32)[:, None] * inv[None, :].astype(np.float32)).astype(np.float32)
    return np.cos(ang), np.sin(ang)


def constants():
    import numpy as np
    c = np.zeros((P, CST_COLS), np.float32)

    def put(name, a):
        c[:, CST[name]:CST[name] + a.shape[1]] = a

    i = np.arange(P)
    put("ident", np.eye(P))
    put("ident_x", np.eye(P) / RS)
    put("ident_y", np.eye(P) * UNSCALE / RS)
    put("ones", np.ones((P, 1)))
    put("tri", (i[:, None] <= i[None, :]))

    def as_bfloat16(a):
        return (a.astype(np.float32).view(np.uint32) >> 16).astype(np.uint16).view(np.float32)

    put("ident16", as_bfloat16(np.eye(P)))
    put("neg16", as_bfloat16(np.where(i[None, :] > i[:, None], -1e30, 0.0)))
    pos = np.arange(S, dtype=np.float64)
    gamma = 1.0 - 2.0 ** (-5.0 - np.arange(NH))
    grow = gamma[None, :] ** (pos[:, None] + 1.0)
    cos, sin = rotary_table(HD, 10000.0, np)

    def tiles(a):
        return a.reshape(NT, P, -1).transpose(1, 0, 2).reshape(P, -1)

    for name, trig, decay in (("rqc", cos, grow * UNSCALE), ("rqs", sin, grow * UNSCALE),
                              ("rkc", cos, UNSCALE * HD ** -0.5 / grow),
                              ("rks", sin, UNSCALE * HD ** -0.5 / grow)):
        put(name, tiles(trig[:, None, :] * decay[:, :, None]))
    mcos, msin = rotary_table(HD // 4, 500000.0, np)
    for name, trig in (("mc", mcos), ("ms", msin)):
        put(name, tiles(np.repeat(trig[:, None, :], NH, axis=1)))
    adj = np.ones((P, 2, 16))
    for g, w in enumerate(WINDOWS):
        rows = slice(HD * (g % 2), HD * (g % 2) + HD)
        adj[rows, g // 2, :] = w / np.minimum(np.arange(16) + 1.0, w)
    put("adj", adj.reshape(P, 32))
    return c


def kernel(x, attn_pre_g, w_in, conv_w, conv_b, conv_ln_g, conv_ln_b, ret_gn_g, ret_gn_b, pool_w, pool_b,
           pool_scale, w_out, attn_post_g, ffn_pre_g, w_gate, w_up, w_down, ffn_post_g):
    import numpy as np
    import concourse.bacc as bacc
    from concourse.bass_utils import run_bass_kernel_spmd

    w_in, w_out, w_gate, w_up, w_down = map(np.asarray, (w_in, w_out, w_gate, w_up, w_down))
    weights = np.empty((L, SLOTS, P, SLOT), np.float32)
    by_col = w_in.reshape(L, KT, P, N_IN, G)
    for slot, blk in BLOCK_OF.items():
        weights[:, slot] = by_col[:, :, :, blk].transpose(0, 2, 1, 3).reshape(L, P, SLOT)
    weights[:, OUT0:GU0] = w_out.reshape(L, KT, P, N_OUT, 2 * P).transpose(0, 3, 2, 1, 4).reshape(
        L, N_OUT, P, SLOT)
    gu = np.stack([w_gate.reshape(L, KT, P, FT, P), w_up.reshape(L, KT, P, FT, P)], axis=4)
    weights[:, GU0:DN0] = gu.transpose(0, 3, 2, 1, 4, 5).reshape(L, N_GU, P, SLOT)
    weights[:, DN0:] = w_down.reshape(L, N_DN, 2, P, DM).transpose(0, 1, 3, 2, 4).reshape(L, N_DN, P, SLOT)

    weights = np.ascontiguousarray(weights.reshape(L * SLOTS, P, PARTS, RAW).transpose(0, 2, 1, 3)).reshape(
        L * SLOTS * PARTS, P, RAW)

    params = np.empty((P, L, PAR_COLS), np.float32)
    for name, a in (("pre", attn_pre_g), ("post", attn_post_g), ("fpre", ffn_pre_g), ("fpost", ffn_post_g),
                    ("cw", conv_w), ("cb", conv_b), ("lng", conv_ln_g), ("lnb", conv_ln_b),
                    ("gng", ret_gn_g), ("gnb", ret_gn_b), ("pb", pool_b), ("ps", pool_scale)):
        a = np.asarray(a).reshape(L, -1, P)
        params[:, :, PAR[name]:PAR[name] + a.shape[1]] = a.transpose(2, 0, 1)

    arrays = {"x": np.ascontiguousarray(np.asarray(x).reshape(S, DM)),
              "weights": weights, "params": params,
              "pool_w": np.ascontiguousarray(pool_w), "consts": constants()}
    nc = bacc.Bacc("TRN2", target_bir_lowering=False, num_devices=1)
    aps = [nc.dram_tensor(f"{n}_dram", a.shape, mybir.dt.from_np(a.dtype), kind="ExternalInput").ap()
           for n, a in arrays.items()]
    out = nc.dram_tensor("out_dram", (S, DM), F32, kind="ExternalOutput").ap()
    trunk_program(nc, *aps, out)
    got = run_bass_kernel_spmd(nc, [{f"{n}_dram": a for n, a in arrays.items()}], core_ids=[0])
    return got.results[0]["out_dram"].reshape(1, S, DM)
```
